# Optimizing a Trainium2 kernel written in Bass

```python
import math
import jax
import jax.numpy as jnp
from jax import lax
import numpy as np

D_MODEL = 2048
BATCH = 1
SEQ = 256
DEPTH = 2
DEC_BATCH = 8
DEC_SEQ = 1
PAST_LEN = 2048
PAGE_SIZE = 128

N_EVEN = (DEPTH + 1) // 2
N_ODD = DEPTH // 2
HEAD_DIM = 128
H_A = D_MODEL // (2 * HEAD_DIM)
DK_A = HEAD_DIM
DV_A = HEAD_DIM
H_B = D_MODEL // (2 * HEAD_DIM)
DH_B = HEAD_DIM
MOBA_BLOCK = 256
MOBA_TOPK = 3
MOBA_QCHUNK = 16
ROT_DIM = DH_B // 4
ROPE_THETA = 500000.0
H_C = 8
DK_C = D_MODEL // H_C
DV_C = D_MODEL // H_C
RET_THETA = 10000.0
SCAN_CHUNK = 64
D_FF = 256 * ((8 * D_MODEL // 3 + 255) // 256)
CONV_W = 3
EPS = 1e-6
A_W = H_A * DK_A
B_W = H_B * DH_B
EVEN_IN = 4 * A_W + 3 * B_W
ODD_IN = 2 * H_C * DK_C + 2 * H_C * DV_C
PAGES_PER_BLOCK = MOBA_BLOCK // PAGE_SIZE

kernel_name = 'hgrn2_moba_retention_convffn_step'

def rms_norm(x, g):
    x32 = x.astype(jnp.float32)
    y = x32 * lax.rsqrt(jnp.mean(x32 * x32, axis=-1, keepdims=True) + EPS)
    return (y * g.astype(jnp.float32)).astype(x.dtype)

def head_rms_norm(o, g):
    return o * lax.rsqrt(jnp.mean(o * o, axis=-1, keepdims=True) + EPS) * g.astype(jnp.float32)

def head_layer_norm(o, g):
    oc = o - jnp.mean(o, axis=-1, keepdims=True)
    return oc * lax.rsqrt(jnp.mean(oc * oc, axis=-1, keepdims=True) + EPS) * g.astype(jnp.float32)

def rope(x, pos, rot_dim, theta):
    half = rot_dim // 2
    inv = theta ** (-jnp.arange(half, dtype=jnp.float32) / half)
    ang = pos.astype(jnp.float32)[:, None] * inv[None, :]
    cos = jnp.cos(ang)[:, None, :]
    sin = jnp.sin(ang)[:, None, :]
    x32 = x.astype(jnp.float32)
    x1 = x32[..., :half]
    x2 = x32[..., half:rot_dim]
    out = jnp.concatenate([x1 * cos - x2 * sin, x2 * cos + x1 * sin, x32[..., rot_dim:]], axis=-1)
    return out.astype(x.dtype)

def gla_scan(q, k, v, logf, s0):
    B, H, T, _ = q.shape
    C = math.gcd(T, SCAN_CHUNK)
    n = T // C
    mask = jnp.tril(jnp.ones((C, C), dtype=bool))

    def split(a):
        return jnp.moveaxis(a.reshape(B, H, n, C, a.shape[-1]), 2, 0)

    def step(S, xs):
        qc, kc, vc, lc = xs
        b = jnp.cumsum(lc, axis=2)
        o_inter = jnp.einsum('bhcd,bhde->bhce', qc * jnp.exp(b), S)
        diff = b[:, :, :, None, :] - b[:, :, None, :, :]
        dec = jnp.exp(jnp.where(mask[:, :, None], diff, -jnp.inf))
        att = jnp.einsum('bhtd,bhsd,bhtsd->bhts', qc, kc, dec)
        o = o_inter + jnp.einsum('bhts,bhse->bhte', att, vc)
        bl = b[:, :, -1:, :]
        S = jnp.exp(bl[:, :, 0, :])[..., None] * S + jnp.einsum('bhsd,bhse->bhde', kc * jnp.exp(bl - b), vc)
        return S, o

    S, o = lax.scan(step, s0, (split(q), split(k), split(v), split(logf)))
    return jnp.moveaxis(o, 0, 2).reshape(B, H, T, -1), S

def retention_scan(q, k, v, s0):
    B, H, T, _ = q.shape
    C = math.gcd(T, SCAN_CHUNK)
    n = T // C
    lg = jnp.log(1.0 - 2.0 ** (-5.0 - jnp.arange(H, dtype=jnp.float32)))
    i = jnp.arange(C, dtype=jnp.float32)
    mask = jnp.tril(jnp.ones((C, C), dtype=bool))
    dmat = jnp.exp(jnp.where(mask, (i[:, None] - i[None, :]) * lg[:, None, None], -jnp.inf))
    inter = jnp.exp((i[None, :] + 1.0) * lg[:, None])
    state_dec = jnp.exp((C - 1.0 - i[None, :]) * lg[:, None])
    chunk_dec = jnp.exp(C * lg)

    def split(a):
        return jnp.moveaxis(a.reshape(B, H, n, C, a.shape[-1]), 2, 0)

    def step(S, xs):
        qc, kc, vc = xs
        att = jnp.einsum('bhtd,bhsd->bhts', qc, kc) * dmat
        o = jnp.einsum('bhts,bhse->bhte', att, vc) + jnp.einsum('bhtd,bhde->bhte', qc, S) * inter[:, :, None]
        S = chunk_dec[:, None, None] * S + jnp.einsum('bhsd,bhse->bhde', kc * state_dec[:, :, None], vc)
        return S, o

    S, o = lax.scan(step, s0, (split(q), split(k), split(v)))
    return jnp.moveaxis(o, 0, 2).reshape(B, H, T, -1), S

def moba_prompt(q, k, v):
    B, T, H, D = q.shape
    scale = D ** -0.5
    nb = -(-T // MOBA_BLOCK)
    tpad = nb * MOBA_BLOCK
    qh = jnp.moveaxis(q, 1, 2)
    pad = ((0, 0), (0, 0), (0, tpad - T), (0, 0))
    kb = jnp.pad(jnp.moveaxis(k, 1, 2), pad).reshape(B, H, nb, MOBA_BLOCK, D)
    vb = jnp.pad(jnp.moveaxis(v, 1, 2), pad).reshape(B, H, nb, MOBA_BLOCK, D)
    kmean = jnp.mean(kb.astype(jnp.float32), axis=3)
    qblk = jnp.arange(T) // MOBA_BLOCK
    kk = max(1, min(MOBA_TOPK, nb - 1))
    gate = jnp.einsum('bhtd,bhjd->bhtj', qh.astype(jnp.float32), kmean)
    gate = jnp.where(jnp.arange(nb)[None, :] < qblk[:, None], gate, -jnp.inf)
    _, idx = lax.top_k(gate, kk)
    valid = idx < qblk[:, None]
    qn = MOBA_QCHUNK
    n = T // qn
    bi = jnp.arange(B)[:, None, None, None]
    hi = jnp.arange(H)[None, :, None, None]

    def chunk(a):
        return jnp.moveaxis(a.reshape(B, H, n, qn, a.shape[-1]), 2, 0)

    def body(xs):
        qc, ic, okc, start = xs
        blk = start // MOBA_BLOCK
        k_own = lax.dynamic_index_in_dim(kb, blk, axis=2, keepdims=False)
        v_own = lax.dynamic_index_in_dim(vb, blk, axis=2, keepdims=False)
        tq = start + jnp.arange(qn)
        tk = blk * MOBA_BLOCK + jnp.arange(MOBA_BLOCK)
        s_own = jnp.einsum('bhqd,bhsd->bhqs', qc, k_own).astype(jnp.float32) * scale
        s_own = jnp.where(tk[None, :] <= tq[:, None], s_own, -jnp.inf)
        k_sel = kb[bi, hi, ic]
        v_sel = vb[bi, hi, ic]
        s_sel = jnp.einsum('bhqd,bhqksd->bhqks', qc, k_sel).astype(jnp.float32) * scale
        s_sel = jnp.where(okc[..., None], s_sel, -jnp.inf).reshape(B, H, qn, kk * MOBA_BLOCK)
        p = jax.nn.softmax(jnp.concatenate([s_sel, s_own], axis=-1), axis=-1).astype(v.dtype)
        p_sel = p[..., :kk * MOBA_BLOCK].reshape(B, H, qn, kk, MOBA_BLOCK)
        return (jnp.einsum('bhqks,bhqksd->bhqd', p_sel, v_sel)
                + jnp.einsum('bhqs,bhsd->bhqd', p[..., kk * MOBA_BLOCK:], v_own))

    starts = jnp.arange(n) * qn
    o = lax.map(body, (chunk(qh), chunk(idx), chunk(valid), starts))
    o = jnp.moveaxis(o, 0, 2).reshape(B, H, T, D)
    return jnp.moveaxis(o, 1, 2)

def gather_blocks(pool, li, page_table, blk_idx):
    B, T, H, kk = blk_idx.shape
    logical = blk_idx[..., None] * PAGES_PER_BLOCK + jnp.arange(PAGES_PER_BLOCK)
    phys = page_table[jnp.arange(B)[:, None, None, None, None], logical]
    rows = pool[li, phys[..., None], jnp.arange(PAGE_SIZE), jnp.arange(H)[:, None, None, None]]
    return rows.reshape(B, T, H, kk, MOBA_BLOCK, pool.shape[-1])

def moba_sample(q, k, v, cache_k, cache_v, li, page_table):
    DB, T, H, D = q.shape
    scale = D ** -0.5
    n_full = PAST_LEN // MOBA_BLOCK
    tail = PAST_LEN - n_full * MOBA_BLOCK
    k_past = cache_k[li, page_table].reshape(DB, PAST_LEN, H, D)
    if tail > 0:
        v_tail = cache_v[li, page_table[:, n_full * PAGES_PER_BLOCK:]].reshape(DB, tail, H, D)
        own_k = jnp.concatenate([k_past[:, n_full * MOBA_BLOCK:].astype(k.dtype), k], axis=1)
        own_v = jnp.concatenate([v_tail.astype(v.dtype), v], axis=1)
    else:
        own_k, own_v = k, v
    jk = jnp.arange(tail + T)
    own_mask = jk[None, :] <= tail + jnp.arange(T)[:, None]
    s_own = jnp.einsum('bthd,bshd->bths', q, own_k).astype(jnp.float32) * scale
    s_own = jnp.where(own_mask[:, None, :], s_own, -jnp.inf)
    if n_full > 0:
        kk = min(MOBA_TOPK, n_full)
        kmean = jnp.mean(k_past[:, :n_full * MOBA_BLOCK].astype(jnp.float32).reshape(DB, n_full, MOBA_BLOCK, H, D), axis=2)
        gate = jnp.einsum('bthd,bjhd->bthj', q.astype(jnp.float32), kmean)
        _, idx = lax.top_k(gate, kk)
        k_sel = gather_blocks(cache_k, li, page_table, idx).astype(q.dtype)
        v_sel = gather_blocks(cache_v, li, page_table, idx).astype(v.dtype)
        s_sel = jnp.einsum('bthd,bthksd->bthks', q, k_sel).astype(jnp.float32).reshape(DB, T, H, kk * MOBA_BLOCK) * scale
        p = jax.nn.softmax(jnp.concatenate([s_sel, s_own], axis=-1), axis=-1).astype(v.dtype)
        p_sel = p[..., :kk * MOBA_BLOCK].reshape(DB, T, H, kk, MOBA_BLOCK)
        return (jnp.einsum('bthks,bthksd->bthd', p_sel, v_sel)
                + jnp.einsum('bths,bshd->bthd', p[..., kk * MOBA_BLOCK:], own_v))
    p = jax.nn.softmax(s_own, axis=-1).astype(v.dtype)
    return jnp.einsum('bths,bshd->bthd', p, own_v)

def even_mix(h, pos, w_in, w_out, gn, lb, s0, attn):
    B, T, _ = h.shape
    z = h @ w_in
    qa, fa, ia, ga, qb, kb, vb = jnp.split(z, [A_W, 2 * A_W, 3 * A_W, 4 * A_W, 4 * A_W + B_W, 4 * A_W + 2 * B_W], axis=-1)

    def heads(a, nh):
        return jnp.moveaxis(a.reshape(B, T, nh, -1), 1, 2).astype(jnp.float32)

    lbh = lb.reshape(H_A, 1, DK_A)
    logf = jnp.logaddexp(jnp.log(lbh), jnp.log1p(-lbh) + jax.nn.log_sigmoid(heads(fa, H_A)))
    ka = -jnp.expm1(logf)
    va = jax.nn.silu(heads(ia, H_A))
    oa, S = gla_scan(heads(qa, H_A), ka, va, logf, s0.astype(jnp.float32))
    oa = head_rms_norm(oa, gn.reshape(H_A, 1, DV_A))
    oa = jnp.moveaxis(oa, 1, 2).reshape(B, T, A_W) * jax.nn.sigmoid(ga.astype(jnp.float32))
    qb = rope(qb.reshape(B, T, H_B, DH_B), pos, ROT_DIM, ROPE_THETA)
    kb = rope(kb.reshape(B, T, H_B, DH_B), pos, ROT_DIM, ROPE_THETA)
    vb = vb.reshape(B, T, H_B, DH_B)
    ob = attn(qb, kb, vb).reshape(B, T, B_W)
    y = jnp.concatenate([oa.astype(h.dtype), ob.astype(h.dtype)], axis=-1) @ w_out
    return y, S, kb, vb

def odd_mix(h, pos, w_in, w_out, gn, s0):
    B, T, _ = h.shape
    z = h @ w_in
    q, k, v, g = jnp.split(z, [H_C * DK_C, 2 * H_C * DK_C, 2 * H_C * DK_C + H_C * DV_C], axis=-1)
    q = rope(q.reshape(B, T, H_C, DK_C), pos, DK_C, RET_THETA)
    k = rope(k.reshape(B, T, H_C, DK_C), pos, DK_C, RET_THETA)
    v = v.reshape(B, T, H_C, DV_C)

    def heads(a):
        return jnp.moveaxis(a, 1, 2).astype(jnp.float32)

    o, S = retention_scan(heads(q), heads(k) * (DK_C ** -0.5), heads(v), s0.astype(jnp.float32))
    o = head_layer_norm(o, gn.reshape(H_C, 1, DV_C))
    o = jnp.moveaxis(o, 1, 2).reshape(B, T, H_C * DV_C) * jax.nn.silu(g.astype(jnp.float32))
    return o.astype(h.dtype) @ w_out, S

def conv_ffn(h, w_in, cw, cb, w_out, buf):
    T = h.shape[1]
    up = h @ w_in
    a, b = up[..., :D_FF], up[..., D_FF:]
    ap = jnp.concatenate([buf.astype(a.dtype), a], axis=1)
    conv = cb.astype(a.dtype)
    for j in range(CONV_W):
        conv = conv + cw[j] * ap[:, j:j + T]
    y = (jax.nn.silu(conv) * b) @ w_out
    return y, ap[:, T:]

def run_trunk(x, pos, attn, s_hgrn, s_ret, s_conv, weights):
    (lb_all, norm_mix, norm_ffn, norm_final, w_in_even, w_out_even, gn_hgrn,
     w_in_odd, w_out_odd, gn_ret, w_ffn_in, conv_w, conv_b, w_ffn_out) = weights
    new_k, new_v, new_h, new_r, new_c = [], [], [], [], []
    for l in range(DEPTH):
        h = rms_norm(x, norm_mix[l])
        if l % 2 == 0:
            e = l // 2

            def attn_e(q, k, v, e=e):
                return attn(e, q, k, v)

            y, S, k_rows, v_rows = even_mix(h, pos, w_in_even[e], w_out_even[e], gn_hgrn[e], lb_all[e], s_hgrn[e], attn_e)
            new_h.append(S)
            new_k.append(k_rows)
            new_v.append(v_rows)
        else:
            r = l // 2
            y, S = odd_mix(h, pos, w_in_odd[r], w_out_odd[r], gn_ret[r], s_ret[r])
            new_r.append(S)
        x = x + y.astype(x.dtype)
        h = rms_norm(x, norm_ffn[l])
        y, buf = conv_ffn(h, w_ffn_in[l], conv_w[l], conv_b[l], w_ffn_out[l], s_conv[l])
        x = x + y.astype(x.dtype)
        new_c.append(buf)
    return (rms_norm(x, norm_final), jnp.stack(new_k), jnp.stack(new_v),
            jnp.stack(new_h), jnp.stack(new_r), jnp.stack(new_c))

def setup_inputs(seed: int = 0) -> dict:
    key = jax.random.key(seed)
    ks = jax.random.split(key, 24)
    f32 = jnp.float32
    n_pages = PAST_LEN // PAGE_SIZE
    used = DEC_BATCH * n_pages
    n_pool = used + max(1, used // 4)

    def nrm(k, shape, s):
        return jax.random.normal(k, shape, f32) * s

    perm = jax.random.permutation(ks[0], n_pool)
    page_table = perm[:used].reshape(DEC_BATCH, n_pages).astype(jnp.int32)
    return {
        'x_prompt': nrm(ks[1], (BATCH, SEQ, D_MODEL), 1.0),
        'x_sample': nrm(ks[2], (DEC_BATCH, DEC_SEQ, D_MODEL), 1.0),
        'cache_k': nrm(ks[3], (N_EVEN, n_pool, PAGE_SIZE, H_B, DH_B), 1.0),
        'cache_v': nrm(ks[4], (N_EVEN, n_pool, PAGE_SIZE, H_B, DH_B), 1.0),
        'page_table': page_table,
        'state_hgrn': nrm(ks[5], (N_EVEN, DEC_BATCH, H_A, DK_A, DV_A), 0.5),
        'state_ret': nrm(ks[6], (N_ODD, DEC_BATCH, H_C, DK_C, DV_C), 1.0),
        'state_conv': nrm(ks[7], (DEPTH, DEC_BATCH, CONV_W - 1, D_FF), 1.0),
        'norm_mix': 1.0 + nrm(ks[8], (DEPTH, D_MODEL), 0.05),
        'norm_ffn': 1.0 + nrm(ks[9], (DEPTH, D_MODEL), 0.05),
        'norm_final': 1.0 + nrm(ks[10], (D_MODEL,), 0.05),
        'w_in_even': nrm(ks[11], (N_EVEN, D_MODEL, EVEN_IN), D_MODEL ** -0.5),
        'w_out_even': nrm(ks[12], (N_EVEN, A_W + B_W, D_MODEL), (A_W + B_W) ** -0.5),
        'gn_hgrn': 1.0 + nrm(ks[13], (N_EVEN, A_W), 0.05),
        'lb_hgrn': nrm(ks[14], (N_EVEN, A_W), 0.5),
        'w_in_odd': nrm(ks[15], (N_ODD, D_MODEL, ODD_IN), D_MODEL ** -0.5),
        'w_out_odd': nrm(ks[16], (N_ODD, H_C * DV_C, D_MODEL), (H_C * DV_C) ** -0.5),
        'gn_ret': 1.0 + nrm(ks[17], (N_ODD, H_C * DV_C), 0.05),
        'w_ffn_in': nrm(ks[18], (DEPTH, D_MODEL, 2 * D_FF), D_MODEL ** -0.5),
        'conv_w': nrm(ks[19], (DEPTH, CONV_W, D_FF), CONV_W ** -0.5),
        'conv_b': nrm(ks[20], (DEPTH, D_FF), 0.01),
        'w_ffn_out': nrm(ks[21], (DEPTH, D_FF, D_MODEL), D_FF ** -0.5),
    }

def reference(x_prompt, x_sample, cache_k, cache_v, page_table, state_hgrn, state_ret, state_conv,
              norm_mix, norm_ffn, norm_final, w_in_even, w_out_even, gn_hgrn, lb_hgrn,
              w_in_odd, w_out_odd, gn_ret, w_ffn_in, conv_w, conv_b, w_ffn_out):
    lb_cum = jnp.cumsum(jax.nn.softmax(lb_hgrn.astype(jnp.float32), axis=0), axis=0)
    lb_all = lb_cum - lb_cum[0:1]
    weights = (lb_all, norm_mix, norm_ffn, norm_final, w_in_even, w_out_even, gn_hgrn,
               w_in_odd, w_out_odd, gn_ret, w_ffn_in, conv_w, conv_b, w_ffn_out)
    bp, tp = x_prompt.shape[0], x_prompt.shape[1]
    ts = x_sample.shape[1]
    h0 = jnp.zeros((N_EVEN, bp, H_A, DK_A, DV_A), jnp.float32)
    r0 = jnp.zeros((N_ODD, bp, H_C, DK_C, DV_C), jnp.float32)
    c0 = jnp.zeros((DEPTH, bp, CONV_W - 1, D_FF), x_prompt.dtype)

    def attn_prompt(e, q, k, v):
        return moba_prompt(q, k, v)

    def attn_sample(e, q, k, v):
        return moba_sample(q, k, v, cache_k, cache_v, e, page_table)

    y_p, k_p, v_p, h_p, r_p, c_p = run_trunk(x_prompt, jnp.arange(tp), attn_prompt, h0, r0, c0, weights)
    y_s, k_s, v_s, h_s, r_s, c_s = run_trunk(x_sample, PAST_LEN + jnp.arange(ts), attn_sample,
                                             state_hgrn, state_ret, state_conv, weights)
    return (y_p, y_s, k_p, v_p, k_s, v_s, h_p, h_s, r_p, r_s, c_p, c_s)


_drawn_inputs = setup_inputs


def setup_inputs(seed=0):
    import zlib

    import numpy as np

    out = dict(_drawn_inputs(seed))
    spreads = {}
    factors = {'conv_b': 7.269}
    for name, (base, spread) in spreads.items():
        noise = np.random.default_rng([zlib.crc32(name.encode()), seed]).standard_normal(out[name].shape)
        drawn = base * np.exp(spread * noise) if base else spread * noise
        out[name] = jnp.asarray(drawn.astype(out[name].dtype))
    for name, factor in factors.items():
        out[name] = (out[name] * factor).astype(out[name].dtype)
    return out
```

```python
from contextlib import ExitStack

import numpy as np

import concourse.bass as bass
from concourse import mybir

F32 = mybir.dt.float32
F32R = mybir.dt.float32r
I32 = mybir.dt.int32
ALU = mybir.AluOpType
ACT = mybir.ActivationFunctionType
AX_X = mybir.AxisListType.X

P = 128
SEQ, DEC = 256, 8
TOK = SEQ + DEC
D_MODEL, D_FF = 2048, 5632
MT = D_MODEL // P
FT = D_FF // P
HEADS = 8
PAGES = 16
PAGE = 128
BLOCKS = 8
TOPK = 3
CHUNK = 64
NCH = SEQ // CHUNK
LEVELS = 6
EPS = 1e-6
RK = 256
SLOTS = 8
UNIT = 4 * P
BIG = 1e30
CHUNKS = (16, 16, 12)
PAD = 2
CONV_COLS = PAD + SEQ + 3 * DEC
CONV_OUT = CONV_COLS - 2

V_MIX0, V_FFN0, V_MIX1, V_FFN1, V_FINAL = (MT * n for n in range(5))
V_GNH = 5 * MT
V_GNR = V_GNH + HEADS
V_CONV = V_GNR + 2 * HEADS
V_ALL = V_CONV + 2 * 4 * FT

Z_QB, Z_KB, Z_VB, Z_QA, Z_FA, Z_IA, Z_GA = (HEADS * n for n in range(7))
ZE = 7 * HEADS
Z_Q, Z_K, Z_V, Z_G = (2 * HEADS * n for n in range(4))
ZO = 8 * HEADS


class Steps:

    def __init__(self, sem, names):
        self.sem, self.names, self.K = sem, list(names), len(names)
        self.index = {n: k + 1 for k, n in enumerate(self.names)}
        assert len(self.index) == self.K
        self.next = 0

    def one(self, name):
        assert self.names[self.next % self.K] == name, (self.names[self.next % self.K], name)
        self.next += 1
        return 1

    def at(self, name, turn=0):
        return turn * self.K + self.index[name]

    def before(self, turn):
        return turn * self.K


class Phase:

    def __init__(self, kind, weights, first, tiles, ktu, src, t0):
        self.kind, self.w, self.first, self.n, self.ktu, self.src, self.t0 = kind, weights, first, tiles, ktu, src, t0
        self.u0 = 4 * t0

    def end(self):
        return self.t0 + self.n


def hybrid_step(nc, x_in, vecs, conv_state, w_even_in, w_even_out, w_odd_in, w_odd_out, w_f0_in, w_f0_o0, w_f0_o1,
                w_f0_o2, w_f1_in, w_f1_o0, w_f1_o1, w_f1_o2, cache_k, cache_v, page_table, state_hgrn, state_ret,
                c_ident, c_eye8, c_eye, c_blk, c_causal, c_rope_b, c_perm, c_rope_c, c_decay, c_sdec, c_gamma,
                c_level, c_reset, y_out, kT_out, vT_out, hgrn_p_out, hgrn_s_out, ret_p_out, ret_s_out, conv_out):
    ctx = ExitStack()
    with ctx:
        def sb(name, shape, dt=F32, stack=ctx):
            return stack.enter_context(nc.sbuf_tensor(name, shape, dt))

        def sem(name):
            return ctx.enter_context(nc.semaphore(name))

        raw = sb("raw", [P, SLOTS, UNIT])
        whi = sb("whi", [P, SLOTS, UNIT], F32R)
        wlo = sb("wlo", [P, SLOTS, UNIT], F32R)
        x = sb("x", [P, MT, TOK])
        hA = (sb("hA_hi", [P, MT, TOK], F32R), sb("hA_lo", [P, MT, TOK], F32R))
        vec = sb("vec", [P, V_ALL])
        rstd = sb("rstd", [P, TOK])
        acc = sb("acc", [P, TOK])
        sq = sb("sq", [P, TOK])
        var = sb("var", [P, TOK])
        root_tmp = sb("root_tmp", [P, TOK])
        ones = sb("ones", [P, P])
        ident = sb("ident", [P, P])

        with ExitStack() as part:
            def se(name, shape, dt=F32):
                return sb(name, shape, dt, part)
            ze = se("ze", [P, ZE, TOK])
            S = se("S", [P, DEC, PAGES, HEADS])
            cau = se("cau", [P, 384])
            ropeb = se("ropeb", [32, 2, TOK])
            perm = se("perm", [32, 32])
            eye8 = se("eye8", [8, 8])
            eye = se("eye", [P, 8, 8])
            rt = se("rt", [32, 2, TOK])
            pt = se("pt", [1, DEC * PAGES], I32)
            own = se("own", [P, DEC, HEADS])
            po = se("po", [P, DEC, HEADS])
            qk = se("qk", [P, HEADS, DEC])
            mxt = se("mxt", [P, DEC, HEADS])
            mxa = se("mxa", [P, DEC, HEADS])
            mx64 = se("mx64", [64, 1])
            dg = se("dg", [64, 64])
            oS = se("oS", [P, HEADS, DEC])
            oS2 = se("oS2", [P, HEADS, DEC])
            vs = se("vs", [P, HEADS, DEC])
            Pb = se("Pb", [P, PAGES * HEADS])
            Sb = se("Sb", [P, PAGES, HEADS])
            with ExitStack() as sub:
                kring = sb("kring", [P, 4, HEADS * P], F32, sub)
                qbc = sb("qbc", [P, HEADS * P], F32, sub)
                qt8 = sb("qt8", [8, HEADS * P], F32, sub)
                qm8 = sb("qm8", [8, HEADS * P], F32, sub)
            with ExitStack() as sub:
                qh = sb("qh", [P, TOK], F32, sub)
                vh = sb("vh", [P, TOK], F32, sub)
                sm = sb("sm", [P, 384], F32, sub)
                mx2 = sb("mx2", [P, 2], F32, sub)
                nmx = sb("nmx", [P, 2], F32, sub)
                lsum = sb("lsum", [P, 2], F32, sub)
                rl = sb("rl", [P, 2], F32, sub)
                vtok = sb("vtok", [P, 2, P], F32, sub)
                pT = sb("pT", [P, 384], F32, sub)
            with ExitStack() as sub:
                def sh(name, shape, dt=F32):
                    return sb(name, shape, dt, sub)
                levm = sh("levm", [P, LEVELS + 1, P])
                reset = sh("reset", [P, SEQ])
                t1 = sh("t1", [P, TOK])
                t2 = sh("t2", [P, TOK])
                lsg = sh("lsg", [P, TOK])
                ka = sh("ka", [P, TOK])
                va = sh("va", [P, TOK])
                sg = sh("sg", [P, TOK])
                fg = sh("fg", [P, 8])
                bcum = sh("bcum", [P, SEQ])
                pr = sh("pr", [P, LEVELS + 1, P])
                Aatt = sh("Aatt", [P, 2, P])
                hv = sh("hv", [P, 2, P])
                hk = sh("hk", [P, 2, P])
                ebl = sh("ebl", [P, NCH])
                kv8 = sh("kv8", [8, 2 * P])
                qm = sh("qm", [P, 8, 8])
                so8 = sh("so8", [8, P])
            with ExitStack() as sub:
                vring = sb("vring", [P, 4, HEADS * P], F32, sub)
                G = sb("G", [P, DEC, BLOCKS, HEADS], F32, sub)
                cmp = sb("cmp", [P, DEC, BLOCKS, HEADS], F32, sub)
                rank = sb("rank", [P, DEC, BLOCKS, HEADS], F32, sub)
                blk = sb("blk", [8, HEADS * P], F32, sub)
                om = sb("om", [8, HEADS * P], F32, sub)
        with ExitStack() as part:
            def sg_(name, shape, dt=F32):
                return sb(name, shape, dt, part)
            EL = sg_("EL", [P, LEVELS, SEQ])
            QE = sg_("QE", [P, LEVELS, P])
            KE = sg_("KE", [P, LEVELS, P])
            qdec = sg_("qdec", [P, SEQ])
            Sst = sg_("Sst", [P, NCH, P])
            S0 = sg_("S0", [P, DEC, P])
            vm8 = sg_("vm8", [8, 8, P])
            oT = sg_("oT", [P, TOK])
        with ExitStack() as part:
            def so(name, shape, dt=F32):
                return sb(name, shape, dt, part)
            zo = so("zo", [P, ZO, TOK])
            ropec = so("ropec", [P, 2, TOK])
            dmat = so("dmat", [P, 384])
            sdec = so("sdec", [P, HEADS, 2])
            gam = so("gam", [P, HEADS])
            reye8 = so("reye8", [8, 8])
            reye = so("reye", [P, 8, 8])
            r1 = so("r1", [P, TOK])
            r2 = so("r2", [P, TOK])
            qr = so("qr", [P, 2, TOK])
            kr = so("kr", [P, 2, TOK])
            vw = so("vw", [P, 2, TOK])
            aT = so("aT", [P, 384])
            rv = so("rv", [P, 2, RK])
            rk_ = so("rk", [P, 2, RK])
            Sf = so("Sf", [P, 2, RK])
            R0 = so("R0", [P, 2, 2, 2, RK])
            rkv8 = so("rkv8", [8, 2 * RK])
            rvm = so("rvm", [8, 2, RK])
            rqm = so("rqm", [P, 2, 8, 8])
            ro8 = so("ro8", [8, RK])
            roT = so("roT", [P, 2, TOK])
        with ExitStack() as part:
            def sf(name, shape, dt=F32):
                return sb(name, shape, dt, part)
            hB = (sf("hB_hi", [P, MT, TOK], F32R), sf("hB_lo", [P, MT, TOK], F32R))
            hid1 = (sf("hid1_hi", [P, MT, TOK], F32R), sf("hid1_lo", [P, MT, TOK], F32R))
            cst = sf("cst", [P, FT, 2 * DEC])
            cout = sf("cout", [P, FT, PAD + 2 * DEC])
            ab = sf("ab", [P, CONV_COLS])
            cv1 = sf("cv1", [P, CONV_OUT])
            cv2 = sf("cv2", [P, CONV_OUT])
            sil = sf("sil", [P, CONV_OUT])
            bt = sf("bt", [P, TOK])
            ug = sf("ug", [P, TOK])

        st = [ctx.enter_context(nc.psum_tensor(f"stream{n}", [P, 512], F32)) for n in range(2)]
        m = [ctx.enter_context(nc.psum_tensor(f"mix{n}", [P, 512], F32)) for n in range(6)]

        phases = []

        def add(kind, w, first, tiles, ktu, src):
            phases.append(Phase(kind, w, first, tiles, ktu, src, phases[-1].end() if phases else 0))
            return phases[-1]
        E_IN = add("z_even", w_even_in, 0, ZE, 4, hA)
        E_OUT = add("out_norm_hB", w_even_out, 0, MT, 4, hA)

        def ffn(w_in, w_o, last):
            a = [add("ffn_hid1", w_in, 0, 2 * CHUNKS[0], 4, hB),
                 add("ffn_hA", w_in, 2 * CHUNKS[0], 2 * CHUNKS[1], 4, hB),
                 add("out", w_o[0], 0, MT, 4, hid1),
                 add("ffn_hid1", w_in, 2 * (CHUNKS[0] + CHUNKS[1]), 2 * CHUNKS[2], 4, hB),
                 add("out", w_o[1], 0, MT, 4, hA),
                 add(last, w_o[2], 0, MT, 3, hid1)]
            layer = 0 if w_in is w_f0_in else 1
            for p, pair0 in zip((a[0], a[1], a[3]), (0, CHUNKS[0], CHUNKS[0] + CHUNKS[1])):
                p.pair0, p.layer = pair0, layer
            for p, need in zip((a[2], a[4], a[5]), (CHUNKS[0], CHUNKS[0] + CHUNKS[1], FT)):
                p.need = need + FT * layer
            return a
        F0 = ffn(w_f0_in, (w_f0_o0, w_f0_o1, w_f0_o2), "out_norm_hA")
        O_IN = add("z_odd", w_odd_in, 0, ZO, 4, hA)
        O_OUT = add("out_norm_hB", w_odd_out, 0, MT, 4, hA)
        F1 = ffn(w_f1_in, (w_f1_o0, w_f1_o1, w_f1_o2), "out_final")
        E_OUT.norm, F0[-1].norm, O_OUT.norm, F1[-1].norm = (1, V_FFN0), (2, V_MIX1), (3, V_FFN1), (4, V_FINAL)

        x_landed = sem("x_landed")
        const_landed = sem("const_landed")
        raw_landed = [sem(f"raw_landed{n}") for n in range(SLOTS // 2)]
        hi_done, lo_done, unit_used, tile_free = sem("hi_done"), sem("lo_done"), sem("unit_used"), sem("tile_free")
        consts_set = sem("consts_set")
        acc_cleared, norm_summed = sem("acc_cleared"), sem("norm_summed")
        NV = Steps(sem("norm_vector"), ["lo", "sum"])
        NA = Steps(sem("norm_scalar"), ["square", "hi"])
        IV = Steps(sem("root_vector"), ["var", "n1", "n2", "rstd"])
        IA = Steps(sem("root_scalar"), ["ln", "rough"])
        FV = Steps(sem("ffn_vector"), ["a_prompt", "c1", "c2", "c3", "u_prompt", "u_sample", "hid_lo"])
        FA = Steps(sem("ffn_scalar"), ["history", "new_p", "new_s", "silu", "hid_hi"])
        y_ready, y_stored = sem("y_ready"), sem("y_stored")
        ab_cleared = sem("ab_cleared")
        cst_landed, cout_stored = sem("cst_landed"), sem("cout_stored")
        RP = sem("rope_swapped")
        RV = Steps(sem("rope_vector"), ["cos", "sin", "add"])
        q8_turned, q8_saved, q_picked, q_spread, q_copied = sem("q8_turned"), sem("q8_saved"), sem("q_picked"), sem("q_spread"), sem("q_copied")
        pt_landed = sem("pt_landed")
        k_landed = [sem(f"k_landed{n}") for n in range(4)]
        k_used, s_saved = sem("k_used"), sem("s_saved")
        kv_stored = sem("kv_stored")
        BV = Steps(sem("attn_vector"), ["masked", "max0", "max1", "negmax", "recip", "p0", "p1", "o_lo"])
        BA = Steps(sem("attn_scalar"), ["q", "v", "v_rows", "exp0", "exp1", "pT", "o_hi"])
        BP = Steps(sem("attn_tensor"), ["scores", "v_turned", "p_turned", "o"])
        HV = Steps(sem("hgrn_vector"),
                   ["ls", "mxf", "g1", "sg", "i1", "ir", "va", "cum"] + [f"d{l}{s}" for l in range(LEVELS) for s in "lr"]
                   + ["qe0", "ke0", "pr0a", "pr0b", "att0", "qe1", "ke1", "pr1a", "pr1b", "att1", "dk", "kd", "qdec",
                      "s1", "s2", "s3", "s4", "vm", "qm"] + [f"sn{b}" for b in range(DEC)] + ["var", "n1", "n2", "rstd", "og", "gated", "o_lo"])
        HA = Steps(sem("hgrn_scalar"),
                   ["abs", "exp", "ln", "ka", "fg", "eg", "ei", "levels", "v_rows", "dke", "k_rows", "ebl", "eb", "kv8", "so8",
                    "o_p", "o_s", "square", "lnv", "rough", "o_hi"])
        HP = Steps(sem("hgrn_tensor"),
                   ["lev0", "lev1", "v_turned", "k_turned", "U", "o", "t8", "kv_a", "kv_b", "so", "so_turned", "ssum"])
        h_s0_landed, h_stored = sem("h_s0_landed"), sem("h_stored")
        SVn = (["qk", "vs", "clear_cmp", "rank0"] + [f"{w}{i}" for i in range(BLOCKS) for w in (("gt", "ge", "add") if 0 < i < BLOCKS - 1 else (("ge", "add") if i == 0 else ("gt", "add")))]
               + ["keep", "minus", "bias", "tmax", "rmax", "diag", "mxa", "shift", "oshift", "tsum", "den", "rden", "p", "po"])
        SV = Steps(sem("sel_vector"), SVn)
        SA = Steps(sem("sel_scalar"), ["own", "G", "exp", "oexp"])
        SP_ = Steps(sem("sel_tensor"), ["own", "gates", "mxT", "mxb", "den"])
        v_landed = [sem(f"v_landed{n}") for n in range(4)]
        v_used, v_saved = sem("v_used"), sem("v_saved")
        pb_ready, om_ready, o8_ready = sem("pb_ready"), sem("om_ready"), sem("o8_ready")
        TV = Steps(sem("tail_vector"), ["pv", "sum", "lo"])
        TA = Steps(sem("tail_scalar"), ["hi"])
        QV = Steps(sem("ret_vector"),
                   [f"{w}{s}" for w in "qk" for s in ("a", "b", "x1", "c", "d", "x2")]
                   + ["att", "k0", "k1", "qm"] + [f"{w}{q}" for q in range(4) for w in ("vm", "s0_", "s1_")]
                   + ["mean", "oc", "var", "n1", "n2", "rstd", "og", "gated", "o_lo"])
        QA = Steps(sem("ret_scalar"), ["vw", "v_rows", "sfin", "kv8", "ro8", "o_p", "o_s", "square", "lnv", "rough", "silu", "o_hi"])
        QP = Steps(sem("ret_tensor"), ["att", "v_turned", "k_turned", "o", "sfin", "t8"] + [f"kv{q}{d}" for q in range(4) for d in range(2)]
                   + ["so", "so_turned", "ssum", "vsum"])
        r_s0_landed, r_s0_stored, r_sf_stored, dm_landed = [sem("r_s0_landed0"), sem("r_s0_landed1")], sem("r_s0_stored"), sem("r_sf_stored"), sem("dm_landed")
        r_so = sem("ret_pairs_multiplied")
        NFV, NFA = sem("final_sum"), sem("final_square")
        consts = [(ident[:, :], c_ident), (eye8[:, :], c_eye8), (eye[:, :, :], c_eye), (cau[:, :], c_causal),
                  (ropeb[:, :, :], c_rope_b), (perm[:, :], c_perm)]
        N_CONST = len(consts)
        oc_landed = sem("odd_const_landed")
        sel_landed = sem("sel_landed")
        hc_landed = sem("hgrn_const_landed")

        def tile(buf, t, a=0, b=TOK):
            return buf[:, bass.ds(t, 1), a:b].rearrange("p o n -> p (o n)")

        def col(t):
            return vec[:, bass.ds(t, 1)]

        ab_s = ab[:, PAD + SEQ:CONV_COLS].rearrange("p (b c) -> p b c", c=3)
        block = ctx.enter_context(nc.Block())

        @block.sync
        def _(sp):
            sp.dma_start(x[:, :, :], x_in).then_inc(x_landed, 16)
            sp.dma_start(vec[:, :], vecs).then_inc(x_landed, 16)

            def hgrn_states():
                sp.wait_ge(BV.sem, BV.before(HEADS))
                sp.wait_ge(BP.sem, BP.before(HEADS))
                sp.wait_ge(BA.sem, BA.before(HEADS))
                sp.wait_ge(kv_stored, 32)
                sp.wait_ge(SV.sem, SV.at("vs"))
                with sp.Fori(0, HEADS) as h:
                    load = state_hgrn[:, bass.ds(h, 1), :, :].rearrange("b o d e -> d (b o) e")
                    sp.wait_ge(h_stored, 32 * h)
                    sp.dma_start(S0[:, :, :], load).then_inc(h_s0_landed, 16)
                    sp.wait_ge(HV.sem, HV.at("s4", h))
                    sp.dma_start(hgrn_p_out[bass.ds(h, 1), :, :].rearrange("o d e -> d (o e)"), Sst[:, NCH - 1, :]).then_inc(h_stored, 16)
                    sp.wait_ge(HP.sem, HP.at("so", h))
                    sp.dma_start(hgrn_s_out[:, bass.ds(h, 1), :, :].rearrange("b o d e -> d (b o) e"), S0[:, :, :]).then_inc(h_stored, 16)

            def retention_states():
                with sp.Fori(0, HEADS) as h:
                    sp.wait_ge(QV.sem, QV.before(h))
                    sp.dma_start(dmat[:, :], c_decay[bass.ds(h, 1), :, :].rearrange("o p n -> p (o n)")).then_inc(dm_landed, 16)

                    def load_state(q):
                        for b in range(2):
                            sp.dma_start(R0[:, q % 2, b, :, :],
                                         state_ret[2 * q + b, bass.ds(h, 1), :, :].rearrange("o (d p) e -> p (o d) e", p=P))\
                                .then_inc(r_s0_landed[q % 2], 16)
                    sp.wait_ge(r_s0_stored, 128 * h)
                    load_state(0)
                    load_state(1)
                    sp.wait_ge(QA.sem, QA.at("sfin", h))
                    sp.dma_start(ret_p_out[bass.ds(h, 1), :, :].rearrange("o (d p) e -> p (o d) e", p=P), Sf[:, :, :])\
                        .then_inc(r_sf_stored, 16)
                    for q in range(4):
                        if q < 3:
                            sp.wait_ge(r_so, 3 * h + q + 1)
                        else:
                            sp.wait_ge(QP.sem, QP.at("so", h))
                        for b in range(2):
                            sp.dma_start(ret_s_out[2 * q + b, bass.ds(h, 1), :, :].rearrange("o (d p) e -> p (o d) e", p=P),
                                         R0[:, q % 2, b, :, :]).then_inc(r_s0_stored, 16)
                        if q < 2:
                            sp.wait_ge(r_s0_stored, 128 * h + 32 * (q + 1))
                            load_state(q + 2)

            def load_pair(p, i):
                for half in range(4):
                    n = p.ktu * P
                    row = i * 2 + (p.first + half // 2)
                    if not (isinstance(i, int) and p is phases[0] and i == 0):
                        row = row if isinstance(i, int) else sp.snap(row)
                        sp.wait_ge(lo_done, i * 8 + (p.u0 + 2 * half + 2 - SLOTS))
                    src = p.w[bass.ds(row, 1), half % 2, :, :].rearrange("o p (s n) -> p (o s) n", s=2)
                    sp.dma_start(raw[:, 2 * half:2 * half + 2, 0:n], src).then_inc(raw_landed[half], 16)

            for p in phases:
                peeled = p is E_IN or p is E_OUT or p is O_OUT
                if peeled:
                    load_pair(p, 0)
                if p is E_OUT:
                    hgrn_states()
                if p is O_OUT:
                    retention_states()
                with sp.Fori(1 if peeled else 0, p.n // 2) as i:
                    load_pair(p, i)
            sp.wait_ge(y_ready, MT)
            sp.dma_start(y_out, x[:, :, :]).then_inc(y_stored, 16)
            sp.wait_ge(y_stored, 16)

        @block.tensor
        def _(pe):
            mm, tr = nc.tensor.matmul, nc.tensor.transpose

            def stream_tile(p, i, j):
                bank = st[j][:, 0:TOK]
                if not (isinstance(i, int) and p.t0 + 2 * i + j < 2):
                    pe.wait_ge(tile_free, 2 * i + (p.t0 + j - 1))
                for k in range(4):
                    pe.wait_ge(lo_done, 8 * i + (p.u0 + 4 * j + k + 1))
                    for q in range(p.ktu):
                        kt, c = k * p.ktu + q, slice(q * P, (q + 1) * P)
                        hi, lo = whi[:, 4 * j + k, c], wlo[:, 4 * j + k, c]
                        first, last = kt == 0, kt == 4 * p.ktu - 1
                        mm(bank, hi, p.src[0][:, kt, :], start=first, stop=False)
                        mm(bank, hi, p.src[1][:, kt, :], start=False, stop=False)
                        ins = mm(bank, lo, p.src[0][:, kt, :], start=False, stop=last)
                    ins.then_inc(unit_used, 1)

            def stream(p, a, b):
                with pe.Fori(a, b) as i:
                    for j in range(2):
                        stream_tile(p, i, j)

            def norm_sum(n):
                if n < 4:
                    pe.wait_ge(NV.sem, NV.before(MT * (n + 1)))
                    pe.wait_ge(NA.sem, NA.before(MT * (n + 1)))
                else:
                    pe.wait_ge(NFV, MT)
                mm(m[5][:, 0:TOK], ones[:, :], acc[:, :], start=True, stop=True).then_inc(norm_summed, 1)

            def rope(first, turn0):
                for half in range(2):
                    for t in range(4):
                        n = turn0 + 4 * half + t
                        if half:
                            pe.wait_ge(RV.sem, RV.at("sin", n - 4))
                        mm(m[t][0:32, 0:TOK], perm[:, :], ze[0:32, first + 4 * half + t, :], start=True, stop=True).then_inc(RP, 1)

            def attention_head(h):
                pe.wait_ge(BV.sem, BV.before(h))
                pe.wait_ge(BA.sem, BA.at("v", h))
                mm(m[0][:, 0:P], qh[:, 0:P], tile(ze, h + Z_KB, 0, P), start=True, stop=False, skip_group_check=True)
                mm(m[0][:, P:384], qh[:, P:SEQ], tile(ze, h + Z_KB, 0, SEQ), start=False, stop=True,
                   skip_group_check=True).then_inc(BP.sem, BP.one("scores"))
                tr(m[1][:, 0:P], vh[:, 0:P], ident[:, :])
                tr(m[1][:, P:SEQ], vh[:, P:SEQ], ident[:, :]).then_inc(BP.sem, BP.one("v_turned"))
                pe.wait_ge(BV.sem, BV.at("p1", h))
                for k in range(3):
                    ins = tr(m[2][:, k * P:(k + 1) * P], sm[:, k * P:(k + 1) * P], ident[:, :])
                ins.then_inc(BP.sem, BP.one("p_turned"))
                pe.wait_ge(BA.sem, BA.at("pT", h))
                mm(m[3][:, 0:SEQ], vtok[:, 0, :], pT[:, 0:SEQ], start=True, stop=False, skip_group_check=True)
                mm(m[3][:, P:SEQ], vtok[:, 1, :], pT[:, SEQ:384], start=False, stop=True,
                   skip_group_check=True).then_inc(BP.sem, BP.one("o"))

            def hgrn_head(h):
                pe.wait_ge(HV.sem, HV.before(h))
                for c in range(2):
                    pe.wait_ge(HV.sem, HV.at(f"ke{c}", h))
                    if c:
                        pe.wait_ge(HV.sem, HV.at("pr0b", h))
                    for l in range(LEVELS + 1):
                        k_, q_ = (KE[:, l, :], QE[:, l, :]) if l < LEVELS else (ka[:, c * P:(c + 1) * P], tile(ze, h + Z_QA, c * P, (c + 1) * P))
                        b_ = l // 4
                        ins = mm(m[b_][:, (l % 4) * P:(l % 4 + 1) * P], k_, q_, start=(l % 4 == 0),
                                 stop=(l in (3, LEVELS)), skip_group_check=True)
                    ins.then_inc(HP.sem, HP.one(f"lev{c}"))
                for c in range(2):
                    ins = tr(m[2][:, c * P:(c + 1) * P], va[:, c * P:(c + 1) * P], ident[:, :])
                ins.then_inc(HP.sem, HP.one("v_turned"))
                pe.wait_ge(HV.sem, HV.at("kd", h))
                for c in range(2):
                    ins = tr(m[3][:, c * P:(c + 1) * P], t2[:, c * P:(c + 1) * P], ident[:, :])
                ins.then_inc(HP.sem, HP.one("k_turned"))
                pe.wait_ge(HA.sem, HA.at("k_rows", h))
                for c in range(NCH):
                    r = slice((c % 2) * CHUNK, (c % 2 + 1) * CHUNK)
                    ins = mm(m[4 - c % 2][:, (c // 2) * P:(c // 2 + 1) * P], hk[r, c // 2, :], hv[r, c // 2, :], start=(c < 2),
                             stop=(c >= NCH - 2), skip_group_check=True)
                ins.then_inc(HP.sem, HP.one("U"))
                pe.wait_ge(HV.sem, HV.at("s4", h))
                for c in range(2):
                    mm(m[5][:, c * P:(c + 1) * P], hv[:, c, :], Aatt[:, c, :], start=(c == 0), stop=False, skip_group_check=True)
                for c in range(1, NCH):
                    ins = mm(m[5][:, c * CHUNK:(c + 1) * CHUNK], Sst[:, c - 1, :], qdec[:, c * CHUNK:(c + 1) * CHUNK],
                             start=False, stop=(c == NCH - 1), skip_group_check=True)
                ins.then_inc(HP.sem, HP.one("o"))
                tr(m[0][0:8, 0:P], ka[:, SEQ:TOK], ident[:, :])
                tr(m[0][0:8, P:2 * P], va[:, SEQ:TOK], ident[:, :]).then_inc(HP.sem, HP.one("t8"))
                pe.wait_ge(HV.sem, HV.at("qm", h))
                for k, w in enumerate("ab"):
                    mm(m[1 + k][:, :], kv8[:, 0:P], vm8[:, 4 * k:4 * k + 4, :], start=True, stop=True)\
                        .then_inc(HP.sem, HP.one(f"kv_{w}"))
                pe.wait_ge(HV.sem, HV.at(f"sn{DEC - 1}", h))
                for b in range(DEC):
                    ins = mm(m[3][0:8, 0:P], qm[:, b, :], S0[:, b, :], start=(b == 0), stop=(b == DEC - 1))
                ins.then_inc(HP.sem, HP.one("so"))
                pe.wait_ge(HA.sem, HA.at("so8", h))
                mm(m[4][:, 0:8], so8[:, :], ident[0:8, 0:8], start=True, stop=True).then_inc(HP.sem, HP.one("so_turned"))
                pe.wait_ge(HA.sem, HA.at("square", h))
                mm(m[0][:, 0:TOK], ones[:, :], t1[:, :], start=True, stop=True).then_inc(HP.sem, HP.one("ssum"))

            def retention_head(h):
                pe.wait_ge(QV.sem, QV.before(h))
                pe.wait_ge(QV.sem, QV.at("kx2", h))
                for d in range(2):
                    mm(m[0][:, 0:SEQ], kr[:, d, 0:P], qr[:, d, 0:SEQ], start=(d == 0), stop=False, skip_group_check=True)
                for d in range(2):
                    ins = mm(m[0][:, SEQ:384], kr[:, d, P:SEQ], qr[:, d, P:SEQ], start=False, stop=(d == 1), skip_group_check=True)
                ins.then_inc(QP.sem, QP.one("att"))
                pe.wait_ge(QA.sem, QA.at("vw", h))
                for s in range(2):
                    for e in range(2):
                        ins = tr(m[1][:, s * RK + e * P:s * RK + (e + 1) * P], vw[:, e, s * P:(s + 1) * P], ident[:, :])
                ins.then_inc(QP.sem, QP.one("v_turned"))
                for s in range(2):
                    for e in range(2):
                        ins = tr(m[2][:, s * RK + e * P:s * RK + (e + 1) * P], kr[:, e, s * P:(s + 1) * P], ident[:, :])
                ins.then_inc(QP.sem, QP.one("k_turned"))
                pe.wait_ge(QV.sem, QV.at("att", h))
                pe.wait_ge(QA.sem, QA.at("v_rows", h))
                for e in range(2):
                    mm(m[3][:, e * SEQ:(e + 1) * SEQ], rv[:, 0, e * P:(e + 1) * P], aT[:, 0:SEQ], start=(e == 0),
                       stop=False, skip_group_check=True)
                    ins = mm(m[3][:, e * SEQ + P:(e + 1) * SEQ], rv[:, 1, e * P:(e + 1) * P], aT[:, SEQ:384], start=False,
                             stop=(e == 1), skip_group_check=True)
                ins.then_inc(QP.sem, QP.one("o"))
                pe.wait_ge(QV.sem, QV.at("k1", h))
                for d in range(2):
                    for s in range(2):
                        ins = mm(m[4][:, d * RK:(d + 1) * RK], rk_[:, s, d * P:(d + 1) * P], rv[:, s, :],
                                 start=(d == 0 and s == 0), stop=(d == 1 and s == 1), skip_group_check=True)
                ins.then_inc(QP.sem, QP.one("sfin"))
                for d in range(2):
                    tr(m[5][0:8, d * P:(d + 1) * P], kr[:, d, SEQ:TOK], ident[:, :])
                for d in range(2):
                    ins = tr(m[5][0:8, RK + d * P:RK + (d + 1) * P], vw[:, d, SEQ:TOK], ident[:, :])
                ins.then_inc(QP.sem, QP.one("t8"))
                for q in range(4):
                    pe.wait_ge(QV.sem, QV.at(f"vm{q}", h))
                    for d in range(2):
                        if q >= 1:
                            pe.wait_ge(QV.sem, QV.at(f"s{d}_{q - 1}", h))
                        mm(m[1 + d][:, :], rkv8[:, d * P:(d + 1) * P], rvm[:, :, :], start=True, stop=True)\
                            .then_inc(QP.sem, QP.one(f"kv{q}{d}"))
                    if q >= 1:
                        sample_out(q - 1)
                pe.wait_ge(QV.sem, QV.at("s1_3", h))
                sample_out(3).then_inc(QP.sem, QP.one("so"))
                pe.wait_ge(QA.sem, QA.at("ro8", h))
                for e in range(2):
                    ins = mm(m[1][:, e * 8:(e + 1) * 8], ro8[:, e * P:(e + 1) * P], ident[0:8, 0:8], start=(e == 0), stop=(e == 1),
                             skip_group_check=True)
                ins.then_inc(QP.sem, QP.one("so_turned"))
                pe.wait_ge(QA.sem, QA.at("o_s", h))
                for e in range(2):
                    ins = mm(m[2][:, 0:TOK], ones[:, :], roT[:, e, :], start=(e == 0), stop=(e == 1))
                ins.then_inc(QP.sem, QP.one("ssum"))
                pe.wait_ge(QA.sem, QA.at("square", h))
                for e in range(2):
                    ins = mm(m[3][:, 0:TOK], ones[:, :], kr[:, e, :], start=(e == 0), stop=(e == 1))
                ins.then_inc(QP.sem, QP.one("vsum"))

            def sample_out(q):
                for b in range(2):
                    for d in range(2):
                        ins = mm(m[0][0:8, 0:RK], rqm[:, d, 2 * q + b, :], R0[:, q % 2, b, d, :],
                                 start=(q == 0 and b == 0 and d == 0), stop=(q == 3 and b == 1 and d == 1))
                if q < 3:
                    ins.then_inc(r_so, 1)
                return ins

            pe.wait_ge(consts_set, 1)
            pe.wait_ge(const_landed, 16 * N_CONST)
            norm_sum(0)
            for j in range(2):
                stream_tile(E_IN, 0, j)
            stream(E_IN, 1, 4)
            pe.wait_ge(tile_free, HEADS)
            rope(Z_QB, 0)
            pe.wait_ge(RV.sem, RV.before(HEADS))
            for h in range(HEADS):
                ins = tr(m[4 + h // 4][0:8, (h % 4) * P:(h % 4 + 1) * P], ze[:, Z_QB + h, SEQ:TOK], ident[:, :])
            ins.then_inc(q8_turned, 1)

            def spread_query():
                for k in range(2):
                    ins = mm(m[4 + k][:, :], ones[0:8, :], qm8[:, k * 512:(k + 1) * 512], start=True, stop=True)
                ins.then_inc(q_spread, 1)
            pe.wait_ge(q_picked, 1)
            spread_query()
            for j in range(2):
                stream_tile(E_IN, 4, j)
            with pe.Fori(0, 7) as b:
                for c in range(3):
                    for j in range(2):
                        stream_tile(E_IN, b * 3 + (5 + c), j)
                    if c == 1:
                        pe.wait_ge(q_picked, b + 2)
                        pe.wait_ge(q_copied, b + 1)
                        spread_query()
            stream(E_IN, 26, 28)
            pe.wait_ge(tile_free, ZE)
            pe.wait_ge(q_copied, DEC)
            rope(Z_KB, HEADS)
            pe.wait_ge(RV.sem, RV.before(2 * HEADS))
            with pe.Fori(0, HEADS) as h:
                attention_head(h)
            pe.wait_ge(BV.sem, BV.before(HEADS))
            pe.wait_ge(BA.sem, BA.before(HEADS))
            with pe.Fori(0, HEADS) as h:
                hgrn_head(h)
            pe.wait_ge(HV.sem, HV.before(HEADS))
            pe.wait_ge(HA.sem, HA.before(HEADS))
            pe.wait_ge(s_saved, DEC)
            pe.wait_ge(SV.sem, SV.at("qk"))
            mm(m[0][:, 0:64], ones[:, :], qk[:, :, :], start=True, stop=True).then_inc(SP_.sem, SP_.one("own"))
            Sv = S[:, :, :, :].rearrange("p b (j two) h -> p b j two h", two=2)
            for k in range(2):
                ins = mm(m[1][:, :], ones[:, :], Sv[:, :, :, k, :], start=(k == 0), stop=(k == 1))
            ins.then_inc(SP_.sem, SP_.one("gates"))
            pe.wait_ge(SV.sem, SV.at("tmax"))
            tr(m[2][0:64, 0:P], mxt[:, :, :].rearrange("p b h -> p (b h)"), ident[:, :]).then_inc(SP_.sem, SP_.one("mxT"))
            pe.wait_ge(SV.sem, SV.at("diag"))
            mm(m[3][:, 0:64], ones[0:64, :], dg[:, :], start=True, stop=True).then_inc(SP_.sem, SP_.one("mxb"))
            pe.wait_ge(SV.sem, SV.at("tsum"))
            mm(m[4][:, 0:64], ones[:, :], mxt[:, :, :], start=True, stop=True).then_inc(SP_.sem, SP_.one("den"))
            pe.wait_ge(SV.sem, SV.before(1))
            with pe.Fori(0, DEC) as b:
                pe.wait_ge(pb_ready, b + 1)
                pe.wait_ge(om_ready, 2 * b)
                for g in range(PAGES):
                    pe.wait_ge(v_landed[g % 4], 64 * b + 16 * (g // 4 + 1))
                    for k in range(2):
                        ins = mm(m[k][0:8, :], Pb[:, g * HEADS:(g + 1) * HEADS], vring[:, g % 4, k * 512:(k + 1) * 512],
                                 start=(g == 0), stop=(g == PAGES - 1))
                    ins.then_inc(v_used, 1)
                pe.wait_ge(om_ready, 2 * b + 2)
                pe.wait_ge(v_saved, b)
                for h in range(HEADS):
                    ins = mm(m[2][:, h:h + 1], om[:, h * P:(h + 1) * P], ones[0:8, 0:1], start=(h == 0), stop=(h == HEADS - 1),
                             skip_group_check=True)
                ins.then_inc(o8_ready, 1)
            pe.wait_ge(TV.sem, TV.before(1))
            pe.wait_ge(TA.sem, TA.before(1))
            stream(E_OUT, 0, MT // 2)
            norm_sum(1)
            for p in F0:
                if p.src is not hB:
                    pe.wait_ge(FV.sem, FV.before(p.need))
                stream(p, 0, p.n // 2)
            norm_sum(2)
            stream(O_IN, 0, ZO // 2)
            pe.wait_ge(tile_free, O_IN.end())
            with pe.Fori(0, HEADS) as h:
                retention_head(h)
            pe.wait_ge(QV.sem, QV.before(HEADS))
            pe.wait_ge(QA.sem, QA.before(HEADS))
            stream(O_OUT, 0, MT // 2)
            norm_sum(3)
            for p in F1:
                if p.src is not hB:
                    pe.wait_ge(FV.sem, FV.before(p.need))
                stream(p, 0, p.n // 2)
            norm_sum(4)

        @block.scalar
        def _(act):
            A = nc.scalar.activation
            for dst, src in consts:
                act.dma_start(dst, src).then_inc(const_landed, 16)

            def hi_tile(p, i, j):
                for k in range(4):
                    if k % 2 == 0:
                        act.wait_ge(raw_landed[2 * j + k // 2], 16 * i + 16 * (p.u0 // 8 + 1))
                    if not (isinstance(i, int) and p.u0 + 8 * i == 0):
                        act.wait_ge(unit_used, 8 * i + (p.u0 + 4 * j + k + 1 - SLOTS))
                    n = p.ktu * P
                    A(whi[:, 4 * j + k, 0:n], raw[:, 4 * j + k, 0:n], ACT.Copy).then_inc(hi_done, 1)

            def norm_tile(n, t, g, dst):
                act.wait_ge(NV.sem, t * 2 + NV.before(MT * n))
                A(sq[:, :], tile(x, t), ACT.Square).then_inc(NA.sem, NA.one("square"))
                A(tile(dst[0], t), tile(x, t), ACT.Copy, scale=col(t + g)).then_inc(NA.sem, NA.one("hi"))

            def rough_root(n):
                act.wait_ge(IV.sem, IV.at("var", n))
                A(sq[:, :], var[:, :], ACT.Ln).then_inc(IA.sem, IA.one("ln"))
                act.wait_ge(IA.sem, IA.at("ln", n))
                A(rstd[:, :], sq[:, :], ACT.Exp, scale=-0.5).then_inc(IA.sem, IA.one("rough"))

            def evac(p, i, j):
                t = 2 * i + j
                if p.kind.startswith("out_"):
                    n, g = p.norm
                    act.wait_ge(tile_free, t + (p.t0 + 1))
                    if p.kind == "out_final":
                        act.wait_ge(NFV, t)
                        A(sq[:, :], tile(x, t), ACT.Square).then_inc(NFA, 1)
                    else:
                        norm_tile(n, t, g, hB if p.kind == "out_norm_hB" else hA)
                elif p.kind.startswith("ffn") and j == 0:
                    pair = i + p.pair0
                    act.wait_ge(FV.sem, FV.before(pair + FT * p.layer))
                    A(ab_s[:, :, 0:2], tile(cst, pair, 0, 2 * DEC).rearrange("p (b c) -> p b c", c=2), ACT.Copy)\
                        .then_inc(FA.sem, FA.one("history"))
                elif p.kind.startswith("ffn"):
                    pair = i + p.pair0
                    turn = pair + FT * p.layer
                    act.wait_ge(tile_free, 2 * i + (p.t0 + 1))
                    act.wait_ge(FA.sem, FA.at("history", turn))
                    A(tile(cout, pair, 0, PAD), ab[:, SEQ:SEQ + PAD], ACT.Copy).then_inc(FA.sem, FA.one("new_p"))
                    A(tile(cout, pair, PAD, PAD + 2 * DEC).rearrange("p (b c) -> p b c", c=2), ab_s[:, :, 1:3], ACT.Copy)\
                        .then_inc(FA.sem, FA.one("new_s"))
                    act.wait_ge(FV.sem, FV.at("c3", turn))
                    A(sil[:, :], cv1[:, :], ACT.Silu).then_inc(FA.sem, FA.one("silu"))
                    act.wait_ge(FV.sem, FV.at("u_sample", turn))
                    A(tile(hid1[0] if p.kind == "ffn_hid1" else hA[0], i), ug[:, :], ACT.Copy).then_inc(FA.sem, FA.one("hid_hi"))

            def body(p):
                with act.Fori(0, p.n // 2 - 1) as i:
                    for j in range(2):
                        hi_tile(p, i + 1, j)
                        evac(p, i, j)

            def turn_over(p, nxt):
                for j in range(2):
                    if nxt is not None:
                        hi_tile(nxt, 0, j)
                    evac(p, p.n // 2 - 1, j)

            def attention_head(h):
                act.wait_ge(BP.sem, BP.before(h))
                A(qh[:, :], tile(ze, h + Z_QB), ACT.Copy).then_inc(BA.sem, BA.one("q"))
                A(vh[:, :], tile(ze, h + Z_VB), ACT.Copy).then_inc(BA.sem, BA.one("v"))
                act.wait_ge(BP.sem, BP.at("v_turned", h))
                A(vtok[:, :, :], m[1][:, 0:SEQ].rearrange("p (s e) -> p s e", s=2), ACT.Copy).then_inc(BA.sem, BA.one("v_rows"))
                act.wait_ge(BV.sem, BV.at("negmax", h))
                for k, (a, b) in enumerate(((0, P), (P, 384))):
                    A(sm[:, a:b], sm[:, a:b], ACT.Exp, bias=nmx[:, k:k + 1], scale=P ** -0.5, accum_out=lsum[:, k:k + 1])\
                        .then_inc(BA.sem, BA.one(f"exp{k}"))
                act.wait_ge(BP.sem, BP.at("p_turned", h))
                A(pT[:, :], m[2][:, 0:384], ACT.Copy).then_inc(BA.sem, BA.one("pT"))
                act.wait_ge(BP.sem, BP.at("o", h))
                A(tile(hA[0], h + HEADS, 0, SEQ), m[3][:, 0:SEQ], ACT.Copy).then_inc(BA.sem, BA.one("o_hi"))

            def hgrn_head(h):
                act.wait_ge(HV.sem, HV.before(h))
                act.wait_ge(HP.sem, HP.before(h))
                f = tile(ze, h + Z_FA)
                A(t1[:, :], f, ACT.Abs).then_inc(HA.sem, HA.one("abs"))
                act.wait_ge(HA.sem, HA.at("abs", h))
                A(t2[:, :], t1[:, :], ACT.Exp, scale=-1.0).then_inc(HA.sem, HA.one("exp"))
                act.wait_ge(HA.sem, HA.at("exp", h))
                A(t1[:, :], t2[:, :], ACT.Ln, bias=1.0).then_inc(HA.sem, HA.one("ln"))
                act.wait_ge(HV.sem, HV.at("mxf", h))
                A(ka[:, :], t2[:, :], ACT.Exp, scale=-1.0).then_inc(HA.sem, HA.one("ka"))
                A(fg[:, :], lsg[:, SEQ:TOK], ACT.Exp).then_inc(HA.sem, HA.one("fg"))
                A(sg[:, :], tile(ze, h + Z_GA), ACT.Exp, scale=-1.0).then_inc(HA.sem, HA.one("eg"))
                A(va[:, :], tile(ze, h + Z_IA), ACT.Exp, scale=-1.0).then_inc(HA.sem, HA.one("ei"))
                act.wait_ge(HV.sem, HV.at(f"d{LEVELS - 1}r", h))
                A(EL[:, :, :], EL[:, :, :], ACT.Exp).then_inc(HA.sem, HA.one("levels"))
                act.wait_ge(HP.sem, HP.at("v_turned", h))
                A(hv[:, :, :], m[2][:, 0:SEQ].rearrange("p (s e) -> p s e", s=2), ACT.Copy).then_inc(HA.sem, HA.one("v_rows"))
                act.wait_ge(HV.sem, HV.at("dk", h))
                A(t2[:, 0:SEQ], t2[:, 0:SEQ], ACT.Exp).then_inc(HA.sem, HA.one("dke"))
                act.wait_ge(HP.sem, HP.at("k_turned", h))
                A(hk[:, :, :], m[3][:, 0:SEQ].rearrange("p (s e) -> p s e", s=2), ACT.Copy).then_inc(HA.sem, HA.one("k_rows"))
                bl = bcum[:, :].rearrange("p (c n) -> p c n", n=CHUNK)[:, :, CHUNK - 1]
                A(ebl[:, :], bl, ACT.Exp).then_inc(HA.sem, HA.one("ebl"))
                A(t1[:, 0:SEQ], bcum[:, :], ACT.Exp).then_inc(HA.sem, HA.one("eb"))
                act.wait_ge(HP.sem, HP.at("t8", h))
                A(kv8[:, :], m[0][0:8, 0:2 * P], ACT.Copy).then_inc(HA.sem, HA.one("kv8"))
                act.wait_ge(HP.sem, HP.at("so", h))
                A(so8[:, :], m[3][0:8, 0:P], ACT.Copy).then_inc(HA.sem, HA.one("so8"))
                A(oT[:, 0:SEQ], m[5][:, 0:SEQ], ACT.Copy).then_inc(HA.sem, HA.one("o_p"))
                act.wait_ge(HP.sem, HP.at("so_turned", h))
                A(oT[:, SEQ:TOK], m[4][:, 0:8], ACT.Copy).then_inc(HA.sem, HA.one("o_s"))
                act.wait_ge(HA.sem, HA.at("o_s", h))
                A(t1[:, :], oT[:, :], ACT.Square).then_inc(HA.sem, HA.one("square"))
                act.wait_ge(HV.sem, HV.at("var", h))
                A(t2[:, :], lsg[:, :], ACT.Ln).then_inc(HA.sem, HA.one("lnv"))
                act.wait_ge(HA.sem, HA.at("lnv", h))
                A(t1[:, :], t2[:, :], ACT.Exp, scale=-0.5).then_inc(HA.sem, HA.one("rough"))
                act.wait_ge(HV.sem, HV.at("gated", h))
                A(tile(hA[0], h), t2[:, :], ACT.Copy).then_inc(HA.sem, HA.one("o_hi"))

            def retention_head(h):
                act.wait_ge(QV.sem, QV.before(h))
                act.wait_ge(QP.sem, QP.before(h))
                A(vw[:, :, :], zo[:, bass.ds(h * 2 + Z_V, 2), :], ACT.Copy).then_inc(QA.sem, QA.one("vw"))
                act.wait_ge(QP.sem, QP.at("v_turned", h))
                A(rv[:, :, :], m[1][:, :].rearrange("p (s e) -> p s e", s=2), ACT.Copy).then_inc(QA.sem, QA.one("v_rows"))
                act.wait_ge(QP.sem, QP.at("sfin", h))
                act.wait_ge(r_sf_stored, 16 * h)
                A(Sf[:, :, :], m[4][:, :].rearrange("p (d e) -> p d e", d=2), ACT.Copy).then_inc(QA.sem, QA.one("sfin"))
                act.wait_ge(QP.sem, QP.at("t8", h))
                A(rkv8[:, :], m[5][0:8, :], ACT.Copy).then_inc(QA.sem, QA.one("kv8"))
                act.wait_ge(QP.sem, QP.at("so", h))
                A(ro8[:, :], m[0][0:8, 0:RK], ACT.Copy).then_inc(QA.sem, QA.one("ro8"))
                A(roT[:, :, 0:SEQ], m[3][:, :].rearrange("p (e t) -> p e t", e=2), ACT.Copy).then_inc(QA.sem, QA.one("o_p"))
                act.wait_ge(QP.sem, QP.at("so_turned", h))
                A(roT[:, :, SEQ:TOK], m[1][:, 0:16].rearrange("p (e t) -> p e t", e=2), ACT.Copy).then_inc(QA.sem, QA.one("o_s"))
                act.wait_ge(QV.sem, QV.at("oc", h))
                A(kr[:, :, :], roT[:, :, :], ACT.Square).then_inc(QA.sem, QA.one("square"))
                act.wait_ge(QV.sem, QV.at("var", h))
                A(r1[:, :], r2[:, :], ACT.Ln).then_inc(QA.sem, QA.one("lnv"))
                act.wait_ge(QA.sem, QA.at("lnv", h))
                A(qr[:, 0, :], r1[:, :], ACT.Exp, scale=-0.5).then_inc(QA.sem, QA.one("rough"))
                A(vw[:, :, :], zo[:, bass.ds(h * 2 + Z_G, 2), :], ACT.Silu).then_inc(QA.sem, QA.one("silu"))
                act.wait_ge(QV.sem, QV.at("gated", h))
                A(hA[0][:, bass.ds(h * 2, 2), :], qr[:, :, :], ACT.Copy).then_inc(QA.sem, QA.one("o_hi"))

            act.wait_ge(x_landed, 32)
            with act.Fori(0, MT) as t:
                norm_tile(0, t, V_MIX0, hA)
            for j in range(2):
                hi_tile(E_IN, 0, j)
            rough_root(0)
            act.wait_ge(const_landed, 16 * N_CONST)

            def pick_query(b):
                act.wait_ge(q_spread, b)
                A(qm8[:, :], qt8[:, :], ACT.Copy, scale=eye8[:, bass.ds(b, 1)]).then_inc(q_picked, 1)

            def copy_query(b):
                act.wait_ge(q_spread, b + 1)
                act.wait_ge(k_used, PAGES * b)
                for k in range(2):
                    ins = A(qbc[:, k * 512:(k + 1) * 512], m[4 + k][:, :], ACT.Copy)
                ins.then_inc(q_copied, 1)
            for i in range(1, 5):
                for j in range(2):
                    hi_tile(E_IN, i, j)
            act.wait_ge(q8_turned, 1)
            for k in range(2):
                ins = A(qt8[:, k * 512:(k + 1) * 512], m[4 + k][0:8, :], ACT.Copy)
            ins.then_inc(q8_saved, 1)
            act.wait_ge(q8_saved, 1)
            pick_query(0)
            copy_query(0)
            with act.Fori(0, 7) as b:
                pick_query(b + 1)
                for c in range(3):
                    for j in range(2):
                        hi_tile(E_IN, b * 3 + (5 + c), j)
                copy_query(b + 1)
            for i in (26, 27):
                for j in range(2):
                    hi_tile(E_IN, i, j)
            for j in range(2):
                hi_tile(E_OUT, 0, j)
            act.wait_ge(RV.sem, RV.before(2 * HEADS))
            act.wait_ge(k_used, DEC * PAGES)
            with act.Fori(0, HEADS) as h:
                attention_head(h)
            act.wait_ge(SV.sem, SV.at("vs"))
            with act.Fori(0, HEADS) as h:
                hgrn_head(h)
            act.wait_ge(HV.sem, HV.before(HEADS))
            act.wait_ge(h_stored, 32 * HEADS)
            act.wait_ge(SP_.sem, SP_.at("own"))
            A(own[:, :, :], m[0][:, 0:64].rearrange("p (h b) -> p b h", h=HEADS), ACT.Copy).then_inc(SA.sem, SA.one("own"))
            act.wait_ge(SP_.sem, SP_.at("gates"))
            A(G[:, :, :, :].rearrange("p b j h -> p (b j h)"), m[1][:, :], ACT.Copy).then_inc(SA.sem, SA.one("G"))
            act.wait_ge(SV.sem, SV.at("oshift"))
            A(S[:, :, :, :], S[:, :, :, :], ACT.Exp, scale=P ** -0.5).then_inc(SA.sem, SA.one("exp"))
            A(po[:, :, :], po[:, :, :], ACT.Exp, scale=P ** -0.5).then_inc(SA.sem, SA.one("oexp"))
            act.wait_ge(SV.sem, SV.before(1))
            with act.Fori(0, DEC) as b:
                act.wait_ge(v_used, PAGES * b)
                A(Pb[:, :], S[:, bass.ds(b, 1), :, :].rearrange("p o g h -> p (o g h)"), ACT.Copy).then_inc(pb_ready, 1)
                act.wait_ge(o8_ready, b + 1)
                A(oS[:, :, bass.ds(b, 1)].rearrange("p h o -> p (h o)"), m[2][:, 0:HEADS], ACT.Copy).then_inc(v_saved, 1)
            act.wait_ge(TV.sem, TV.at("sum"))
            A(hA[0][:, HEADS:MT, SEQ:TOK], oS2[:, :, :], ACT.Copy).then_inc(TA.sem, TA.one("hi"))
            act.wait_ge(kv_stored, 32)
            body(E_OUT)
            turn_over(E_OUT, F0[0])
            rough_root(1)
            for a, b in zip(F0, F0[1:] + [O_IN]):
                if a is F0[0]:
                    act.wait_ge(cst_landed, 16)
                body(a)
                turn_over(a, b)
            rough_root(2)
            act.wait_ge(cout_stored, 16)
            body(O_IN)
            turn_over(O_IN, O_OUT)
            act.wait_ge(tile_free, O_IN.end())
            with act.Fori(0, HEADS) as h:
                retention_head(h)
            act.wait_ge(QV.sem, QV.before(HEADS))
            act.wait_ge(r_s0_stored, 128 * HEADS)
            act.wait_ge(r_sf_stored, 16 * HEADS)
            body(O_OUT)
            turn_over(O_OUT, F1[0])
            rough_root(3)
            for a, b in zip(F1, F1[1:] + [None]):
                if a is F1[0]:
                    act.wait_ge(cst_landed, 32)
                body(a)
                turn_over(a, b)
            rough_root(4)

        @block.vector
        def _(dve):
            v = nc.vector

            def lo_tile(p, i, j):
                for k in range(4):
                    dve.wait_ge(hi_done, 8 * i + (p.u0 + 4 * j + k + 1))
                    n = p.ktu * P
                    v.tensor_tensor(wlo[:, 4 * j + k, 0:n], raw[:, 4 * j + k, 0:n], whi[:, 4 * j + k, 0:n].bitcast(F32),
                                    ALU.subtract).then_inc(lo_done, 1)

            def clear_sum(n):
                if n:
                    dve.wait_ge(norm_summed, n)
                v.memset(acc[:, :], 0.0).then_inc(acc_cleared, 1)

            def norm_tile(n, t, g, dst):
                dve.wait_ge(NA.sem, t * 2 + NA.at("hi", MT * n))
                v.scalar_tensor_tensor(out=tile(dst[1], t), in0=tile(x, t), scalar=col(t + g),
                                       in1=tile(dst[0], t).bitcast(F32), op0=ALU.mult, op1=ALU.subtract)\
                    .then_inc(NV.sem, NV.one("lo"))
                dve.wait_ge(NA.sem, t * 2 + NA.at("square", MT * n))
                dve.wait_ge(NV.sem, t * 2 + NV.at("lo", MT * n))
                v.tensor_tensor(acc[:, :], acc[:, :], sq[:, :], ALU.add).then_inc(NV.sem, NV.one("sum"))

            def norm_factor(n):
                dve.wait_ge(norm_summed, n + 1)
                v.tensor_scalar(var[:, :], m[5][:, 0:TOK], 1.0 / D_MODEL, EPS, ALU.mult, ALU.add).then_inc(IV.sem, IV.one("var"))

            def refine(root, square, a, b, count, steps, turn):
                v.scalar_tensor_tensor(out=a, in0=square, scalar=-0.5, in1=root, op0=ALU.mult, op1=ALU.mult)\
                    .then_inc(count.sem, count.one(steps[0]))
                dve.wait_ge(count.sem, count.at(steps[0], turn))
                v.tensor_tensor(b, a, root, ALU.mult).then_inc(count.sem, count.one(steps[1]))
                dve.wait_ge(count.sem, count.at(steps[1], turn))
                v.scalar_tensor_tensor(out=root, in0=b, scalar=1.5, in1=root, op0=ALU.add, op1=ALU.mult)\
                    .then_inc(count.sem, count.one(steps[2]))

            def norm_root(n):
                dve.wait_ge(IA.sem, IA.at("rough", n))
                refine(rstd[:, :], var[:, :], sq[:, :], root_tmp[:, :], IV, ("n1", "n2", "rstd"), n)
                dve.wait_ge(IV.sem, IV.at("rstd", n))

            def evac(p, i, j):
                t = 2 * i + j
                if not p.kind.startswith("ffn") or j == 0:
                    dve.wait_ge(unit_used, 4 * t + (p.u0 + 4))
                bank = st[j]
                if p.kind.startswith("z_"):
                    v.tensor_tensor(tile(ze if p.kind == "z_even" else zo, t), bank[:, 0:TOK], rstd[:, :], ALU.mult)\
                        .then_inc(tile_free, 1)
                elif p.kind.startswith("out"):
                    v.tensor_tensor(tile(x, t), bank[:, 0:TOK], tile(x, t), ALU.add).then_inc(tile_free, 1)
                    if p.kind == "out_final":
                        dve.wait_ge(NFA, t + 1)
                        dve.wait_ge(NFV, t)
                        v.tensor_tensor(acc[:, :], acc[:, :], sq[:, :], ALU.add).then_inc(NFV, 1)
                    elif p.kind != "out":
                        n, g = p.norm
                        dve.wait_ge(tile_free, t + (p.t0 + 1))
                        norm_tile(n, t, g, hB if p.kind == "out_norm_hB" else hA)
                elif j == 0:
                    pair = i + p.pair0
                    turn = pair + FT * p.layer
                    w = V_CONV + 4 * FT * p.layer
                    dve.wait_ge(FA.sem, FA.before(turn))
                    v.tensor_tensor(ab[:, PAD:PAD + SEQ], bank[:, 0:SEQ], rstd[:, 0:SEQ], ALU.mult)\
                        .then_inc(FV.sem, FV.one("a_prompt"))
                    v.tensor_tensor(ab_s[:, :, 2], bank[:, SEQ:TOK], rstd[:, SEQ:TOK], ALU.mult).then_inc(tile_free, 1)
                    dve.wait_ge(FA.sem, FA.at("history", turn))
                    dve.wait_ge(tile_free, 2 * i + (p.t0 + 1))
                    v.tensor_scalar(cv1[:, :], ab[:, 0:CONV_OUT], col(pair + w), col(pair + (w + 3 * FT)), ALU.mult, ALU.add)\
                        .then_inc(FV.sem, FV.one("c1"))
                    dve.wait_ge(FV.sem, FV.at("c1", turn))
                    v.scalar_tensor_tensor(out=cv2[:, :], in0=ab[:, 1:1 + CONV_OUT], scalar=col(pair + (w + FT)), in1=cv1[:, :],
                                           op0=ALU.mult, op1=ALU.add).then_inc(FV.sem, FV.one("c2"))
                    dve.wait_ge(FV.sem, FV.at("c2", turn))
                    v.scalar_tensor_tensor(out=cv1[:, :], in0=ab[:, 2:2 + CONV_OUT], scalar=col(pair + (w + 2 * FT)), in1=cv2[:, :],
                                           op0=ALU.mult, op1=ALU.add).then_inc(FV.sem, FV.one("c3"))
                else:
                    pair = i + p.pair0
                    turn = pair + FT * p.layer
                    dve.wait_ge(unit_used, 4 * t + (p.u0 + 4))
                    v.tensor_tensor(bt[:, :], bank[:, 0:TOK], rstd[:, :], ALU.mult).then_inc(tile_free, 1)
                    dve.wait_ge(FA.sem, FA.at("silu", turn))
                    dve.wait_ge(tile_free, 2 * i + (p.t0 + 2))
                    v.tensor_tensor(ug[:, 0:SEQ], sil[:, 0:SEQ], bt[:, 0:SEQ], ALU.mult).then_inc(FV.sem, FV.one("u_prompt"))
                    v.tensor_tensor(ug[:, SEQ:TOK], sil[:, PAD + SEQ:CONV_OUT:3], bt[:, SEQ:TOK], ALU.mult)\
                        .then_inc(FV.sem, FV.one("u_sample"))
                    dst = hid1 if p.kind == "ffn_hid1" else hA
                    dve.wait_ge(FA.sem, FA.at("hid_hi", turn))
                    v.tensor_tensor(tile(dst[1], i), ug[:, :], tile(dst[0], i).bitcast(F32), ALU.subtract)\
                        .then_inc(FV.sem, FV.one("hid_lo"))

            def start_phase(p):
                if p.kind == "out" or p.kind.startswith("out_"):
                    dve.wait_ge(tile_free, p.t0)
                if p.kind.startswith("out_"):
                    clear_sum(p.norm[0])
                    dve.wait_ge(acc_cleared, p.norm[0] + 1)

            def body(p):
                with dve.Fori(0, p.n // 2 - 1) as i:
                    for j in range(2):
                        lo_tile(p, i + 1, j)
                        evac(p, i, j)

            def turn_over(p, nxt):
                for j in range(2):
                    if nxt is not None:
                        lo_tile(nxt, 0, j)
                    evac(p, p.n // 2 - 1, j)

            def rope(first, turn0):
                with dve.Fori(0, 2) as half:
                    for t in range(4):
                        n = half * 4 + (turn0 + t)
                        z_ = ze[0:32, bass.ds(half * 4 + (first + t), 1), :].rearrange("p o n -> p (o n)")
                        dve.wait_ge(RP, n + 1)
                        dve.wait_ge(RV.sem, RV.before(n))
                        v.tensor_tensor(rt[:, 0, :], z_, ropeb[:, 0, :], ALU.mult).then_inc(RV.sem, RV.one("cos"))
                        v.tensor_tensor(rt[:, 1, :], m[t][0:32, 0:TOK], ropeb[:, 1, :], ALU.mult).then_inc(RV.sem, RV.one("sin"))
                        dve.wait_ge(RV.sem, RV.at("sin", n))
                        v.tensor_tensor(z_, rt[:, 0, :], rt[:, 1, :], ALU.add).then_inc(RV.sem, RV.one("add"))

            def score_page(b, g):
                dve.wait_ge(k_landed[g % 4], 64 * b + 16 * (g // 4 + 1))
                for h in range(HEADS):
                    kk = kring[:, g % 4, h * P:(h + 1) * P]
                    ins = v.tensor_tensor_reduce(kk, kk, qbc[:, h * P:(h + 1) * P], 1.0, 0.0, ALU.mult, ALU.add,
                                                 Sb[:, g, h:h + 1])
                ins.then_inc(k_used, 1)

            def save_scores(b):
                dve.wait_ge(k_used, PAGES * (b + 1))
                v.tensor_copy(S[:, bass.ds(b, 1), :, :].rearrange("p o g h -> p (o g h)"),
                              Sb[:, :, :].rearrange("p g h -> p (g h)")).then_inc(s_saved, 1)

            def attention_head(h):
                dve.wait_ge(BP.sem, BP.at("scores", h))
                v.tensor_tensor(sm[:, :], m[0][:, 0:384], cau[:, :], ALU.add).then_inc(BV.sem, BV.one("masked"))
                dve.wait_ge(BV.sem, BV.at("masked", h))
                v.tensor_reduce(mx2[:, 0:1], sm[:, 0:P], AX_X, ALU.max).then_inc(BV.sem, BV.one("max0"))
                v.tensor_reduce(mx2[:, 1:2], sm[:, P:384], AX_X, ALU.max).then_inc(BV.sem, BV.one("max1"))
                dve.wait_ge(BV.sem, BV.at("max1", h))
                v.tensor_scalar(nmx[:, :], mx2[:, :], -(P ** -0.5), None, ALU.mult).then_inc(BV.sem, BV.one("negmax"))
                dve.wait_ge(BA.sem, BA.at("exp1", h))
                v.reciprocal(rl[:, :], lsum[:, :]).then_inc(BV.sem, BV.one("recip"))
                dve.wait_ge(BV.sem, BV.at("recip", h))
                v.tensor_scalar(sm[:, 0:P], sm[:, 0:P], rl[:, 0:1], None, ALU.mult).then_inc(BV.sem, BV.one("p0"))
                v.tensor_scalar(sm[:, P:384], sm[:, P:384], rl[:, 1:2], None, ALU.mult).then_inc(BV.sem, BV.one("p1"))
                dve.wait_ge(BA.sem, BA.at("o_hi", h))
                v.tensor_tensor(tile(hA[1], h + HEADS, 0, SEQ), m[3][:, 0:SEQ], tile(hA[0], h + HEADS, 0, SEQ).bitcast(F32),
                                ALU.subtract).then_inc(BV.sem, BV.one("o_lo"))

            def hgrn_head(h):
                f = tile(ze, h + Z_FA)
                dve.wait_ge(HA.sem, HA.at("ln", h))
                v.scalar_tensor_tensor(out=lsg[:, :], in0=f, scalar=0.0, in1=t1[:, :], op0=ALU.min, op1=ALU.subtract)\
                    .then_inc(HV.sem, HV.one("ls"))
                v.scalar_tensor_tensor(out=t2[:, :], in0=f, scalar=0.0, in1=t1[:, :], op0=ALU.max, op1=ALU.add)\
                    .then_inc(HV.sem, HV.one("mxf"))
                dve.wait_ge(HA.sem, HA.at("ei", h))
                v.tensor_scalar(sg[:, :], sg[:, :], 1.0, None, ALU.add).then_inc(HV.sem, HV.one("g1"))
                dve.wait_ge(HV.sem, HV.at("g1", h))
                v.reciprocal(sg[:, :], sg[:, :]).then_inc(HV.sem, HV.one("sg"))
                v.tensor_scalar(va[:, :], va[:, :], 1.0, None, ALU.add).then_inc(HV.sem, HV.one("i1"))
                dve.wait_ge(HV.sem, HV.at("i1", h))
                v.reciprocal(va[:, :], va[:, :]).then_inc(HV.sem, HV.one("ir"))
                dve.wait_ge(HV.sem, HV.at("ir", h))
                v.tensor_tensor(va[:, :], va[:, :], tile(ze, h + Z_IA), ALU.mult).then_inc(HV.sem, HV.one("va"))
                v.tensor_tensor_scan(bcum[:, :], reset[:, :], lsg[:, 0:SEQ], 0.0, ALU.mult, ALU.add).then_inc(HV.sem, HV.one("cum"))
                dve.wait_ge(HV.sem, HV.at("cum", h))
                for l in range(LEVELS):
                    B = 1 << l
                    bv = bcum[:, :].rearrange("p (n w) -> p n w", w=2 * B)
                    ev = EL[:, l, :].rearrange("p (n w) -> p n w", w=2 * B)
                    ref = bv[:, :, B - 1:B].to_broadcast([P, SEQ // (2 * B), B])
                    v.tensor_tensor(ev[:, :, 0:B], ref, bv[:, :, 0:B], ALU.subtract).then_inc(HV.sem, HV.one(f"d{l}l"))
                    v.tensor_tensor(ev[:, :, B:2 * B], bv[:, :, B:2 * B], ref, ALU.subtract).then_inc(HV.sem, HV.one(f"d{l}r"))
                dve.wait_ge(HA.sem, HA.at("levels", h))
                for c in range(2):
                    s = slice(c * P, (c + 1) * P)
                    if c:
                        dve.wait_ge(HP.sem, HP.at("lev0", h))
                    q_ = ze[:, bass.ds(h + Z_QA, 1), s].to_broadcast([P, LEVELS, P])
                    v.tensor_tensor(QE[:, :, :], EL[:, :, s], q_, ALU.mult).then_inc(HV.sem, HV.one(f"qe{c}"))
                    v.tensor_tensor(KE[:, :, :], EL[:, :, s], ka[:, None, s].to_broadcast([P, LEVELS, P]), ALU.mult)\
                        .then_inc(HV.sem, HV.one(f"ke{c}"))
                    dve.wait_ge(HP.sem, HP.at(f"lev{c}", h))
                    v.tensor_tensor(pr[:, 0:4, :], m[0][:, :].rearrange("p (l t) -> p l t", l=4), levm[:, 0:4, :], ALU.mult)\
                        .then_inc(HV.sem, HV.one(f"pr{c}a"))
                    v.tensor_tensor(pr[:, 4:7, :], m[1][:, 0:384].rearrange("p (l t) -> p l t", l=3), levm[:, 4:7, :], ALU.mult)\
                        .then_inc(HV.sem, HV.one(f"pr{c}b"))
                    dve.wait_ge(HV.sem, HV.at(f"pr{c}b", h))
                    v.tensor_reduce(Aatt[:, c, :], pr[:, :, :].rearrange("p l t -> p t l"), AX_X, ALU.add)\
                        .then_inc(HV.sem, HV.one(f"att{c}"))
                bc = bcum[:, :].rearrange("p (c n) -> p c n", n=CHUNK)
                v.tensor_tensor(t2[:, 0:SEQ].rearrange("p (c n) -> p c n", n=CHUNK), bc[:, :, CHUNK - 1:CHUNK].to_broadcast([P, NCH, CHUNK]),
                                bc, ALU.subtract).then_inc(HV.sem, HV.one("dk"))
                dve.wait_ge(HA.sem, HA.at("dke", h))
                v.tensor_tensor(t2[:, 0:SEQ], t2[:, 0:SEQ], ka[:, 0:SEQ], ALU.mult).then_inc(HV.sem, HV.one("kd"))
                dve.wait_ge(HA.sem, HA.at("eb", h))
                v.tensor_tensor(qdec[:, :], t1[:, 0:SEQ], tile(ze, h + Z_QA, 0, SEQ), ALU.mult).then_inc(HV.sem, HV.one("qdec"))
                dve.wait_ge(HP.sem, HP.at("U", h))
                dve.wait_ge(h_stored, 32 * h)
                v.tensor_copy(Sst[:, 0, :], m[4][:, 0:P]).then_inc(HV.sem, HV.one("s1"))
                for c in range(1, NCH):
                    dve.wait_ge(HV.sem, HV.at(f"s{c}", h))
                    v.scalar_tensor_tensor(out=Sst[:, c, :], in0=Sst[:, c - 1, :], scalar=ebl[:, c:c + 1],
                                           in1=m[4 - c % 2][:, (c // 2) * P:(c // 2 + 1) * P], op0=ALU.mult, op1=ALU.add)\
                        .then_inc(HV.sem, HV.one(f"s{c + 1}"))
                dve.wait_ge(HA.sem, HA.at("kv8", h))
                v.tensor_tensor(vm8[:, :, :], kv8[:, None, P:2 * P].to_broadcast([8, 8, P]), eye8[:, :, None].to_broadcast([8, 8, P]),
                                ALU.mult).then_inc(HV.sem, HV.one("vm"))
                v.tensor_tensor(qm[:, :, :], ze[:, bass.ds(h + Z_QA, 1), SEQ:TOK].to_broadcast([P, 8, 8]), eye[:, :, :], ALU.mult)\
                    .then_inc(HV.sem, HV.one("qm"))
                dve.wait_ge(h_s0_landed, 16 * h + 16)
                for b in range(DEC):
                    if b % 4 == 0:
                        dve.wait_ge(HP.sem, HP.at("kv_a" if b == 0 else "kv_b", h))
                    v.scalar_tensor_tensor(out=S0[:, b, :], in0=S0[:, b, :], scalar=fg[:, b:b + 1],
                                           in1=m[1 + b // 4][:, (b % 4) * P:(b % 4 + 1) * P], op0=ALU.mult, op1=ALU.add)\
                        .then_inc(HV.sem, HV.one(f"sn{b}"))
                dve.wait_ge(HP.sem, HP.at("ssum", h))
                v.tensor_scalar(lsg[:, :], m[0][:, 0:TOK], 1.0 / P, EPS, ALU.mult, ALU.add).then_inc(HV.sem, HV.one("var"))
                dve.wait_ge(HA.sem, HA.at("rough", h))
                refine(t1[:, :], lsg[:, :], t2[:, :], ka[:, :], HV, ("n1", "n2", "rstd"), h)
                dve.wait_ge(HV.sem, HV.at("rstd", h))
                v.scalar_tensor_tensor(out=t1[:, :], in0=oT[:, :], scalar=col(h + V_GNH), in1=t1[:, :], op0=ALU.mult, op1=ALU.mult)\
                    .then_inc(HV.sem, HV.one("og"))
                dve.wait_ge(HV.sem, HV.at("og", h))
                v.tensor_tensor(t2[:, :], t1[:, :], sg[:, :], ALU.mult).then_inc(HV.sem, HV.one("gated"))
                dve.wait_ge(HA.sem, HA.at("o_hi", h))
                v.tensor_tensor(tile(hA[1], h), t2[:, :], tile(hA[0], h).bitcast(F32), ALU.subtract).then_inc(HV.sem, HV.one("o_lo"))

            def select_blocks():
                v.memset(cmp[:, :, :, :], 0.0).then_inc(SV.sem, SV.one("clear_cmp"))
                v.memset(rank[:, :, :, :], 0.0).then_inc(SV.sem, SV.one("rank0"))
                dve.wait_ge(SA.sem, SA.at("G"))
                last = "rank0"
                for i in range(BLOCKS):
                    dve.wait_ge(SV.sem, SV.at(last))
                    if i > 0:
                        v.tensor_tensor(cmp[:, :, 0:i, :], G[:, :, i:i + 1, :].to_broadcast([P, DEC, i, HEADS]), G[:, :, 0:i, :],
                                        ALU.is_gt).then_inc(SV.sem, SV.one(f"gt{i}"))
                        last = f"gt{i}"
                    if i < BLOCKS - 1:
                        n = BLOCKS - 1 - i
                        v.tensor_tensor(cmp[:, :, i + 1:BLOCKS, :], G[:, :, i:i + 1, :].to_broadcast([P, DEC, n, HEADS]),
                                        G[:, :, i + 1:BLOCKS, :], ALU.is_ge).then_inc(SV.sem, SV.one(f"ge{i}"))
                        last = f"ge{i}"
                    dve.wait_ge(SV.sem, SV.at(last))
                    if i > 0:
                        ins = v.tensor_tensor(rank[:, :, 0:i, :], rank[:, :, 0:i, :], cmp[:, :, 0:i, :], ALU.add)
                    if i < BLOCKS - 1:
                        ins = v.tensor_tensor(rank[:, :, i + 1:BLOCKS, :], rank[:, :, i + 1:BLOCKS, :], cmp[:, :, i + 1:BLOCKS, :], ALU.add)
                    ins.then_inc(SV.sem, SV.one(f"add{i}"))
                    last = f"add{i}"
                dve.wait_ge(SV.sem, SV.at(last))
                v.tensor_scalar(cmp[:, :, :, :], rank[:, :, :, :], float(TOPK), -1.0, ALU.is_lt, ALU.add).then_inc(SV.sem, SV.one("keep"))
                dve.wait_ge(SV.sem, SV.at("keep"))
                v.tensor_scalar(cmp[:, :, :, :], cmp[:, :, :, :], BIG, None, ALU.mult).then_inc(SV.sem, SV.one("minus"))
                dve.wait_ge(SV.sem, SV.at("minus"))
                Sv = S[:, :, :, :].rearrange("p b (j two) h -> p (b j) two h", two=2)
                kb = cmp[:, :, :, :].rearrange("p b j h -> p (b j) h")[:, :, None, :].to_broadcast([P, DEC * BLOCKS, 2, HEADS])
                dve.wait_ge(SP_.sem, SP_.at("gates"))
                v.tensor_tensor(Sv, Sv, kb, ALU.add).then_inc(SV.sem, SV.one("bias"))
                dve.wait_ge(SV.sem, SV.at("bias"))
                v.tensor_reduce(mxt[:, :, :], S[:, :, :, :].rearrange("p b g h -> p b h g"), AX_X, ALU.max).then_inc(SV.sem, SV.one("tmax"))
                dve.wait_ge(SP_.sem, SP_.at("mxT"))
                v.tensor_reduce(mx64[:, :], m[2][0:64, 0:P], AX_X, ALU.max).then_inc(SV.sem, SV.one("rmax"))
                dve.wait_ge(SV.sem, SV.at("rmax"))
                v.tensor_scalar(dg[:, :], ident[0:64, 0:64], mx64[:, :], None, ALU.mult).then_inc(SV.sem, SV.one("diag"))
                dve.wait_ge(SP_.sem, SP_.at("mxb"))
                v.tensor_tensor(mxa[:, :, :], m[3][:, 0:64].rearrange("p (b h) -> p b h", b=DEC), own[:, :, :], ALU.max)\
                    .then_inc(SV.sem, SV.one("mxa"))
                dve.wait_ge(SV.sem, SV.at("mxa"))
                v.tensor_tensor(S[:, :, :, :], S[:, :, :, :], mxa[:, :, None, :].to_broadcast([P, DEC, PAGES, HEADS]), ALU.subtract)\
                    .then_inc(SV.sem, SV.one("shift"))
                v.tensor_tensor(po[:, :, :], own[:, :, :], mxa[:, :, :], ALU.subtract).then_inc(SV.sem, SV.one("oshift"))
                dve.wait_ge(SA.sem, SA.at("oexp"))
                v.tensor_reduce(mxt[:, :, :], S[:, :, :, :].rearrange("p b g h -> p b h g"), AX_X, ALU.add).then_inc(SV.sem, SV.one("tsum"))
                dve.wait_ge(SP_.sem, SP_.at("den"))
                v.tensor_tensor(mxa[:, :, :], m[4][:, 0:64].rearrange("p (b h) -> p b h", b=DEC), po[:, :, :], ALU.add)\
                    .then_inc(SV.sem, SV.one("den"))
                dve.wait_ge(SV.sem, SV.at("den"))
                v.reciprocal(own[:, :, :], mxa[:, :, :]).then_inc(SV.sem, SV.one("rden"))
                dve.wait_ge(SV.sem, SV.at("rden"))
                v.tensor_tensor(S[:, :, :, :], S[:, :, :, :], own[:, :, None, :].to_broadcast([P, DEC, PAGES, HEADS]), ALU.mult)\
                    .then_inc(SV.sem, SV.one("p"))
                v.tensor_tensor(po[:, :, :], po[:, :, :], own[:, :, :], ALU.mult).then_inc(SV.sem, SV.one("po"))

            def retention_head(h):
                for w, first, dst, s in (("q", Z_Q, qr, 1.0), ("k", Z_K, kr, RK ** -0.5)):
                    x1, x2 = tile(zo, h * 2 + first), tile(zo, h * 2 + (first + 1))
                    if w == "q":
                        dve.wait_ge(QA.sem, QA.before(h))
                        dve.wait_ge(QP.sem, QP.before(h))
                        dve.wait_ge(QV.sem, QV.before(h))
                    else:
                        dve.wait_ge(QV.sem, QV.at("qx2", h))
                    for a, b, o, op, n in ((x1, x2, 0, ALU.subtract, ("a", "b", "x1")), (x2, x1, 1, ALU.add, ("c", "d", "x2"))):
                        if o:
                            dve.wait_ge(QV.sem, QV.at(w + "x1", h))
                        v.scalar_tensor_tensor(out=r1[:, :], in0=a, scalar=s, in1=ropec[:, 0, :], op0=ALU.mult, op1=ALU.mult)\
                            .then_inc(QV.sem, QV.one(w + n[0]))
                        v.scalar_tensor_tensor(out=r2[:, :], in0=b, scalar=s, in1=ropec[:, 1, :], op0=ALU.mult, op1=ALU.mult)\
                            .then_inc(QV.sem, QV.one(w + n[1]))
                        dve.wait_ge(QV.sem, QV.at(w + n[1], h))
                        v.tensor_tensor(dst[:, o, :], r1[:, :], r2[:, :], op).then_inc(QV.sem, QV.one(w + n[2]))
                dve.wait_ge(QP.sem, QP.at("att", h))
                dve.wait_ge(dm_landed, 16 * h + 16)
                v.tensor_tensor(aT[:, :], m[0][:, 0:384], dmat[:, :], ALU.mult).then_inc(QV.sem, QV.one("att"))
                dve.wait_ge(QP.sem, QP.at("k_turned", h))
                for s in range(2):
                    v.tensor_scalar(rk_[:, s, :], m[2][:, s * RK:(s + 1) * RK],
                                    sdec[:, bass.ds(h, 1), s:s + 1].rearrange("p o n -> p (o n)"), None, ALU.mult)\
                        .then_inc(QV.sem, QV.one(f"k{s}"))
                for d in range(2):
                    ins = v.tensor_tensor(rqm[:, d, :, :], qr[:, d:d + 1, SEQ:TOK].to_broadcast([P, 8, 8]), reye[:, :, :], ALU.mult)
                ins.then_inc(QV.sem, QV.one("qm"))
                dve.wait_ge(QA.sem, QA.at("kv8", h))
                for q in range(4):
                    if q:
                        dve.wait_ge(QP.sem, QP.at(f"kv{q - 1}1", h))
                    v.tensor_tensor(rvm[:, :, :], rkv8[:, None, RK:2 * RK].to_broadcast([8, 2, RK]),
                                    reye8[:, 2 * q:2 * q + 2, None].to_broadcast([8, 2, RK]), ALU.mult)\
                        .then_inc(QV.sem, QV.one(f"vm{q}"))
                    dve.wait_ge(r_s0_landed[q % 2], 64 * h + 32 * (q // 2) + 32)
                    for d in range(2):
                        dve.wait_ge(QP.sem, QP.at(f"kv{q}{d}", h))
                        v.scalar_tensor_tensor(out=R0[:, q % 2, :, d, :], in0=R0[:, q % 2, :, d, :], scalar=gam[:, bass.ds(h, 1)],
                                               in1=m[1 + d][:, :].rearrange("p (b e) -> p b e", b=2), op0=ALU.mult, op1=ALU.add)\
                            .then_inc(QV.sem, QV.one(f"s{d}_{q}"))
                dve.wait_ge(QP.sem, QP.at("ssum", h))
                v.tensor_scalar(r1[:, :], m[2][:, 0:TOK], 1.0 / RK, None, ALU.mult).then_inc(QV.sem, QV.one("mean"))
                dve.wait_ge(QV.sem, QV.at("mean", h))
                v.tensor_tensor(roT[:, :, :], roT[:, :, :], r1[:, None, :].to_broadcast([P, 2, TOK]), ALU.subtract)\
                    .then_inc(QV.sem, QV.one("oc"))
                dve.wait_ge(QP.sem, QP.at("vsum", h))
                v.tensor_scalar(r2[:, :], m[3][:, 0:TOK], 1.0 / RK, EPS, ALU.mult, ALU.add).then_inc(QV.sem, QV.one("var"))
                dve.wait_ge(QA.sem, QA.at("rough", h))
                refine(qr[:, 0, :], r2[:, :], r1[:, :], qr[:, 1, :], QV, ("n1", "n2", "rstd"), h)
                dve.wait_ge(QV.sem, QV.at("rstd", h))
                for e in range(2):
                    ins = v.scalar_tensor_tensor(out=roT[:, e, :], in0=roT[:, e, :], scalar=col(h * 2 + (V_GNR + e)), in1=qr[:, 0, :],
                                                 op0=ALU.mult, op1=ALU.mult)
                ins.then_inc(QV.sem, QV.one("og"))
                dve.wait_ge(QV.sem, QV.at("og", h))
                dve.wait_ge(QA.sem, QA.at("silu", h))
                v.tensor_tensor(qr[:, :, :], roT[:, :, :], vw[:, :, :], ALU.mult).then_inc(QV.sem, QV.one("gated"))
                dve.wait_ge(QA.sem, QA.at("o_hi", h))
                v.tensor_tensor(hA[1][:, bass.ds(h * 2, 2), :], qr[:, :, :], hA[0][:, bass.ds(h * 2, 2), :].bitcast(F32), ALU.subtract)\
                    .then_inc(QV.sem, QV.one("o_lo"))

            v.memset(ones[:, :], 1.0).then_inc(consts_set, 1)
            clear_sum(0)
            dve.wait_ge(acc_cleared, 1)
            dve.wait_ge(x_landed, 32)
            with dve.Fori(0, MT) as t:
                norm_tile(0, t, V_MIX0, hA)
            norm_factor(0)
            for j in range(2):
                lo_tile(E_IN, 0, j)
            norm_root(0)
            with dve.Fori(0, 4) as i:
                for j in range(2):
                    lo_tile(E_IN, i + 1, j)
                    evac(E_IN, i, j)
            dve.wait_ge(const_landed, 16 * N_CONST)
            dve.wait_ge(tile_free, HEADS)
            rope(Z_QB, 0)
            share = (3, 3, 3, 3, 2, 2)
            with dve.Fori(0, 7) as b:
                g = 0
                dve.wait_ge(q_copied, b + 1)
                for n, k in enumerate(share):
                    lo_tile(E_IN, b * 3 + (5 + n // 2), n % 2)
                    evac(E_IN, b * 3 + (4 + n // 2), n % 2)
                    if n == 0:
                        dve.wait_ge(s_saved, b)
                    for _ in range(k):
                        score_page(b, g)
                        g += 1
                save_scores(b)
            for i in (26, 27):
                for j in range(2):
                    lo_tile(E_IN, i, j)
                    evac(E_IN, i - 1, j)
            dve.wait_ge(q_copied, DEC)
            dve.wait_ge(s_saved, DEC - 1)
            for g in range(PAGES):
                score_page(7, g)
            save_scores(7)
            turn_over(E_IN, E_OUT)
            dve.wait_ge(tile_free, ZE)
            rope(Z_KB, HEADS)
            dve.wait_ge(RV.sem, RV.before(2 * HEADS))
            with dve.Fori(0, HEADS) as h:
                attention_head(h)
            dve.wait_ge(BV.sem, BV.before(HEADS))
            v.tensor_tensor(qk[:, :, :], ze[:, Z_QB:Z_QB + HEADS, SEQ:TOK], ze[:, Z_KB:Z_KB + HEADS, SEQ:TOK], ALU.mult)\
                .then_inc(SV.sem, SV.one("qk"))
            v.tensor_copy(vs[:, :, :], ze[:, Z_VB:Z_VB + HEADS, SEQ:TOK]).then_inc(SV.sem, SV.one("vs"))
            dve.wait_ge(SV.sem, SV.at("vs"))
            dve.wait_ge(hc_landed, 32)
            with dve.Fori(0, HEADS) as h:
                hgrn_head(h)
            dve.wait_ge(HV.sem, HV.before(HEADS))
            dve.wait_ge(HP.sem, HP.before(HEADS))
            dve.wait_ge(h_stored, 32 * HEADS)
            select_blocks()
            dve.wait_ge(sel_landed, 16)
            with dve.Fori(0, DEC) as b:
                dve.wait_ge(v_used, PAGES * (b + 1))
                dve.wait_ge(o8_ready, b)
                for k in range(2):
                    v.tensor_tensor(om[:, k * 512:(k + 1) * 512], m[k][0:8, :], blk[:, k * 512:(k + 1) * 512], ALU.mult)\
                        .then_inc(om_ready, 1)
            dve.wait_ge(SV.sem, SV.before(1))
            v.tensor_tensor(oS2[:, :, :], po[:, :, :].rearrange("p b h -> p h b"), vs[:, :, :], ALU.mult)\
                .then_inc(TV.sem, TV.one("pv"))
            dve.wait_ge(v_saved, DEC)
            dve.wait_ge(TV.sem, TV.at("pv"))
            v.tensor_tensor(oS2[:, :, :], oS2[:, :, :], oS[:, :, :], ALU.add).then_inc(TV.sem, TV.one("sum"))
            dve.wait_ge(TA.sem, TA.at("hi"))
            v.tensor_tensor(hA[1][:, HEADS:MT, SEQ:TOK], oS2[:, :, :], hA[0][:, HEADS:MT, SEQ:TOK].bitcast(F32), ALU.subtract)\
                .then_inc(TV.sem, TV.one("lo"))
            dve.wait_ge(kv_stored, 32)
            start_phase(E_OUT)
            body(E_OUT)
            turn_over(E_OUT, F0[0])

            def clear_pad(n):
                v.memset(ab[:, 0:PAD], 0.0).then_inc(ab_cleared, 1)
                dve.wait_ge(ab_cleared, n)
            norm_factor(1)
            norm_root(1)
            clear_pad(1)
            for a, b in zip(F0, F0[1:] + [O_IN]):
                start_phase(a)
                body(a)
                turn_over(a, b)
            norm_factor(2)
            norm_root(2)
            dve.wait_ge(cout_stored, 16)
            body(O_IN)
            turn_over(O_IN, O_OUT)
            dve.wait_ge(tile_free, O_IN.end())
            dve.wait_ge(oc_landed, 16 * 5)
            with dve.Fori(0, HEADS) as h:
                retention_head(h)
            dve.wait_ge(QV.sem, QV.before(HEADS))
            dve.wait_ge(QP.sem, QP.before(HEADS))
            dve.wait_ge(r_s0_stored, 128 * HEADS)
            dve.wait_ge(r_sf_stored, 16 * HEADS)
            start_phase(O_OUT)
            body(O_OUT)
            turn_over(O_OUT, F1[0])
            norm_factor(3)
            norm_root(3)
            clear_pad(2)
            for a, b in zip(F1, F1[1:] + [None]):
                start_phase(a)
                body(a)
                turn_over(a, b)
            norm_factor(4)
            norm_root(4)
            with dve.Fori(0, MT) as t:
                v.scalar_tensor_tensor(out=tile(x, t), in0=tile(x, t), scalar=col(t + V_FINAL), in1=rstd[:, :],
                                       op0=ALU.mult, op1=ALU.mult).then_inc(y_ready, 1)

        @block.gpsimd
        def _(pool):
            pool.dma_start(pt[:, :], page_table).then_inc(pt_landed, 16)
            pool.wait_ge(pt_landed, 16)

            def load_page(cache, ring, b, g, landed, used, first):
                page = pool.snap(pool.value_load(pt[0:1, bass.ds(b * PAGES + g, 1)], min_val=0, max_val=cache.shape[0] - 1))
                if not first:
                    pool.wait_ge(used, b * PAGES + (g - 3))
                pool.dma_start(ring[:, g % 4, :], cache[bass.ds(page, 1), :, :].rearrange("o t n -> t (o n)"))\
                    .then_inc(landed[g % 4], 16)

            for g in range(PAGES):
                load_page(cache_k, kring, 0, g, k_landed, k_used, g < 4)
            with pool.Fori(1, DEC) as b:
                for g in range(PAGES):
                    load_page(cache_k, kring, b, g, k_landed, k_used, False)
            pool.wait_ge(tile_free, ZE)
            pool.wait_ge(RV.sem, RV.before(2 * HEADS))
            pool.dma_start(kT_out, ze[:, Z_KB:Z_KB + HEADS, :]).then_inc(kv_stored, 16)
            pool.dma_start(vT_out, ze[:, Z_VB:Z_VB + HEADS, :]).then_inc(kv_stored, 16)
            pool.wait_ge(BV.sem, BV.before(HEADS))
            pool.wait_ge(BP.sem, BP.before(HEADS))
            pool.wait_ge(BA.sem, BA.before(HEADS))
            pool.wait_ge(SV.sem, SV.at("vs"))
            pool.wait_ge(kv_stored, 32)
            pool.dma_start(levm[:, :, :], c_level).then_inc(hc_landed, 16)
            pool.dma_start(reset[:, :], c_reset).then_inc(hc_landed, 16)
            pool.wait_ge(HV.sem, HV.before(HEADS))
            pool.wait_ge(HP.sem, HP.before(HEADS))
            pool.wait_ge(HA.sem, HA.before(HEADS))
            pool.wait_ge(h_stored, 32 * HEADS)
            pool.dma_start(blk[:, :], c_blk).then_inc(sel_landed, 16)
            for g in range(PAGES):
                load_page(cache_v, vring, 0, g, v_landed, v_used, g < 4)
            with pool.Fori(1, DEC) as b:
                for g in range(PAGES):
                    load_page(cache_v, vring, b, g, v_landed, v_used, False)
            pool.wait_ge(TV.sem, TV.before(1))
            pool.wait_ge(kv_stored, 32)
            pool.dma_start(cst[:, :, :], conv_state[0]).then_inc(cst_landed, 16)
            pool.wait_ge(FA.sem, FA.before(FT))
            pool.dma_start(conv_out[0], cout[:, :, :]).then_inc(cout_stored, 16)
            pool.wait_ge(cout_stored, 16)
            pool.wait_ge(FV.sem, FV.before(FT))
            for dst, src in ((ropec[:, :, :], c_rope_c), (sdec[:, :, :], c_sdec), (gam[:, :], c_gamma), (reye8[:, :], c_eye8),
                             (reye[:, :, :], c_eye)):
                pool.dma_start(dst, src).then_inc(oc_landed, 16)

            pool.wait_ge(QA.sem, QA.before(HEADS))
            pool.wait_ge(QV.sem, QV.before(HEADS))
            pool.wait_ge(QP.sem, QP.before(HEADS))
            pool.wait_ge(r_s0_stored, 128 * HEADS)
            pool.wait_ge(r_sf_stored, 16 * HEADS)
            pool.dma_start(cst[:, :, :], conv_state[1]).then_inc(cst_landed, 16)
            pool.wait_ge(FA.sem, FA.before(2 * FT))
            pool.dma_start(conv_out[1], cout[:, :, :]).then_inc(cout_stored, 16)
            pool.wait_ge(cout_stored, 32)


def _tiles(w, ktu):
    k, n = w.shape
    return np.ascontiguousarray(w.reshape(2, k // 256, P, n // P, P).transpose(3, 0, 2, 1, 4)).reshape(n // P, 2, P, 2 * ktu * P)


def _columns(a):
    return np.ascontiguousarray(a.reshape(-1, P).T)


def _constants():
    f = np.float32
    pos = np.concatenate([np.arange(SEQ), np.full(DEC, 2048)]).astype(f)

    def angles(half, theta):
        inv = f(theta) ** (-np.arange(half, dtype=f) / f(half))
        return (pos[None, :] * inv.astype(f)[:, None]).astype(f)
    ab_, ac = angles(16, 500000.0), angles(P, 10000.0)
    rope_b = np.stack([np.concatenate([np.cos(ab_)] * 2), np.concatenate([-np.sin(ab_), np.sin(ab_)])], 1).astype(f)
    rope_c = np.stack([np.cos(ac), np.sin(ac)], 1).astype(f)
    perm = np.zeros((32, 32), f)
    perm[np.arange(32), (np.arange(32) + 16) % 32] = 1
    i = np.arange(P)
    causal = np.where(i[None, :] <= i[:, None], 0, -BIG).astype(f)
    cau = np.concatenate([causal, np.zeros((P, P), f), causal], 1)
    lg = np.log(1.0 - 2.0 ** (-5.0 - np.arange(HEADS)))
    t = np.arange(SEQ)
    d = np.where(t[None, :] >= t[:, None], t[None, :] - t[:, None], 0)
    full = np.where(t[None, :] >= t[:, None], np.exp(d * lg[:, None, None]), 0.0)
    decay = np.concatenate([full[:, 0:P, :], full[:, P:, P:]], 2).astype(f)
    sdec = np.exp((SEQ - 1 - t)[None, :] * lg[:, None]).reshape(HEADS, 2, P).transpose(2, 0, 1).astype(f)
    gamma = np.broadcast_to(np.exp(lg)[None, :], (P, HEADS)).astype(f)
    level = np.zeros((P, LEVELS + 1, P), f)
    for l in range(LEVELS):
        B = 1 << l
        level[:, l, :] = ((i[:, None] // (2 * B)) == (i[None, :] // (2 * B))) & (i[:, None] % (2 * B) < B) & (i[None, :] % (2 * B) >= B)
    level[:, LEVELS, :] = np.eye(P)
    reset = np.broadcast_to((t % CHUNK != 0).astype(f), (P, SEQ))
    return {
        "c_ident": np.eye(P, dtype=f), "c_eye8": np.eye(8, dtype=f),
        "c_eye": np.broadcast_to(np.eye(8, dtype=f), (P, 8, 8)), "c_blk": np.kron(np.eye(8), np.ones((1, P))).astype(f),
        "c_causal": cau, "c_rope_b": rope_b, "c_perm": perm, "c_rope_c": rope_c, "c_decay": decay, "c_sdec": sdec,
        "c_gamma": gamma, "c_level": level, "c_reset": reset,
    }


_OUTS = [("y_out", (P, MT, TOK)), ("kT_out", (P, HEADS, TOK)), ("vT_out", (P, HEADS, TOK)), ("hgrn_p_out", (HEADS, P, P)),
         ("hgrn_s_out", (DEC, HEADS, P, P)), ("ret_p_out", (HEADS, RK, RK)), ("ret_s_out", (DEC, HEADS, RK, RK)),
         ("conv_out", (2, P, FT, PAD + 2 * DEC))]


def _layout(inp):
    x = np.concatenate([inp["x_prompt"][0], inp["x_sample"][:, 0]], 0)
    a = {"x_in": x.T.reshape(MT, P, TOK).transpose(1, 0, 2)}
    a["vecs"] = np.concatenate(
        [_columns(inp[n][l]) for l in range(2) for n in ("norm_mix", "norm_ffn")]
        + [_columns(inp["norm_final"]), _columns(inp["gn_hgrn"]), _columns(inp["gn_ret"])]
        + [b for l in range(2) for b in (_columns(inp["conv_w"][l]), _columns(inp["conv_b"][l]))], 1)
    a["conv_state"] = inp["state_conv"].transpose(0, 3, 1, 2).reshape(2, FT, P, 2 * DEC).transpose(0, 2, 1, 3)
    w = inp["w_in_even"][0]
    A, B = 4 * HEADS * P, HEADS * P
    a["w_even_in"] = _tiles(np.concatenate([w[:, A:A + 3 * B], w[:, :A]], 1), 4)
    a["w_even_out"] = _tiles(inp["w_out_even"][0], 4)
    a["w_odd_in"] = _tiles(inp["w_in_odd"][0], 4)
    a["w_odd_out"] = _tiles(inp["w_out_odd"][0], 4)
    for l in range(2):
        t = _tiles(inp["w_ffn_in"][l], 4)
        a[f"w_f{l}_in"] = t.reshape(2, FT, 2, P, 8 * P).transpose(1, 0, 2, 3, 4).reshape(2 * FT, 2, P, 8 * P)
        r = 0
        for n, c in enumerate(CHUNKS):
            a[f"w_f{l}_o{n}"] = _tiles(inp["w_ffn_out"][l][r * P:(r + c) * P], c // 4)
            r += c
    for n in ("cache_k", "cache_v"):
        a[n] = inp[n][0].reshape(-1, PAGE, HEADS * P)
    a["page_table"] = inp["page_table"].reshape(1, -1)
    a["state_hgrn"], a["state_ret"] = inp["state_hgrn"][0], inp["state_ret"][0]
    a.update(_constants())
    return {k: np.ascontiguousarray(v) for k, v in a.items()}


def kernel(**inputs):
    import concourse.bacc as bacc
    from concourse.bass_utils import run_bass_kernel_spmd as run
    inputs = {k: np.asarray(v) for k, v in inputs.items()}
    arrays = _layout(inputs)
    nc = bacc.Bacc("TRN2", target_bir_lowering=False, num_devices=1)
    aps = {k: nc.dram_tensor("in_" + k, a.shape, mybir.dt.from_np(a.dtype), kind="ExternalInput").ap() for k, a in arrays.items()}
    for k, shape in _OUTS:
        aps[k] = nc.dram_tensor("out_" + k, shape, F32, kind="ExternalOutput").ap()
    hybrid_step(nc, **aps)
    r = run(nc, [{"in_" + k: a for k, a in arrays.items()}], core_ids=[0]).results[0]
    o = {k: np.asarray(r["out_" + k]) for k, _ in _OUTS}

    def rows(t):
        return np.ascontiguousarray(t.transpose(2, 1, 0).reshape(TOK, -1))
    y, k, v = rows(o["y_out"]), rows(o["kT_out"]), rows(o["vT_out"])
    c = o["conv_out"].transpose(0, 3, 2, 1).reshape(2, PAD + 2 * DEC, D_FF)
    return (y[:SEQ][None], y[SEQ:][:, None],
            k[:SEQ].reshape(1, 1, SEQ, HEADS, P), v[:SEQ].reshape(1, 1, SEQ, HEADS, P),
            k[SEQ:].reshape(1, DEC, 1, HEADS, P), v[SEQ:].reshape(1, DEC, 1, HEADS, P),
            o["hgrn_p_out"][None, None], o["hgrn_s_out"][None], o["ret_p_out"][None, None], o["ret_s_out"][None],
            np.ascontiguousarray(c[:, None, :PAD]), np.ascontiguousarray(c[:, PAD:].reshape(2, DEC, 2, D_FF)))
```

```python
from contextlib import ExitStack

import numpy as np

import concourse.bass as bass
from concourse import mybir

F32 = mybir.dt.float32
F32R = mybir.dt.float32r
I32 = mybir.dt.int32
ALU = mybir.AluOpType
ACT = mybir.ActivationFunctionType
AX_X = mybir.AxisListType.X

P = 128
SEQ, DEC = 256, 8
TOK = SEQ + DEC
D_MODEL, D_FF = 2048, 5632
MT = D_MODEL // P
FT = D_FF // P
HEADS = 8
PAGES = 16
PAGE = 128
BLOCKS = 8
TOPK = 3
CHUNK = 64
NCH = SEQ // CHUNK
LEVELS = 6
EPS = 1e-6
RK = 256
SLOTS = 8
UNIT = 4 * P
BIG = 1e30
CHUNKS = (16, 16, 12)
PAD = 2
CONV_COLS = PAD + SEQ + 3 * DEC
CONV_OUT = CONV_COLS - 2

V_MIX0, V_FFN0, V_MIX1, V_FFN1, V_FINAL = (MT * n for n in range(5))
V_GNH = 5 * MT
V_GNR = V_GNH + HEADS
V_CONV = V_GNR + 2 * HEADS
V_ALL = V_CONV + 2 * 4 * FT

Z_QB, Z_KB, Z_VB, Z_QA, Z_FA, Z_IA, Z_GA = (HEADS * n for n in range(7))
ZE = 7 * HEADS
Z_Q, Z_K, Z_V, Z_G = range(0, 8, 2)
ZH = 8
ZO = ZH * HEADS


class Steps:

    def __init__(self, sem, names):
        self.sem, self.names, self.K = sem, list(names), len(names)
        self.index = {n: k + 1 for k, n in enumerate(self.names)}
        assert len(self.index) == self.K
        self.next = 0

    def start(self, engine):
        engine.sem_inc(self.sem, 1)

    def one(self, name):
        assert self.names[self.next % self.K] == name, (self.names[self.next % self.K], name)
        self.next += 1
        return 1

    def at(self, name, turn=0):
        return turn * self.K + (1 + self.index[name])

    def before(self, turn):
        return turn * self.K + 1


class Phase:

    def __init__(self, kind, weights, first, tiles, ktu, src, t0):
        self.kind, self.w, self.first, self.n, self.ktu, self.src, self.t0 = kind, weights, first, tiles, ktu, src, t0
        self.u0 = 4 * t0

    def end(self):
        return self.t0 + self.n


def hybrid_step(nc, x_in, vecs, conv_state, w_even_in, w_even_out, w_odd_in, w_odd_out, w_f0_in, w_f0_o0, w_f0_o1,
                w_f0_o2, w_f1_in, w_f1_o0, w_f1_o1, w_f1_o2, cache_k, cache_v, page_table, state_hgrn, state_ret,
                c_ident, c_eye8, c_eye, c_blk, c_causal, c_rope_b, c_perm, c_rope_c, c_decay, c_sdec, c_gamma,
                c_level, c_reset, y_out, kT_out, vT_out, hgrn_p_out, hgrn_s_out, ret_p_out, ret_s_out, conv_out):
    ctx = ExitStack()
    with ctx:
        def sb(name, shape, dt=F32, stack=ctx):
            return stack.enter_context(nc.sbuf_tensor(name, shape, dt))

        def sem(name):
            return ctx.enter_context(nc.semaphore(name))

        raw = sb("raw", [P, SLOTS, UNIT])
        with ExitStack() as part:
            whi = sb("whi", [P, SLOTS, UNIT], F32R, part)
            wlo = sb("wlo", [P, SLOTS, UNIT], F32R, part)
        with ExitStack() as part:
            vring = sb("vring", [P, 4, HEADS * P], F32, part)
            blk = sb("blk", [8, HEADS * P], F32, part)
            om = sb("om", [8, HEADS * P], F32, part)
        ring_space = sb("ring_space", [P, 2 * SLOTS, UNIT])
        x = sb("x", [P, MT, TOK])
        hA = (sb("hA_hi", [P, MT, TOK], F32R), sb("hA_lo", [P, MT, TOK], F32R))
        vec = sb("vec", [P, V_ALL])
        rstd = sb("rstd", [P, TOK])
        acc = sb("acc", [P, TOK])
        sq = sb("sq", [P, TOK])
        var = sb("var", [P, TOK])
        root_tmp = sb("root_tmp", [P, TOK])
        ones = sb("ones", [P, P])
        ident = sb("ident", [P, P])

        with ExitStack() as part:
            def se(name, shape, dt=F32):
                return sb(name, shape, dt, part)
            ze = se("ze", [P, ZE, TOK])
            S = se("S", [P, DEC, PAGES, HEADS])
            cau = se("cau", [P, 384])
            ropeb = se("ropeb", [32, 2, TOK])
            perm = se("perm", [32, 32])
            eye8 = se("eye8", [8, 8])
            eye = se("eye", [P, 8, 8])
            rt = se("rt", [32, 2, TOK])
            pt = se("pt", [1, DEC * PAGES], I32)
            own = se("own", [P, DEC, HEADS])
            po = se("po", [P, DEC, HEADS])
            qk = se("qk", [P, HEADS, DEC])
            mxt = se("mxt", [P, DEC, HEADS])
            mxa = se("mxa", [P, DEC, HEADS])
            mx64 = se("mx64", [64, 1])
            dg = se("dg", [64, 64])
            oS = se("oS", [P, HEADS, DEC])
            oS2 = se("oS2", [P, HEADS, DEC])
            vs = se("vs", [P, HEADS, DEC])
            Pb = se("Pb", [P, PAGES * HEADS])
            Sb = se("Sb", [P, PAGES, HEADS])
            with ExitStack() as sub:
                kring = sb("kring", [P, 4, HEADS * P], F32, sub)
                qbc = sb("qbc", [P, HEADS * P], F32, sub)
                qt8 = sb("qt8", [8, HEADS * P], F32, sub)
                qm8 = sb("qm8", [8, HEADS * P], F32, sub)
            with ExitStack() as sub:
                qh = sb("qh", [P, TOK], F32, sub)
                vh = sb("vh", [P, TOK], F32, sub)
                sm = sb("sm", [P, 384], F32, sub)
                mx2 = sb("mx2", [P, 2], F32, sub)
                nmx = sb("nmx", [P, 2], F32, sub)
                lsum = sb("lsum", [P, 2], F32, sub)
                rl = sb("rl", [P, 2], F32, sub)
                vtok = sb("vtok", [P, 2, P], F32, sub)
                pT = sb("pT", [P, 384], F32, sub)
            with ExitStack() as sub:
                G = sb("G", [P, DEC, BLOCKS, HEADS], F32, sub)
                cmp = sb("cmp", [P, DEC, BLOCKS, HEADS], F32, sub)
                rank = sb("rank", [P, DEC, BLOCKS, HEADS], F32, sub)
            with ExitStack() as sub:
                def sh(name, shape, dt=F32):
                    return sb(name, shape, dt, sub)
                levm = sh("levm", [P, LEVELS + 1, P])
                reset = sh("reset", [P, SEQ])
                t1 = sh("t1", [P, TOK])
                t2 = sh("t2", [P, TOK])
                lsg = sh("lsg", [P, TOK])
                ka = sh("ka", [P, TOK])
                va = sh("va", [P, TOK])
                sg = sh("sg", [P, TOK])
                fg = sh("fg", [P, 8])
                bcum = sh("bcum", [P, SEQ])
                pr = sh("pr", [P, LEVELS + 1, P])
                Aatt = sh("Aatt", [P, 2, P])
                hv = sh("hv", [P, 2, P])
                hk = sh("hk", [P, 2, P])
                ebl = sh("ebl", [P, NCH])
                kv8 = sh("kv8", [8, 2 * P])
                qm = sh("qm", [P, 8, 8])
                so8 = sh("so8", [8, P])
        with ExitStack() as part:
            def sg_(name, shape, dt=F32):
                return sb(name, shape, dt, part)
            EL = sg_("EL", [P, LEVELS, SEQ])
            QE = sg_("QE", [P, LEVELS, P])
            KE = sg_("KE", [P, LEVELS, P])
            qdec = sg_("qdec", [P, SEQ])
            Sst = sg_("Sst", [P, NCH, P])
            S0 = sg_("S0", [P, DEC, P])
            vm8 = sg_("vm8", [8, 8, P])
            oT = sg_("oT", [P, TOK])
        with ExitStack() as part:
            def so(name, shape, dt=F32):
                return sb(name, shape, dt, part)
            zo = so("zo", [P, 2 * ZH, TOK])
            R0 = so("R0", [P, 2, DEC, RK])
            ropec = so("ropec", [P, 2, TOK])
            mixed = (so("mixed_hi", [P, MT, TOK], F32R), so("mixed_lo", [P, MT, TOK], F32R))
            dmat = so("dmat", [P, 384])
            sdec = so("sdec", [P, HEADS, 2])
            gam = so("gam", [P, HEADS])
            reye8 = so("reye8", [8, 8])
            reye = so("reye", [P, 8, 8])
            r1 = so("r1", [P, TOK])
            r2 = so("r2", [P, TOK])
            qr = so("qr", [P, 2, TOK])
            kr = so("kr", [P, 2, TOK])
            gate = so("gate", [P, 2, TOK])
            aT = so("aT", [P, 384])
            rv = so("rv", [P, 2, RK])
            rk_ = so("rk", [P, 2, RK])
            Sf = so("Sf", [P, 2, RK])
            rkv8 = so("rkv8", [8, 2 * RK])
            rvm = so("rvm", [8, 4, RK])
            rqm = so("rqm", [P, 2, 8, 8])
            ro8 = so("ro8", [8, RK])
            roT = so("roT", [P, 2, TOK])
        with ExitStack() as part:
            def sf(name, shape, dt=F32):
                return sb(name, shape, dt, part)
            hB = (sf("hB_hi", [P, MT, TOK], F32R), sf("hB_lo", [P, MT, TOK], F32R))
            hid1 = (sf("hid1_hi", [P, MT, TOK], F32R), sf("hid1_lo", [P, MT, TOK], F32R))
            bt = sf("bt", [P, TOK])
            ug = sf("ug", [P, TOK])
            cst = sf("cst", [P, FT, 2 * DEC])
            cout = sf("cout", [P, FT, PAD + 2 * DEC])
            ab = sf("ab", [P, CONV_COLS])
            cv1 = sf("cv1", [P, CONV_OUT])
            cv2 = sf("cv2", [P, CONV_OUT])
            sil = sf("sil", [P, CONV_OUT])

        st = [ctx.enter_context(nc.psum_tensor(f"stream{n}", [P, 512], F32)) for n in range(2)]
        m = [ctx.enter_context(nc.psum_tensor(f"mix{n}", [P, 512], F32)) for n in range(6)]

        phases = []

        def add(kind, w, first, tiles, ktu, src):
            phases.append(Phase(kind, w, first, tiles, ktu, src, phases[-1].end() if phases else 0))
            return phases[-1]
        E_IN = add("z_even", w_even_in, 0, ZE, 4, hA)
        E_OUT = add("out_norm_hB", w_even_out, 0, MT, 4, hA)

        def ffn(w_in, w_o, last):
            a = [add("ffn_hid1", w_in, 0, 2 * CHUNKS[0], 4, hB),
                 add("ffn_hA", w_in, 2 * CHUNKS[0], 2 * CHUNKS[1], 4, hB),
                 add("out", w_o[0], 0, MT, 4, hid1),
                 add("ffn_hid1", w_in, 2 * (CHUNKS[0] + CHUNKS[1]), 2 * CHUNKS[2], 4, hB),
                 add("out", w_o[1], 0, MT, 4, hA),
                 add(last, w_o[2], 0, MT, 3, hid1)]
            layer = 0 if w_in is w_f0_in else 1
            for p, pair0 in zip((a[0], a[1], a[3]), (0, CHUNKS[0], CHUNKS[0] + CHUNKS[1])):
                p.pair0, p.layer = pair0, layer
            for p, need in zip((a[2], a[4], a[5]), (CHUNKS[0], CHUNKS[0] + CHUNKS[1], FT)):
                p.need = need + FT * layer
            return a
        F0 = ffn(w_f0_in, (w_f0_o0, w_f0_o1, w_f0_o2), "out_norm_hA")
        O_IN = add("z_odd", w_odd_in, 0, ZO, 4, hA)
        O_OUT = add("out_norm_hB", w_odd_out, 0, MT, 4, mixed)
        F1 = ffn(w_f1_in, (w_f1_o0, w_f1_o1, w_f1_o2), "out_final")
        E_OUT.norm, F0[-1].norm, O_OUT.norm, F1[-1].norm = (1, V_FFN0), (2, V_MIX1), (3, V_FFN1), (4, V_FINAL)

        x_landed, vec_landed = [sem(f"x_landed{c}") for c in range(4)], sem("vec_landed")
        first_hi, first_lo, first_squares = sem("first_hi"), sem("first_lo"), sem("first_squares")
        const_landed = sem("const_landed")
        raw_landed = [sem(f"raw_landed{n}") for n in range(SLOTS // 2)]
        hi_done, lo_done, unit_used, tile_free = sem("hi_done"), sem("lo_done"), sem("unit_used"), sem("tile_free")
        consts_set = sem("consts_set")
        acc_cleared, norm_summed = sem("acc_cleared"), sem("norm_summed")
        NV = Steps(sem("norm_vector"), ["lo", "sum"])
        NA = Steps(sem("norm_scalar"), ["square", "hi"])
        IV = Steps(sem("root_vector"), ["var", "n1", "n2", "rstd"])
        IA = Steps(sem("root_scalar"), ["ln", "rough"])
        FV = Steps(sem("ffn_vector"), ["a_prompt", "c1", "c2", "c3", "u_prompt", "u_sample", "hid_lo"])
        FA = Steps(sem("ffn_scalar"), ["history", "new_p", "new_s", "silu", "hid_hi"])
        y_ready, y_stored = sem("y_ready"), sem("y_stored")
        ab_cleared = sem("ab_cleared")
        cst_landed, cout_stored = sem("cst_landed"), sem("cout_stored")
        RP = sem("rope_swapped")
        RV = Steps(sem("rope_vector"), ["cos", "sin", "add"])
        q8_turned, q8_saved, q_picked, q_spread, q_copied = sem("q8_turned"), sem("q8_saved"), sem("q_picked"), sem("q_spread"), sem("q_copied")
        pt_landed = sem("pt_landed")
        k_landed = [sem(f"k_landed{n}") for n in range(4)]
        k_used, s_saved = sem("k_used"), sem("s_saved")
        kv_stored = sem("kv_stored")
        BV = Steps(sem("attn_vector"), ["masked", "max0", "max1", "negmax", "recip", "p0", "p1", "o_lo"])
        BA = Steps(sem("attn_scalar"), ["q", "v", "v_rows", "exp0", "exp1", "pT", "o_hi"])
        BP = Steps(sem("attn_tensor"), ["scores", "v_turned", "p_turned", "o"])
        HV = Steps(sem("hgrn_vector"),
                   ["ls", "mxf", "g1", "sg", "i1", "ir", "va", "cum"] + [f"d{l}{s}" for l in range(LEVELS) for s in "lr"]
                   + ["qe0", "ke0", "pr0a", "pr0b", "att0", "qe1", "ke1", "pr1a", "pr1b", "att1", "dk", "kd", "qdec",
                      "s1", "s2", "s3", "s4", "vm", "qm"] + [f"sn{b}" for b in range(DEC)] + ["var", "n1", "n2", "rstd", "og", "gated", "o_lo"])
        HA = Steps(sem("hgrn_scalar"),
                   ["abs", "exp", "ln", "ka", "fg", "eg", "ei", "levels", "v_rows", "dke", "k_rows", "ebl", "eb", "kv8", "so8",
                    "o_p", "o_s", "square", "lnv", "rough", "o_hi"])
        HP = Steps(sem("hgrn_tensor"),
                   ["lev0", "lev1", "v_turned", "k_turned", "U", "o", "t8", "kv_a", "kv_b", "so", "so_turned", "ssum"])
        h_s0_landed, h_stored = sem("h_s0_landed"), sem("h_stored")
        SVn = (["qk", "vs", "clear_cmp", "rank0"] + [f"{w}{i}" for i in range(BLOCKS) for w in (("gt", "ge", "add") if 0 < i < BLOCKS - 1 else (("ge", "add") if i == 0 else ("gt", "add")))]
               + ["keep", "minus", "bias", "tmax", "rmax", "diag", "mxa", "shift", "oshift", "tsum", "den", "rden", "p", "po"])
        SV = Steps(sem("sel_vector"), SVn)
        SA = Steps(sem("sel_scalar"), ["own", "G", "exp", "oexp"])
        SP_ = Steps(sem("sel_tensor"), ["own", "gates", "mxT", "mxb", "den"])
        v_landed = [sem(f"v_landed{n}") for n in range(4)]
        v_used, v_saved = sem("v_used"), sem("v_saved")
        pb_ready, om_ready, o8_ready = sem("pb_ready"), sem("om_ready"), sem("o8_ready")
        TV = Steps(sem("tail_vector"), ["pv", "sum", "lo"])
        TA = Steps(sem("tail_scalar"), ["hi"])
        QV = Steps(sem("ret_vector"),
                   [f"{w}{s}" for w in "qk" for s in ("a", "b", "x1", "c", "d", "x2")]
                   + ["att", "k0", "k1", "qm", "vm0", "s0_0", "s1_0", "s0_1", "s1_1", "vm1", "s0_2", "s1_2", "s0_3", "s1_3",
                      "mean", "oc", "var", "n1", "n2", "rstd", "og", "gated", "o_lo"])
        QA = Steps(sem("ret_scalar"), ["silu", "v_rows", "kv8", "o_p", "sfin", "ro8", "o_s", "square", "lnv", "rough", "o_hi"])
        QP = Steps(sem("ret_tensor"), ["v_turned", "att", "k_turned", "t8", "o", "sfin", "kv00", "kv01", "kv10", "kv11",
                                       "kv20", "kv21", "kv30", "kv31", "so", "so_turned", "ssum", "vsum"])
        r_s0_landed, r_s0_stored, r_sf_stored, dm_landed = sem("r_s0_landed"), sem("r_s0_stored"), sem("r_sf_stored"), sem("dm_landed")
        XV, NFA = Steps(sem("final_sum"), ["sum"]), sem("final_square")
        consts = [(ident[:, :], c_ident), (eye8[:, :], c_eye8), (eye[:, :, :], c_eye), (cau[:, :], c_causal),
                  (ropeb[:, :, :], c_rope_b), (perm[:, :], c_perm)]
        N_CONST = len(consts)
        oc_landed = sem("odd_const_landed")
        hc_landed = sem("hgrn_const_landed")

        def tile(buf, t, a=0, b=TOK):
            return buf[:, bass.ds(t, 1), a:b].rearrange("p o n -> p (o n)")

        def col(t):
            return vec[:, bass.ds(t, 1)]

        ab_s = ab[:, PAD + SEQ:CONV_COLS].rearrange("p (b c) -> p b c", c=3)
        block = ctx.enter_context(nc.Block())

        @block.sync
        def _(sp):
            sp.sem_inc(h_stored, 1)
            sp.dma_start(vec[:, :], vecs).then_inc(vec_landed, 16)
            for c in range(4):
                sp.dma_start(x[:, 4 * c:4 * c + 4, :], x_in[:, 4 * c:4 * c + 4, :]).then_inc(x_landed[c], 16)

            def hgrn_states():
                sp.wait_ge(BV.sem, BV.before(HEADS))
                sp.wait_ge(BP.sem, BP.before(HEADS))
                sp.wait_ge(BA.sem, BA.before(HEADS))
                sp.wait_ge(kv_stored, 32)
                sp.wait_ge(SV.sem, SV.at("vs"))
                with sp.Fori(0, HEADS) as h:
                    load = state_hgrn[:, bass.ds(h, 1), :, :].rearrange("b o d e -> d (b o) e")
                    sp.wait_ge(h_stored, 32 * h + 1)
                    sp.dma_start(S0[:, :, :], load).then_inc(h_s0_landed, 16)
                    sp.wait_ge(HV.sem, HV.at("s4", h))
                    sp.dma_start(hgrn_p_out[bass.ds(h, 1), :, :].rearrange("o d e -> d (o e)"), Sst[:, NCH - 1, :]).then_inc(h_stored, 16)
                    sp.wait_ge(HP.sem, HP.at("so", h))
                    sp.dma_start(hgrn_s_out[:, bass.ds(h, 1), :, :].rearrange("b o d e -> d (b o) e"), S0[:, :, :]).then_inc(h_stored, 16)

            def load_pair(p, i):
                for half in range(4):
                    n = p.ktu * P
                    row = i * 2 + (p.first + half // 2)
                    if not (isinstance(i, int) and p is phases[0] and i == 0):
                        row = row if isinstance(i, int) else sp.snap(row)
                        sp.wait_ge(lo_done, i * 8 + (p.u0 + 2 * half + 2 - SLOTS))
                    src = p.w[bass.ds(row, 1), half % 2, :, :].rearrange("o p (s n) -> p (o s) n", s=2)
                    sp.dma_start(raw[:, 2 * half:2 * half + 2, 0:n], src).then_inc(raw_landed[half], 16)

            for p in phases:
                peeled = p is E_IN or p is E_OUT
                if peeled:
                    load_pair(p, 0)
                if p is E_OUT:
                    hgrn_states()
                with sp.Fori(1 if peeled else 0, p.n // 2) as i:
                    load_pair(p, i)
            sp.wait_ge(y_ready, MT)
            sp.dma_start(y_out, x[:, :, :]).then_inc(y_stored, 16)
            sp.wait_ge(y_stored, 16)

        @block.tensor
        def _(pe):
            mm, tr = nc.tensor.matmul, nc.tensor.transpose
            for steps in (BP, HP, SP_, QP):
                steps.start(pe)

            def stream_tile(p, i, j, last_k=None):
                bank = st[j][:, 0:TOK]
                if not (isinstance(i, int) and p.t0 + 2 * i + j < 2):
                    pe.wait_ge(tile_free, 2 * i + (p.t0 + j - 1))
                for k in range(4):
                    pe.wait_ge(lo_done, 8 * i + (p.u0 + 4 * j + k + 1))
                    for q in range(p.ktu):
                        kt, c = k * p.ktu + q, slice(q * P, (q + 1) * P)
                        hi, lo = whi[:, 4 * j + k, c], wlo[:, 4 * j + k, c]
                        first, last = kt == 0, kt == 4 * p.ktu - 1
                        if p is E_IN and isinstance(i, int) and i == 0 and j == 0:
                            pe.wait_ge(first_lo, kt + 1)
                        if last_k is not None and last:
                            pe.wait_ge(NV.sem, NV.at("lo", MT * last_k - 1))
                        mm(bank, hi, p.src[0][:, kt, :], start=first, stop=False)
                        mm(bank, hi, p.src[1][:, kt, :], start=False, stop=False)
                        ins = mm(bank, lo, p.src[0][:, kt, :], start=False, stop=last)
                    ins.then_inc(unit_used, 1)

            def stream(p, a, b):
                with pe.Fori(a, b) as i:
                    for j in range(2):
                        stream_tile(p, i, j)

            def norm_sum(n):
                if n < 4:
                    pe.wait_ge(NV.sem, NV.before(MT * n))
                    pe.wait_ge(NA.sem, NA.before(MT * n))
                else:
                    pe.wait_ge(XV.sem, XV.before(MT))
                mm(m[5][:, 0:TOK], ones[:, :], acc[:, :], start=True, stop=True).then_inc(norm_summed, 1)

            def stream_under_norm(p, n):
                pe.wait_ge(NV.sem, NV.before(MT * n - 1))
                pe.wait_ge(NA.sem, NA.before(MT * n - 1))
                stream_tile(p, 0, 0, last_k=n)
                norm_sum(n)
                stream_tile(p, 0, 1)
                stream(p, 1, p.n // 2)

            def rope(first, turn0):
                for half in range(2):
                    for t in range(4):
                        n = turn0 + 4 * half + t
                        if half:
                            pe.wait_ge(RV.sem, RV.at("sin", n - 4))
                        mm(m[t][0:32, 0:TOK], perm[:, :], ze[0:32, first + 4 * half + t, :], start=True, stop=True).then_inc(RP, 1)

            def attention_head(h):
                pe.wait_ge(BV.sem, BV.before(h))
                pe.wait_ge(BA.sem, BA.at("v", h))
                mm(m[0][:, 0:P], qh[:, 0:P], tile(ze, h + Z_KB, 0, P), start=True, stop=False, skip_group_check=True)
                mm(m[0][:, P:384], qh[:, P:SEQ], tile(ze, h + Z_KB, 0, SEQ), start=False, stop=True,
                   skip_group_check=True).then_inc(BP.sem, BP.one("scores"))
                tr(m[1][:, 0:P], vh[:, 0:P], ident[:, :])
                tr(m[1][:, P:SEQ], vh[:, P:SEQ], ident[:, :]).then_inc(BP.sem, BP.one("v_turned"))
                pe.wait_ge(BV.sem, BV.at("p1", h))
                for k in range(3):
                    ins = tr(m[2][:, k * P:(k + 1) * P], sm[:, k * P:(k + 1) * P], ident[:, :])
                ins.then_inc(BP.sem, BP.one("p_turned"))
                pe.wait_ge(BA.sem, BA.at("pT", h))
                mm(m[3][:, 0:SEQ], vtok[:, 0, :], pT[:, 0:SEQ], start=True, stop=False, skip_group_check=True)
                mm(m[3][:, P:SEQ], vtok[:, 1, :], pT[:, SEQ:384], start=False, stop=True,
                   skip_group_check=True).then_inc(BP.sem, BP.one("o"))

            def value_pages(b, first, last):
                if first == 0:
                    pe.wait_ge(pb_ready, b + 1)
                for g in range(first, last):
                    pe.wait_ge(v_landed[g % 4], 64 * b + 16 * (g // 4 + 1))
                    for k in range(2):
                        ins = mm(st[k][0:8, :], Pb[:, g * HEADS:(g + 1) * HEADS], vring[:, g % 4, k * 512:(k + 1) * 512],
                                 start=(g == 0), stop=(g == PAGES - 1))
                    ins.then_inc(v_used, 1)

            def value_columns(b):
                pe.wait_ge(om_ready, 2 * b + 2)
                for h in range(HEADS):
                    ins = mm(st[0][:, h:h + 1], om[:, h * P:(h + 1) * P], ones[0:8, 0:1], start=(h == 0), stop=(h == HEADS - 1),
                             skip_group_check=True)
                ins.then_inc(o8_ready, 1)

            def hgrn_head(h):
                value_pages(h, 0, 10)
                pe.wait_ge(HV.sem, HV.before(h))
                for c in range(2):
                    pe.wait_ge(HV.sem, HV.at(f"ke{c}", h))
                    if c:
                        pe.wait_ge(HV.sem, HV.at("pr0b", h))
                    for l in range(LEVELS + 1):
                        k_, q_ = (KE[:, l, :], QE[:, l, :]) if l < LEVELS else (ka[:, c * P:(c + 1) * P], tile(ze, h + Z_QA, c * P, (c + 1) * P))
                        b_ = l // 4
                        ins = mm(m[b_][:, (l % 4) * P:(l % 4 + 1) * P], k_, q_, start=(l % 4 == 0),
                                 stop=(l in (3, LEVELS)), skip_group_check=True)
                    ins.then_inc(HP.sem, HP.one(f"lev{c}"))
                    if c == 0:
                        value_pages(h, 10, 12)
                for c in range(2):
                    ins = tr(m[2][:, c * P:(c + 1) * P], va[:, c * P:(c + 1) * P], ident[:, :])
                ins.then_inc(HP.sem, HP.one("v_turned"))
                value_pages(h, 12, 13)
                pe.wait_ge(HV.sem, HV.at("kd", h))
                for c in range(2):
                    ins = tr(m[3][:, c * P:(c + 1) * P], t2[:, c * P:(c + 1) * P], ident[:, :])
                ins.then_inc(HP.sem, HP.one("k_turned"))
                pe.wait_ge(HA.sem, HA.at("k_rows", h))
                for c in range(NCH):
                    r = slice((c % 2) * CHUNK, (c % 2 + 1) * CHUNK)
                    ins = mm(m[4 - c % 2][:, (c // 2) * P:(c // 2 + 1) * P], hk[r, c // 2, :], hv[r, c // 2, :], start=(c < 2),
                             stop=(c >= NCH - 2), skip_group_check=True)
                ins.then_inc(HP.sem, HP.one("U"))
                value_pages(h, 13, 14)
                pe.wait_ge(HV.sem, HV.at("s4", h))
                for c in range(2):
                    mm(m[5][:, c * P:(c + 1) * P], hv[:, c, :], Aatt[:, c, :], start=(c == 0), stop=False, skip_group_check=True)
                for c in range(1, NCH):
                    ins = mm(m[5][:, c * CHUNK:(c + 1) * CHUNK], Sst[:, c - 1, :], qdec[:, c * CHUNK:(c + 1) * CHUNK],
                             start=False, stop=(c == NCH - 1), skip_group_check=True)
                ins.then_inc(HP.sem, HP.one("o"))
                tr(m[0][0:8, 0:P], ka[:, SEQ:TOK], ident[:, :])
                tr(m[0][0:8, P:2 * P], va[:, SEQ:TOK], ident[:, :]).then_inc(HP.sem, HP.one("t8"))
                pe.wait_ge(HV.sem, HV.at("qm", h))
                for k, w in enumerate("ab"):
                    mm(m[1 + k][:, :], kv8[:, 0:P], vm8[:, 4 * k:4 * k + 4, :], start=True, stop=True)\
                        .then_inc(HP.sem, HP.one(f"kv_{w}"))
                value_pages(h, 14, 16)
                pe.wait_ge(HV.sem, HV.at(f"sn{DEC - 1}", h))
                for b in range(DEC):
                    ins = mm(m[3][0:8, 0:P], qm[:, b, :], S0[:, b, :], start=(b == 0), stop=(b == DEC - 1))
                ins.then_inc(HP.sem, HP.one("so"))
                pe.wait_ge(HA.sem, HA.at("so8", h))
                mm(m[4][:, 0:8], so8[:, :], ident[0:8, 0:8], start=True, stop=True).then_inc(HP.sem, HP.one("so_turned"))
                value_columns(h)
                pe.wait_ge(HA.sem, HA.at("square", h))
                mm(m[0][:, 0:TOK], ones[:, :], t1[:, :], start=True, stop=True).then_inc(HP.sem, HP.one("ssum"))
                pe.wait_ge(v_saved, h + 1)

            def retention_stage(h, par, stage):
                z = ZH * par
                if stage == 0:
                    pe.wait_ge(QV.sem, QV.before(h))
                    pe.wait_ge(tile_free, ZH * h + (O_IN.t0 + ZH))
                    for s in range(2):
                        for e in range(2):
                            ins = tr(m[1][:, s * RK + e * P:s * RK + (e + 1) * P], zo[:, z + Z_V + e, s * P:(s + 1) * P], ident[:, :])
                    ins.then_inc(QP.sem, QP.one("v_turned"))
                elif stage == 1:
                    pe.wait_ge(QV.sem, QV.at("kx2", h))
                    for d in range(2):
                        mm(m[0][:, 0:SEQ], kr[:, d, 0:P], qr[:, d, 0:SEQ], start=(d == 0), stop=False, skip_group_check=True)
                    for d in range(2):
                        ins = mm(m[0][:, SEQ:384], kr[:, d, P:SEQ], qr[:, d, P:SEQ], start=False, stop=(d == 1), skip_group_check=True)
                    ins.then_inc(QP.sem, QP.one("att"))
                    for s in range(2):
                        for e in range(2):
                            ins = tr(m[2][:, s * RK + e * P:s * RK + (e + 1) * P], kr[:, e, s * P:(s + 1) * P], ident[:, :])
                    ins.then_inc(QP.sem, QP.one("k_turned"))
                    for d in range(2):
                        tr(m[5][0:8, d * P:(d + 1) * P], kr[:, d, SEQ:TOK], ident[:, :])
                    for d in range(2):
                        ins = tr(m[5][0:8, RK + d * P:RK + (d + 1) * P], zo[:, z + Z_V + d, SEQ:TOK], ident[:, :])
                    ins.then_inc(QP.sem, QP.one("t8"))
                elif stage == 2:
                    pe.wait_ge(QV.sem, QV.at("att", h))
                    pe.wait_ge(QA.sem, QA.at("v_rows", h))
                    for e in range(2):
                        mm(m[3][:, e * SEQ:(e + 1) * SEQ], rv[:, 0, e * P:(e + 1) * P], aT[:, 0:SEQ], start=(e == 0),
                           stop=False, skip_group_check=True)
                        ins = mm(m[3][:, e * SEQ + P:(e + 1) * SEQ], rv[:, 1, e * P:(e + 1) * P], aT[:, SEQ:384], start=False,
                                 stop=(e == 1), skip_group_check=True)
                    ins.then_inc(QP.sem, QP.one("o"))
                    pe.wait_ge(QV.sem, QV.at("k1", h))
                    for d in range(2):
                        for s in range(2):
                            ins = mm(m[4][:, d * RK:(d + 1) * RK], rk_[:, s, d * P:(d + 1) * P], rv[:, s, :],
                                     start=(d == 0 and s == 0), stop=(d == 1 and s == 1), skip_group_check=True)
                    ins.then_inc(QP.sem, QP.one("sfin"))
                    pe.wait_ge(QV.sem, QV.at("vm0", h))
                    sample_updates(0, (1, 2, 5, 0))
                elif stage == 3:
                    pe.wait_ge(QV.sem, QV.at("vm1", h))
                    pe.wait_ge(QA.sem, QA.at("sfin", h))
                    sample_out(0)
                    sample_updates(2, (1, 2, 5, 4))
                elif stage == 4:
                    pe.wait_ge(QV.sem, QV.at("s1_3", h))
                    sample_out(1).then_inc(QP.sem, QP.one("so"))
                elif stage == 5:
                    pe.wait_ge(QA.sem, QA.at("ro8", h))
                    for e in range(2):
                        ins = mm(m[0][:, e * 8:(e + 1) * 8], ro8[:, e * P:(e + 1) * P], ident[0:8, 0:8], start=(e == 0), stop=(e == 1),
                                 skip_group_check=True)
                    ins.then_inc(QP.sem, QP.one("so_turned"))
                    pe.wait_ge(QA.sem, QA.at("o_s", h))
                    for e in range(2):
                        ins = mm(m[1][:, 0:TOK], ones[:, :], roT[:, e, :], start=(e == 0), stop=(e == 1))
                    ins.then_inc(QP.sem, QP.one("ssum"))
                elif stage == 6:
                    pe.wait_ge(QA.sem, QA.at("square", h))
                    for e in range(2):
                        ins = mm(m[2][:, 0:TOK], ones[:, :], kr[:, e, :], start=(e == 0), stop=(e == 1))
                    ins.then_inc(QP.sem, QP.one("vsum"))

            def sample_updates(q0, banks):
                for q in range(2):
                    for d in range(2):
                        mm(m[banks[2 * q + d]][:, :], rkv8[:, d * P:(d + 1) * P], rvm[:, 2 * q:2 * q + 2, :], start=True, stop=True)\
                            .then_inc(QP.sem, QP.one(f"kv{q0 + q}{d}"))

            def sample_out(half):
                for b in range(4 * half, 4 * half + 4):
                    for d in range(2):
                        ins = mm(m[3][0:8, 0:RK], rqm[:, d, b, :], R0[:, d, b, :], start=(b == 0 and d == 0),
                                 stop=(b == DEC - 1 and d == 1))
                return ins

            pe.wait_ge(consts_set, 1)
            pe.wait_ge(const_landed, 16 * N_CONST)
            for j in range(2):
                stream_tile(E_IN, 0, j)
                if j == 0:
                    pe.wait_ge(first_squares, 4)
                    for t in range(MT):
                        ins = mm(m[5][:, 0:TOK], ones[:, :], ze[:, t, :], start=(t == 0), stop=(t == MT - 1))
                    ins.then_inc(norm_summed, 1)
            stream(E_IN, 1, 4)
            pe.wait_ge(tile_free, HEADS)
            rope(Z_QB, 0)
            pe.wait_ge(RV.sem, RV.before(HEADS))
            for h in range(HEADS):
                ins = tr(m[4 + h // 4][0:8, (h % 4) * P:(h % 4 + 1) * P], ze[:, Z_QB + h, SEQ:TOK], ident[:, :])
            ins.then_inc(q8_turned, 1)

            def spread_query():
                for k in range(2):
                    ins = mm(m[4 + k][:, :], ones[0:8, :], qm8[:, k * 512:(k + 1) * 512], start=True, stop=True)
                ins.then_inc(q_spread, 1)
            pe.wait_ge(q_picked, 1)
            spread_query()
            for j in range(2):
                stream_tile(E_IN, 4, j)
            with pe.Fori(0, 7) as b:
                for c in range(3):
                    for j in range(2):
                        stream_tile(E_IN, b * 3 + (5 + c), j)
                    if c == 1:
                        pe.wait_ge(q_picked, b + 2)
                        pe.wait_ge(q_copied, b + 1)
                        spread_query()
            stream(E_IN, 26, 28)
            pe.wait_ge(tile_free, ZE)
            pe.wait_ge(q_copied, DEC)
            rope(Z_KB, HEADS)
            pe.wait_ge(RV.sem, RV.before(2 * HEADS))
            with pe.Fori(0, HEADS) as h:
                attention_head(h)
            pe.wait_ge(BV.sem, BV.before(HEADS))
            pe.wait_ge(BA.sem, BA.before(HEADS))
            pe.wait_ge(s_saved, DEC)
            pe.wait_ge(SV.sem, SV.at("qk"))
            mm(m[0][:, 0:64], ones[:, :], qk[:, :, :], start=True, stop=True).then_inc(SP_.sem, SP_.one("own"))
            Sv = S[:, :, :, :].rearrange("p b (j two) h -> p b j two h", two=2)
            for k in range(2):
                ins = mm(m[1][:, :], ones[:, :], Sv[:, :, :, k, :], start=(k == 0), stop=(k == 1))
            ins.then_inc(SP_.sem, SP_.one("gates"))
            pe.wait_ge(SV.sem, SV.at("tmax"))
            tr(m[2][0:64, 0:P], mxt[:, :, :].rearrange("p b h -> p (b h)"), ident[:, :]).then_inc(SP_.sem, SP_.one("mxT"))
            pe.wait_ge(SV.sem, SV.at("diag"))
            mm(m[3][:, 0:64], ones[0:64, :], dg[:, :], start=True, stop=True).then_inc(SP_.sem, SP_.one("mxb"))
            pe.wait_ge(SV.sem, SV.at("tsum"))
            mm(m[4][:, 0:64], ones[:, :], mxt[:, :, :], start=True, stop=True).then_inc(SP_.sem, SP_.one("den"))
            pe.wait_ge(SV.sem, SV.before(1))
            with pe.Fori(0, HEADS) as h:
                hgrn_head(h)
            pe.wait_ge(HV.sem, HV.before(HEADS))
            pe.wait_ge(HA.sem, HA.before(HEADS))
            pe.wait_ge(TV.sem, TV.before(1))
            pe.wait_ge(TA.sem, TA.before(1))
            stream(E_OUT, 0, MT // 2)
            for p in F0:
                if p.src is not hB:
                    pe.wait_ge(FV.sem, FV.before(p.need))
                if p is F0[0]:
                    stream_under_norm(p, 1)
                else:
                    stream(p, 0, p.n // 2)
            def project(h, s):
                stream_tile(O_IN, h * (ZH // 2) + s // 2, s % 2)
            pe.wait_ge(NV.sem, NV.before(MT * 2 - 1))
            pe.wait_ge(NA.sem, NA.before(MT * 2 - 1))
            stream_tile(O_IN, 0, 0, last_k=2)
            norm_sum(2)
            for s in range(1, ZH):
                project(0, s)
            with pe.Fori(0, HEADS // 2 - 1) as i:
                for j in range(2):
                    for s in range(ZH):
                        project(i * 2 + (j + 1), s)
                        retention_stage(i * 2 + j, j, s)
            for s in range(ZH):
                project(HEADS - 1, s)
                retention_stage(HEADS - 2, 0, s)
            for s in range(ZH):
                retention_stage(HEADS - 1, 1, s)
            pe.wait_ge(QV.sem, QV.before(HEADS))
            pe.wait_ge(QA.sem, QA.before(HEADS))
            stream(O_OUT, 0, MT // 2)
            for p in F1:
                if p.src is not hB:
                    pe.wait_ge(FV.sem, FV.before(p.need))
                if p is F1[0]:
                    stream_under_norm(p, 3)
                else:
                    stream(p, 0, p.n // 2)
            norm_sum(4)

        @block.scalar
        def _(act):
            A = nc.scalar.activation
            for steps in (NA, FA, BA, HA, SA, TA, QA, IA):
                steps.start(act)
            for dst, src in consts:
                act.dma_start(dst, src).then_inc(const_landed, 16)

            def hi_tile(p, i, j):
                for k in range(4):
                    if k % 2 == 0:
                        act.wait_ge(raw_landed[2 * j + k // 2], 16 * i + 16 * (p.u0 // 8 + 1))
                    if not (isinstance(i, int) and p.u0 + 8 * i == 0):
                        act.wait_ge(unit_used, 8 * i + (p.u0 + 4 * j + k + 1 - SLOTS))
                    n = p.ktu * P
                    A(whi[:, 4 * j + k, 0:n], raw[:, 4 * j + k, 0:n], ACT.Copy).then_inc(hi_done, 1)

            def norm_tile(n, t, g, dst):
                act.wait_ge(NV.sem, t * 2 + NV.before(MT * (n - 1)))
                A(sq[:, :], tile(x, t), ACT.Square).then_inc(NA.sem, NA.one("square"))
                A(tile(dst[0], t), tile(x, t), ACT.Copy, scale=col(t + g)).then_inc(NA.sem, NA.one("hi"))

            def rough_root(n):
                act.wait_ge(IV.sem, IV.at("var", n))
                A(sq[:, :], var[:, :], ACT.Ln).then_inc(IA.sem, IA.one("ln"))
                act.wait_ge(IA.sem, IA.at("ln", n))
                A(rstd[:, :], sq[:, :], ACT.Exp, scale=-0.5).then_inc(IA.sem, IA.one("rough"))

            def evac(p, i, j):
                t = 2 * i + j
                if p.kind.startswith("out_"):
                    n, g = p.norm
                    act.wait_ge(tile_free, t + (p.t0 + 1))
                    if p.kind == "out_final":
                        act.wait_ge(XV.sem, XV.before(t))
                        A(sq[:, :], tile(x, t), ACT.Square).then_inc(NFA, 1)
                    else:
                        norm_tile(n, t, g, hB if p.kind == "out_norm_hB" else hA)
                elif p.kind.startswith("ffn") and j == 0:
                    pair = i + p.pair0
                    act.wait_ge(FV.sem, FV.before(pair + FT * p.layer))
                    A(ab_s[:, :, 0:2], tile(cst, pair, 0, 2 * DEC).rearrange("p (b c) -> p b c", c=2), ACT.Copy)\
                        .then_inc(FA.sem, FA.one("history"))
                elif p.kind.startswith("ffn"):
                    pair = i + p.pair0
                    turn = pair + FT * p.layer
                    act.wait_ge(tile_free, 2 * i + (p.t0 + 1))
                    act.wait_ge(FA.sem, FA.at("history", turn))
                    A(tile(cout, pair, 0, PAD), ab[:, SEQ:SEQ + PAD], ACT.Copy).then_inc(FA.sem, FA.one("new_p"))
                    A(tile(cout, pair, PAD, PAD + 2 * DEC).rearrange("p (b c) -> p b c", c=2), ab_s[:, :, 1:3], ACT.Copy)\
                        .then_inc(FA.sem, FA.one("new_s"))
                    act.wait_ge(FV.sem, FV.at("c3", turn))
                    A(sil[:, :], cv1[:, :], ACT.Silu).then_inc(FA.sem, FA.one("silu"))
                    act.wait_ge(FV.sem, FV.at("u_sample", turn))
                    A(tile(hid1[0] if p.kind == "ffn_hid1" else hA[0], i), ug[:, :], ACT.Copy).then_inc(FA.sem, FA.one("hid_hi"))

            def body(p):
                with act.Fori(0, p.n // 2 - 1) as i:
                    for j in range(2):
                        hi_tile(p, i + 1, j)
                        evac(p, i, j)

            def turn_over(p, nxt):
                for j in range(2):
                    if nxt is not None:
                        hi_tile(nxt, 0, j)
                    evac(p, p.n // 2 - 1, j)

            def attention_head(h):
                act.wait_ge(BP.sem, BP.before(h))
                A(qh[:, :], tile(ze, h + Z_QB), ACT.Copy).then_inc(BA.sem, BA.one("q"))
                A(vh[:, :], tile(ze, h + Z_VB), ACT.Copy).then_inc(BA.sem, BA.one("v"))
                act.wait_ge(BP.sem, BP.at("v_turned", h))
                A(vtok[:, :, :], m[1][:, 0:SEQ].rearrange("p (s e) -> p s e", s=2), ACT.Copy).then_inc(BA.sem, BA.one("v_rows"))
                act.wait_ge(BV.sem, BV.at("negmax", h))
                for k, (a, b) in enumerate(((0, P), (P, 384))):
                    A(sm[:, a:b], sm[:, a:b], ACT.Exp, bias=nmx[:, k:k + 1], scale=P ** -0.5, accum_out=lsum[:, k:k + 1])\
                        .then_inc(BA.sem, BA.one(f"exp{k}"))
                act.wait_ge(BP.sem, BP.at("p_turned", h))
                A(pT[:, :], m[2][:, 0:384], ACT.Copy).then_inc(BA.sem, BA.one("pT"))
                act.wait_ge(BP.sem, BP.at("o", h))
                A(tile(hA[0], h + HEADS, 0, SEQ), m[3][:, 0:SEQ], ACT.Copy).then_inc(BA.sem, BA.one("o_hi"))

            def hgrn_head(h):
                act.wait_ge(HP.sem, HP.before(h))
                A(Pb[:, :], S[:, bass.ds(h, 1), :, :].rearrange("p o g h -> p (o g h)"), ACT.Copy).then_inc(pb_ready, 1)
                act.wait_ge(HV.sem, HV.before(h))
                f = tile(ze, h + Z_FA)
                A(t1[:, :], f, ACT.Abs).then_inc(HA.sem, HA.one("abs"))
                act.wait_ge(HA.sem, HA.at("abs", h))
                A(t2[:, :], t1[:, :], ACT.Exp, scale=-1.0).then_inc(HA.sem, HA.one("exp"))
                act.wait_ge(HA.sem, HA.at("exp", h))
                A(t1[:, :], t2[:, :], ACT.Ln, bias=1.0).then_inc(HA.sem, HA.one("ln"))
                act.wait_ge(HV.sem, HV.at("mxf", h))
                A(ka[:, :], t2[:, :], ACT.Exp, scale=-1.0).then_inc(HA.sem, HA.one("ka"))
                A(fg[:, :], lsg[:, SEQ:TOK], ACT.Exp).then_inc(HA.sem, HA.one("fg"))
                A(sg[:, :], tile(ze, h + Z_GA), ACT.Exp, scale=-1.0).then_inc(HA.sem, HA.one("eg"))
                A(va[:, :], tile(ze, h + Z_IA), ACT.Exp, scale=-1.0).then_inc(HA.sem, HA.one("ei"))
                act.wait_ge(HV.sem, HV.at(f"d{LEVELS - 1}r", h))
                A(EL[:, :, :], EL[:, :, :], ACT.Exp).then_inc(HA.sem, HA.one("levels"))
                act.wait_ge(HP.sem, HP.at("v_turned", h))
                A(hv[:, :, :], m[2][:, 0:SEQ].rearrange("p (s e) -> p s e", s=2), ACT.Copy).then_inc(HA.sem, HA.one("v_rows"))
                act.wait_ge(HV.sem, HV.at("dk", h))
                A(t2[:, 0:SEQ], t2[:, 0:SEQ], ACT.Exp).then_inc(HA.sem, HA.one("dke"))
                act.wait_ge(HP.sem, HP.at("k_turned", h))
                A(hk[:, :, :], m[3][:, 0:SEQ].rearrange("p (s e) -> p s e", s=2), ACT.Copy).then_inc(HA.sem, HA.one("k_rows"))
                bl = bcum[:, :].rearrange("p (c n) -> p c n", n=CHUNK)[:, :, CHUNK - 1]
                A(ebl[:, :], bl, ACT.Exp).then_inc(HA.sem, HA.one("ebl"))
                A(t1[:, 0:SEQ], bcum[:, :], ACT.Exp).then_inc(HA.sem, HA.one("eb"))
                act.wait_ge(HP.sem, HP.at("t8", h))
                A(kv8[:, :], m[0][0:8, 0:2 * P], ACT.Copy).then_inc(HA.sem, HA.one("kv8"))
                act.wait_ge(HP.sem, HP.at("so", h))
                A(so8[:, :], m[3][0:8, 0:P], ACT.Copy).then_inc(HA.sem, HA.one("so8"))
                A(oT[:, 0:SEQ], m[5][:, 0:SEQ], ACT.Copy).then_inc(HA.sem, HA.one("o_p"))
                act.wait_ge(HP.sem, HP.at("so_turned", h))
                A(oT[:, SEQ:TOK], m[4][:, 0:8], ACT.Copy).then_inc(HA.sem, HA.one("o_s"))
                act.wait_ge(HA.sem, HA.at("o_s", h))
                A(t1[:, :], oT[:, :], ACT.Square).then_inc(HA.sem, HA.one("square"))
                act.wait_ge(o8_ready, h + 1)
                A(oS[:, :, bass.ds(h, 1)].rearrange("p h o -> p (h o)"), st[0][:, 0:HEADS], ACT.Copy).then_inc(v_saved, 1)
                act.wait_ge(HV.sem, HV.at("var", h))
                A(t2[:, :], lsg[:, :], ACT.Ln).then_inc(HA.sem, HA.one("lnv"))
                act.wait_ge(HA.sem, HA.at("lnv", h))
                A(t1[:, :], t2[:, :], ACT.Exp, scale=-0.5).then_inc(HA.sem, HA.one("rough"))
                act.wait_ge(HV.sem, HV.at("gated", h))
                A(tile(hA[0], h), t2[:, :], ACT.Copy).then_inc(HA.sem, HA.one("o_hi"))

            def load_states(h):
                for d in range(2):
                    act.dma_start(R0[:, d, :, :], state_ret[:, bass.ds(h, 1), d * P:(d + 1) * P, :].rearrange("b o p e -> p (b o) e"))\
                        .then_inc(r_s0_landed, 16)

            def load_decay(h):
                act.dma_start(dmat[:, :], c_decay[bass.ds(h, 1), :, :].rearrange("o p n -> p (o n)")).then_inc(dm_landed, 16)

            def retention_stage(h, par, stage, more=True):
                z = ZH * par
                if stage == 0:
                    act.wait_ge(QV.sem, QV.before(h))
                    act.wait_ge(QP.sem, QP.before(h))
                    act.wait_ge(tile_free, ZH * h + (O_IN.t0 + ZH))
                    A(gate[:, :, :], zo[:, z + Z_G:z + Z_G + 2, :], ACT.Silu).then_inc(QA.sem, QA.one("silu"))
                    act.wait_ge(QP.sem, QP.at("v_turned", h))
                    A(rv[:, :, :], m[1][:, :].rearrange("p (s e) -> p s e", s=2), ACT.Copy).then_inc(QA.sem, QA.one("v_rows"))
                elif stage == 1:
                    act.wait_ge(QP.sem, QP.at("t8", h))
                    A(rkv8[:, :], m[5][0:8, :], ACT.Copy).then_inc(QA.sem, QA.one("kv8"))
                elif stage == 2:
                    if more:
                        act.wait_ge(QV.sem, QV.at("att", h))
                        load_decay(h + 1)
                    act.wait_ge(QP.sem, QP.at("o", h))
                    A(roT[:, :, 0:SEQ], m[3][:, :].rearrange("p (e t) -> p e t", e=2), ACT.Copy).then_inc(QA.sem, QA.one("o_p"))
                    act.wait_ge(QP.sem, QP.at("sfin", h))
                    A(Sf[:, :, :], m[4][:, :].rearrange("p (d e) -> p d e", d=2), ACT.Copy).then_inc(QA.sem, QA.one("sfin"))
                elif stage == 3:
                    act.wait_ge(QA.sem, QA.at("sfin", h))
                    act.dma_start(ret_p_out[bass.ds(h, 1), :, :].rearrange("o (d p) e -> p (o d) e", p=P), Sf[:, :, :])\
                        .then_inc(r_sf_stored, 16)
                elif stage == 4:
                    act.wait_ge(QP.sem, QP.at("so", h))
                    A(ro8[:, :], m[3][0:8, 0:RK], ACT.Copy).then_inc(QA.sem, QA.one("ro8"))
                    for d in range(2):
                        act.dma_start(ret_s_out[:, bass.ds(h, 1), d * P:(d + 1) * P, :].rearrange("b o p e -> p (b o) e"), R0[:, d, :, :])\
                            .then_inc(r_s0_stored, 16)
                elif stage == 5:
                    act.wait_ge(QP.sem, QP.at("so_turned", h))
                    A(roT[:, :, SEQ:TOK], m[0][:, 0:16].rearrange("p (e t) -> p e t", e=2), ACT.Copy).then_inc(QA.sem, QA.one("o_s"))
                    act.wait_ge(QV.sem, QV.at("oc", h))
                    A(kr[:, :, :], roT[:, :, :], ACT.Square).then_inc(QA.sem, QA.one("square"))
                elif stage == 6:
                    act.wait_ge(QV.sem, QV.at("var", h))
                    A(r1[:, :], r2[:, :], ACT.Ln).then_inc(QA.sem, QA.one("lnv"))
                    act.wait_ge(QA.sem, QA.at("lnv", h))
                    A(qr[:, 0, :], r1[:, :], ACT.Exp, scale=-0.5).then_inc(QA.sem, QA.one("rough"))
                    if more:
                        act.wait_ge(r_s0_stored, 32 * h + 32)
                        load_states(h + 1)
                elif stage == 7:
                    act.wait_ge(r_sf_stored, 16 * h + 16)
                    act.wait_ge(QV.sem, QV.at("gated", h))
                    A(mixed[0][:, bass.ds(h * 2, 2), :], qr[:, :, :], ACT.Copy).then_inc(QA.sem, QA.one("o_hi"))

            act.wait_ge(vec_landed, 16)
            for c in range(4):
                act.wait_ge(x_landed[c], 16)
                for t in range(4 * c, 4 * c + 4):
                    A(hA[0][:, t, :], x[:, t, :], ACT.Copy, scale=vec[:, V_MIX0 + t:V_MIX0 + t + 1]).then_inc(first_hi, 1)
                if c == 0:
                    hi_tile(E_IN, 0, 0)
            for c in range(4):
                A(ze[:, 4 * c:4 * c + 4, :], x[:, 4 * c:4 * c + 4, :], ACT.Square).then_inc(first_squares, 1)
            hi_tile(E_IN, 0, 1)
            rough_root(0)
            act.wait_ge(const_landed, 16 * N_CONST)

            def pick_query(b):
                act.wait_ge(q_spread, b)
                A(qm8[:, :], qt8[:, :], ACT.Copy, scale=eye8[:, bass.ds(b, 1)]).then_inc(q_picked, 1)

            def copy_query(b):
                act.wait_ge(q_spread, b + 1)
                act.wait_ge(k_used, PAGES * b)
                for k in range(2):
                    ins = A(qbc[:, k * 512:(k + 1) * 512], m[4 + k][:, :], ACT.Copy)
                ins.then_inc(q_copied, 1)
            for i in range(1, 5):
                for j in range(2):
                    hi_tile(E_IN, i, j)
            act.wait_ge(q8_turned, 1)
            for k in range(2):
                ins = A(qt8[:, k * 512:(k + 1) * 512], m[4 + k][0:8, :], ACT.Copy)
            ins.then_inc(q8_saved, 1)
            act.wait_ge(q8_saved, 1)
            pick_query(0)
            copy_query(0)
            with act.Fori(0, 7) as b:
                pick_query(b + 1)
                for c in range(3):
                    for j in range(2):
                        hi_tile(E_IN, b * 3 + (5 + c), j)
                copy_query(b + 1)
            for i in (26, 27):
                for j in range(2):
                    hi_tile(E_IN, i, j)
            act.wait_ge(RV.sem, RV.before(2 * HEADS))
            act.wait_ge(k_used, DEC * PAGES)
            with act.Fori(0, HEADS) as h:
                attention_head(h)
            act.wait_ge(SV.sem, SV.at("vs"))
            act.wait_ge(SP_.sem, SP_.at("own"))
            A(own[:, :, :], m[0][:, 0:64].rearrange("p (h b) -> p b h", h=HEADS), ACT.Copy).then_inc(SA.sem, SA.one("own"))
            act.wait_ge(SP_.sem, SP_.at("gates"))
            A(G[:, :, :, :].rearrange("p b j h -> p (b j h)"), m[1][:, :], ACT.Copy).then_inc(SA.sem, SA.one("G"))
            act.wait_ge(SV.sem, SV.at("oshift"))
            A(S[:, :, :, :], S[:, :, :, :], ACT.Exp, scale=P ** -0.5).then_inc(SA.sem, SA.one("exp"))
            A(po[:, :, :], po[:, :, :], ACT.Exp, scale=P ** -0.5).then_inc(SA.sem, SA.one("oexp"))
            act.wait_ge(SV.sem, SV.before(1))
            with act.Fori(0, HEADS) as h:
                hgrn_head(h)
            act.wait_ge(HV.sem, HV.before(HEADS))
            act.wait_ge(h_stored, 32 * HEADS + 1)
            act.wait_ge(TV.sem, TV.at("sum"))
            A(hA[0][:, HEADS:MT, SEQ:TOK], oS2[:, :, :], ACT.Copy).then_inc(TA.sem, TA.one("hi"))
            act.wait_ge(kv_stored, 32)
            for j in range(2):
                hi_tile(E_OUT, 0, j)
            body(E_OUT)
            turn_over(E_OUT, F0[0])
            rough_root(1)
            for a, b in zip(F0, F0[1:] + [O_IN]):
                if a is F0[0]:
                    act.wait_ge(cst_landed, 16)
                body(a)
                turn_over(a, b)
            rough_root(2)
            act.wait_ge(cout_stored, 16)
            load_states(0)
            load_decay(0)

            def project(h, s):
                if isinstance(h, int) and h == HEADS - 1 and s >= ZH - 2:
                    hi_tile(O_OUT, 0, s % 2)
                else:
                    hi_tile(O_IN, h * (ZH // 2) + (s // 2 + 1), s % 2)
            for s in range(ZH):
                project(0, s)
            with act.Fori(0, HEADS // 2 - 1) as i:
                for j in range(2):
                    for s in range(ZH):
                        project(i * 2 + (j + 1), s)
                        retention_stage(i * 2 + j, j, s)
            for s in range(ZH):
                project(HEADS - 1, s)
                retention_stage(HEADS - 2, 0, s)
            for s in range(ZH):
                retention_stage(HEADS - 1, 1, s, more=False)
            act.wait_ge(QV.sem, QV.before(HEADS))
            act.wait_ge(r_s0_stored, 32 * HEADS)
            act.wait_ge(r_sf_stored, 16 * HEADS)
            body(O_OUT)
            turn_over(O_OUT, F1[0])
            rough_root(3)
            for a, b in zip(F1, F1[1:] + [None]):
                if a is F1[0]:
                    act.wait_ge(cst_landed, 32)
                body(a)
                turn_over(a, b)
            rough_root(4)

        @block.vector
        def _(dve):
            v = nc.vector
            for steps in (NV, FV, RV, BV, HV, SV, TV, QV, IV, XV):
                steps.start(dve)

            def lo_tile(p, i, j):
                for k in range(4):
                    dve.wait_ge(hi_done, 8 * i + (p.u0 + 4 * j + k + 1))
                    n = p.ktu * P
                    v.tensor_tensor(wlo[:, 4 * j + k, 0:n], raw[:, 4 * j + k, 0:n], whi[:, 4 * j + k, 0:n].bitcast(F32),
                                    ALU.subtract).then_inc(lo_done, 1)

            def clear_sum(n):
                dve.wait_ge(norm_summed, n)
                v.memset(acc[:, :], 0.0).then_inc(acc_cleared, 1)

            def norm_tile(n, t, g, dst):
                dve.wait_ge(NA.sem, t * 2 + NA.at("hi", MT * (n - 1)))
                v.scalar_tensor_tensor(out=tile(dst[1], t), in0=tile(x, t), scalar=col(t + g),
                                       in1=tile(dst[0], t).bitcast(F32), op0=ALU.mult, op1=ALU.subtract)\
                    .then_inc(NV.sem, NV.one("lo"))
                dve.wait_ge(NA.sem, t * 2 + NA.at("square", MT * (n - 1)))
                dve.wait_ge(NV.sem, t * 2 + NV.at("lo", MT * (n - 1)))
                v.tensor_tensor(acc[:, :], acc[:, :], sq[:, :], ALU.add).then_inc(NV.sem, NV.one("sum"))

            def norm_factor(n):
                dve.wait_ge(norm_summed, n + 1)
                v.tensor_scalar(var[:, :], m[5][:, 0:TOK], 1.0 / D_MODEL, EPS, ALU.mult, ALU.add).then_inc(IV.sem, IV.one("var"))

            def refine(root, square, a, b, count, steps, turn):
                v.scalar_tensor_tensor(out=a, in0=square, scalar=-0.5, in1=root, op0=ALU.mult, op1=ALU.mult)\
                    .then_inc(count.sem, count.one(steps[0]))
                dve.wait_ge(count.sem, count.at(steps[0], turn))
                v.tensor_tensor(b, a, root, ALU.mult).then_inc(count.sem, count.one(steps[1]))
                dve.wait_ge(count.sem, count.at(steps[1], turn))
                v.scalar_tensor_tensor(out=root, in0=b, scalar=1.5, in1=root, op0=ALU.add, op1=ALU.mult)\
                    .then_inc(count.sem, count.one(steps[2]))

            def norm_root(n):
                dve.wait_ge(IA.sem, IA.at("rough", n))
                refine(rstd[:, :], var[:, :], sq[:, :], root_tmp[:, :], IV, ("n1", "n2", "rstd"), n)
                dve.wait_ge(IV.sem, IV.at("rstd", n))

            def evac(p, i, j):
                t = 2 * i + j
                if not p.kind.startswith("ffn") or j == 0:
                    dve.wait_ge(unit_used, 4 * t + (p.u0 + 4))
                bank = st[j]
                if p.kind.startswith("z_"):
                    v.tensor_tensor(tile(ze if p.kind == "z_even" else zo, t), bank[:, 0:TOK], rstd[:, :], ALU.mult)\
                        .then_inc(tile_free, 1)
                elif p.kind.startswith("out"):
                    v.tensor_tensor(tile(x, t), bank[:, 0:TOK], tile(x, t), ALU.add).then_inc(tile_free, 1)
                    if p.kind == "out_final":
                        dve.wait_ge(NFA, t + 1)
                        dve.wait_ge(XV.sem, XV.before(t))
                        v.tensor_tensor(acc[:, :], acc[:, :], sq[:, :], ALU.add).then_inc(XV.sem, XV.one("sum"))
                    elif p.kind != "out":
                        n, g = p.norm
                        dve.wait_ge(tile_free, t + (p.t0 + 1))
                        norm_tile(n, t, g, hB if p.kind == "out_norm_hB" else hA)
                elif j == 0:
                    pair = i + p.pair0
                    turn = pair + FT * p.layer
                    w = V_CONV + 4 * FT * p.layer
                    dve.wait_ge(FA.sem, FA.before(turn))
                    v.tensor_tensor(ab[:, PAD:PAD + SEQ], bank[:, 0:SEQ], rstd[:, 0:SEQ], ALU.mult)\
                        .then_inc(FV.sem, FV.one("a_prompt"))
                    v.tensor_tensor(ab_s[:, :, 2], bank[:, SEQ:TOK], rstd[:, SEQ:TOK], ALU.mult).then_inc(tile_free, 1)
                    dve.wait_ge(FA.sem, FA.at("history", turn))
                    dve.wait_ge(tile_free, 2 * i + (p.t0 + 1))
                    v.tensor_scalar(cv1[:, :], ab[:, 0:CONV_OUT], col(pair + w), col(pair + (w + 3 * FT)), ALU.mult, ALU.add)\
                        .then_inc(FV.sem, FV.one("c1"))
                    dve.wait_ge(FV.sem, FV.at("c1", turn))
                    v.scalar_tensor_tensor(out=cv2[:, :], in0=ab[:, 1:1 + CONV_OUT], scalar=col(pair + (w + FT)), in1=cv1[:, :],
                                           op0=ALU.mult, op1=ALU.add).then_inc(FV.sem, FV.one("c2"))
                    dve.wait_ge(FV.sem, FV.at("c2", turn))
                    v.scalar_tensor_tensor(out=cv1[:, :], in0=ab[:, 2:2 + CONV_OUT], scalar=col(pair + (w + 2 * FT)), in1=cv2[:, :],
                                           op0=ALU.mult, op1=ALU.add).then_inc(FV.sem, FV.one("c3"))
                else:
                    pair = i + p.pair0
                    turn = pair + FT * p.layer
                    dve.wait_ge(unit_used, 4 * t + (p.u0 + 4))
                    v.tensor_tensor(bt[:, :], bank[:, 0:TOK], rstd[:, :], ALU.mult).then_inc(tile_free, 1)
                    dve.wait_ge(FA.sem, FA.at("silu", turn))
                    dve.wait_ge(tile_free, 2 * i + (p.t0 + 2))
                    v.tensor_tensor(ug[:, 0:SEQ], sil[:, 0:SEQ], bt[:, 0:SEQ], ALU.mult).then_inc(FV.sem, FV.one("u_prompt"))
                    v.tensor_tensor(ug[:, SEQ:TOK], sil[:, PAD + SEQ:CONV_OUT:3], bt[:, SEQ:TOK], ALU.mult)\
                        .then_inc(FV.sem, FV.one("u_sample"))
                    dst = hid1 if p.kind == "ffn_hid1" else hA
                    dve.wait_ge(FA.sem, FA.at("hid_hi", turn))
                    v.tensor_tensor(tile(dst[1], i), ug[:, :], tile(dst[0], i).bitcast(F32), ALU.subtract)\
                        .then_inc(FV.sem, FV.one("hid_lo"))

            def start_phase(p):
                if p.kind == "out" or p.kind.startswith("out_"):
                    dve.wait_ge(tile_free, p.t0)
                if p.kind.startswith("out_"):
                    clear_sum(p.norm[0])
                    dve.wait_ge(acc_cleared, p.norm[0])

            def body(p):
                with dve.Fori(0, p.n // 2 - 1) as i:
                    for j in range(2):
                        lo_tile(p, i + 1, j)
                        evac(p, i, j)

            def turn_over(p, nxt):
                for j in range(2):
                    if nxt is not None:
                        lo_tile(nxt, 0, j)
                    evac(p, p.n // 2 - 1, j)

            def rope(first, turn0):
                with dve.Fori(0, 2) as half:
                    for t in range(4):
                        n = half * 4 + (turn0 + t)
                        z_ = ze[0:32, bass.ds(half * 4 + (first + t), 1), :].rearrange("p o n -> p (o n)")
                        dve.wait_ge(RP, n + 1)
                        dve.wait_ge(RV.sem, RV.before(n))
                        v.tensor_tensor(rt[:, 0, :], z_, ropeb[:, 0, :], ALU.mult).then_inc(RV.sem, RV.one("cos"))
                        v.tensor_tensor(rt[:, 1, :], m[t][0:32, 0:TOK], ropeb[:, 1, :], ALU.mult).then_inc(RV.sem, RV.one("sin"))
                        dve.wait_ge(RV.sem, RV.at("sin", n))
                        v.tensor_tensor(z_, rt[:, 0, :], rt[:, 1, :], ALU.add).then_inc(RV.sem, RV.one("add"))

            def score_page(b, g):
                dve.wait_ge(k_landed[g % 4], 64 * b + 16 * (g // 4 + 1))
                for h in range(HEADS):
                    kk = kring[:, g % 4, h * P:(h + 1) * P]
                    ins = v.tensor_tensor_reduce(kk, kk, qbc[:, h * P:(h + 1) * P], 1.0, 0.0, ALU.mult, ALU.add,
                                                 Sb[:, g, h:h + 1])
                ins.then_inc(k_used, 1)

            def save_scores(b):
                dve.wait_ge(k_used, PAGES * (b + 1))
                v.tensor_copy(S[:, bass.ds(b, 1), :, :].rearrange("p o g h -> p (o g h)"),
                              Sb[:, :, :].rearrange("p g h -> p (g h)")).then_inc(s_saved, 1)
                dve.wait_ge(s_saved, b + 1)

            def attention_head(h):
                dve.wait_ge(BP.sem, BP.at("scores", h))
                v.tensor_tensor(sm[:, :], m[0][:, 0:384], cau[:, :], ALU.add).then_inc(BV.sem, BV.one("masked"))
                dve.wait_ge(BV.sem, BV.at("masked", h))
                v.tensor_reduce(mx2[:, 0:1], sm[:, 0:P], AX_X, ALU.max).then_inc(BV.sem, BV.one("max0"))
                v.tensor_reduce(mx2[:, 1:2], sm[:, P:384], AX_X, ALU.max).then_inc(BV.sem, BV.one("max1"))
                dve.wait_ge(BV.sem, BV.at("max1", h))
                v.tensor_scalar(nmx[:, :], mx2[:, :], -(P ** -0.5), None, ALU.mult).then_inc(BV.sem, BV.one("negmax"))
                dve.wait_ge(BA.sem, BA.at("exp1", h))
                v.reciprocal(rl[:, :], lsum[:, :]).then_inc(BV.sem, BV.one("recip"))
                dve.wait_ge(BV.sem, BV.at("recip", h))
                v.tensor_scalar(sm[:, 0:P], sm[:, 0:P], rl[:, 0:1], None, ALU.mult).then_inc(BV.sem, BV.one("p0"))
                v.tensor_scalar(sm[:, P:384], sm[:, P:384], rl[:, 1:2], None, ALU.mult).then_inc(BV.sem, BV.one("p1"))
                dve.wait_ge(BA.sem, BA.at("o_hi", h))
                v.tensor_tensor(tile(hA[1], h + HEADS, 0, SEQ), m[3][:, 0:SEQ], tile(hA[0], h + HEADS, 0, SEQ).bitcast(F32),
                                ALU.subtract).then_inc(BV.sem, BV.one("o_lo"))

            def hgrn_head(h):
                f = tile(ze, h + Z_FA)
                dve.wait_ge(HA.sem, HA.at("ln", h))
                v.scalar_tensor_tensor(out=lsg[:, :], in0=f, scalar=0.0, in1=t1[:, :], op0=ALU.min, op1=ALU.subtract)\
                    .then_inc(HV.sem, HV.one("ls"))
                v.scalar_tensor_tensor(out=t2[:, :], in0=f, scalar=0.0, in1=t1[:, :], op0=ALU.max, op1=ALU.add)\
                    .then_inc(HV.sem, HV.one("mxf"))
                dve.wait_ge(HA.sem, HA.at("ei", h))
                v.tensor_scalar(sg[:, :], sg[:, :], 1.0, None, ALU.add).then_inc(HV.sem, HV.one("g1"))
                dve.wait_ge(HV.sem, HV.at("g1", h))
                v.reciprocal(sg[:, :], sg[:, :]).then_inc(HV.sem, HV.one("sg"))
                v.tensor_scalar(va[:, :], va[:, :], 1.0, None, ALU.add).then_inc(HV.sem, HV.one("i1"))
                dve.wait_ge(HV.sem, HV.at("i1", h))
                v.reciprocal(va[:, :], va[:, :]).then_inc(HV.sem, HV.one("ir"))
                dve.wait_ge(HV.sem, HV.at("ir", h))
                v.tensor_tensor(va[:, :], va[:, :], tile(ze, h + Z_IA), ALU.mult).then_inc(HV.sem, HV.one("va"))
                v.tensor_tensor_scan(bcum[:, :], reset[:, :], lsg[:, 0:SEQ], 0.0, ALU.mult, ALU.add).then_inc(HV.sem, HV.one("cum"))
                dve.wait_ge(HV.sem, HV.at("cum", h))
                for l in range(LEVELS):
                    B = 1 << l
                    bv = bcum[:, :].rearrange("p (n w) -> p n w", w=2 * B)
                    ev = EL[:, l, :].rearrange("p (n w) -> p n w", w=2 * B)
                    ref = bv[:, :, B - 1:B].to_broadcast([P, SEQ // (2 * B), B])
                    v.tensor_tensor(ev[:, :, 0:B], ref, bv[:, :, 0:B], ALU.subtract).then_inc(HV.sem, HV.one(f"d{l}l"))
                    v.tensor_tensor(ev[:, :, B:2 * B], bv[:, :, B:2 * B], ref, ALU.subtract).then_inc(HV.sem, HV.one(f"d{l}r"))
                dve.wait_ge(HA.sem, HA.at("levels", h))
                for c in range(2):
                    s = slice(c * P, (c + 1) * P)
                    if c:
                        dve.wait_ge(HP.sem, HP.at("lev0", h))
                    q_ = ze[:, bass.ds(h + Z_QA, 1), s].to_broadcast([P, LEVELS, P])
                    v.tensor_tensor(QE[:, :, :], EL[:, :, s], q_, ALU.mult).then_inc(HV.sem, HV.one(f"qe{c}"))
                    v.tensor_tensor(KE[:, :, :], EL[:, :, s], ka[:, None, s].to_broadcast([P, LEVELS, P]), ALU.mult)\
                        .then_inc(HV.sem, HV.one(f"ke{c}"))
                    dve.wait_ge(HP.sem, HP.at(f"lev{c}", h))
                    v.tensor_tensor(pr[:, 0:4, :], m[0][:, :].rearrange("p (l t) -> p l t", l=4), levm[:, 0:4, :], ALU.mult)\
                        .then_inc(HV.sem, HV.one(f"pr{c}a"))
                    v.tensor_tensor(pr[:, 4:7, :], m[1][:, 0:384].rearrange("p (l t) -> p l t", l=3), levm[:, 4:7, :], ALU.mult)\
                        .then_inc(HV.sem, HV.one(f"pr{c}b"))
                    dve.wait_ge(HV.sem, HV.at(f"pr{c}b", h))
                    v.tensor_reduce(Aatt[:, c, :], pr[:, :, :].rearrange("p l t -> p t l"), AX_X, ALU.add)\
                        .then_inc(HV.sem, HV.one(f"att{c}"))
                bc = bcum[:, :].rearrange("p (c n) -> p c n", n=CHUNK)
                v.tensor_tensor(t2[:, 0:SEQ].rearrange("p (c n) -> p c n", n=CHUNK), bc[:, :, CHUNK - 1:CHUNK].to_broadcast([P, NCH, CHUNK]),
                                bc, ALU.subtract).then_inc(HV.sem, HV.one("dk"))
                dve.wait_ge(HA.sem, HA.at("dke", h))
                v.tensor_tensor(t2[:, 0:SEQ], t2[:, 0:SEQ], ka[:, 0:SEQ], ALU.mult).then_inc(HV.sem, HV.one("kd"))
                dve.wait_ge(HA.sem, HA.at("eb", h))
                v.tensor_tensor(qdec[:, :], t1[:, 0:SEQ], tile(ze, h + Z_QA, 0, SEQ), ALU.mult).then_inc(HV.sem, HV.one("qdec"))
                dve.wait_ge(HP.sem, HP.at("U", h))
                dve.wait_ge(h_s0_landed, 16 * h + 16)
                v.tensor_copy(Sst[:, 0, :], m[4][:, 0:P]).then_inc(HV.sem, HV.one("s1"))
                for c in range(1, NCH):
                    dve.wait_ge(HV.sem, HV.at(f"s{c}", h))
                    v.scalar_tensor_tensor(out=Sst[:, c, :], in0=Sst[:, c - 1, :], scalar=ebl[:, c:c + 1],
                                           in1=m[4 - c % 2][:, (c // 2) * P:(c // 2 + 1) * P], op0=ALU.mult, op1=ALU.add)\
                        .then_inc(HV.sem, HV.one(f"s{c + 1}"))
                dve.wait_ge(HA.sem, HA.at("kv8", h))
                v.tensor_tensor(vm8[:, :, :], kv8[:, None, P:2 * P].to_broadcast([8, 8, P]), eye8[:, :, None].to_broadcast([8, 8, P]),
                                ALU.mult).then_inc(HV.sem, HV.one("vm"))
                v.tensor_tensor(qm[:, :, :], ze[:, bass.ds(h + Z_QA, 1), SEQ:TOK].to_broadcast([P, 8, 8]), eye[:, :, :], ALU.mult)\
                    .then_inc(HV.sem, HV.one("qm"))
                dve.wait_ge(h_s0_landed, 16 * h + 16)
                for b in range(DEC):
                    if b % 4 == 0:
                        dve.wait_ge(HP.sem, HP.at("kv_a" if b == 0 else "kv_b", h))
                    v.scalar_tensor_tensor(out=S0[:, b, :], in0=S0[:, b, :], scalar=fg[:, b:b + 1],
                                           in1=m[1 + b // 4][:, (b % 4) * P:(b % 4 + 1) * P], op0=ALU.mult, op1=ALU.add)\
                        .then_inc(HV.sem, HV.one(f"sn{b}"))
                dve.wait_ge(v_used, PAGES * (h + 1))
                for k in range(2):
                    v.tensor_tensor(om[:, k * 512:(k + 1) * 512], st[k][0:8, :], blk[:, k * 512:(k + 1) * 512], ALU.mult)\
                        .then_inc(om_ready, 1)
                dve.wait_ge(HP.sem, HP.at("ssum", h))
                v.tensor_scalar(lsg[:, :], m[0][:, 0:TOK], 1.0 / P, EPS, ALU.mult, ALU.add).then_inc(HV.sem, HV.one("var"))
                dve.wait_ge(HA.sem, HA.at("rough", h))
                refine(t1[:, :], lsg[:, :], t2[:, :], ka[:, :], HV, ("n1", "n2", "rstd"), h)
                dve.wait_ge(HV.sem, HV.at("rstd", h))
                v.scalar_tensor_tensor(out=t1[:, :], in0=oT[:, :], scalar=col(h + V_GNH), in1=t1[:, :], op0=ALU.mult, op1=ALU.mult)\
                    .then_inc(HV.sem, HV.one("og"))
                dve.wait_ge(HV.sem, HV.at("og", h))
                v.tensor_tensor(t2[:, :], t1[:, :], sg[:, :], ALU.mult).then_inc(HV.sem, HV.one("gated"))
                dve.wait_ge(HA.sem, HA.at("o_hi", h))
                v.tensor_tensor(tile(hA[1], h), t2[:, :], tile(hA[0], h).bitcast(F32), ALU.subtract).then_inc(HV.sem, HV.one("o_lo"))

            def select_blocks():
                v.memset(cmp[:, :, :, :], 0.0).then_inc(SV.sem, SV.one("clear_cmp"))
                v.memset(rank[:, :, :, :], 0.0).then_inc(SV.sem, SV.one("rank0"))
                dve.wait_ge(SA.sem, SA.at("G"))
                last = "rank0"
                for i in range(BLOCKS):
                    dve.wait_ge(SV.sem, SV.at(last))
                    if i > 0:
                        v.tensor_tensor(cmp[:, :, 0:i, :], G[:, :, i:i + 1, :].to_broadcast([P, DEC, i, HEADS]), G[:, :, 0:i, :],
                                        ALU.is_gt).then_inc(SV.sem, SV.one(f"gt{i}"))
                        last = f"gt{i}"
                    if i < BLOCKS - 1:
                        n = BLOCKS - 1 - i
                        v.tensor_tensor(cmp[:, :, i + 1:BLOCKS, :], G[:, :, i:i + 1, :].to_broadcast([P, DEC, n, HEADS]),
                                        G[:, :, i + 1:BLOCKS, :], ALU.is_ge).then_inc(SV.sem, SV.one(f"ge{i}"))
                        last = f"ge{i}"
                    dve.wait_ge(SV.sem, SV.at(last))
                    if i > 0:
                        ins = v.tensor_tensor(rank[:, :, 0:i, :], rank[:, :, 0:i, :], cmp[:, :, 0:i, :], ALU.add)
                    if i < BLOCKS - 1:
                        ins = v.tensor_tensor(rank[:, :, i + 1:BLOCKS, :], rank[:, :, i + 1:BLOCKS, :], cmp[:, :, i + 1:BLOCKS, :], ALU.add)
                    ins.then_inc(SV.sem, SV.one(f"add{i}"))
                    last = f"add{i}"
                dve.wait_ge(SV.sem, SV.at(last))
                v.tensor_scalar(cmp[:, :, :, :], rank[:, :, :, :], float(TOPK), -1.0, ALU.is_lt, ALU.add).then_inc(SV.sem, SV.one("keep"))
                dve.wait_ge(SV.sem, SV.at("keep"))
                v.tensor_scalar(cmp[:, :, :, :], cmp[:, :, :, :], BIG, None, ALU.mult).then_inc(SV.sem, SV.one("minus"))
                dve.wait_ge(SV.sem, SV.at("minus"))
                Sv = S[:, :, :, :].rearrange("p b (j two) h -> p (b j) two h", two=2)
                kb = cmp[:, :, :, :].rearrange("p b j h -> p (b j) h")[:, :, None, :].to_broadcast([P, DEC * BLOCKS, 2, HEADS])
                dve.wait_ge(SP_.sem, SP_.at("gates"))
                v.tensor_tensor(Sv, Sv, kb, ALU.add).then_inc(SV.sem, SV.one("bias"))
                dve.wait_ge(SV.sem, SV.at("bias"))
                v.tensor_reduce(mxt[:, :, :], S[:, :, :, :].rearrange("p b g h -> p b h g"), AX_X, ALU.max).then_inc(SV.sem, SV.one("tmax"))
                dve.wait_ge(SP_.sem, SP_.at("mxT"))
                v.tensor_reduce(mx64[:, :], m[2][0:64, 0:P], AX_X, ALU.max).then_inc(SV.sem, SV.one("rmax"))
                dve.wait_ge(SV.sem, SV.at("rmax"))
                v.tensor_scalar(dg[:, :], ident[0:64, 0:64], mx64[:, :], None, ALU.mult).then_inc(SV.sem, SV.one("diag"))
                dve.wait_ge(SP_.sem, SP_.at("mxb"))
                v.tensor_tensor(mxa[:, :, :], m[3][:, 0:64].rearrange("p (b h) -> p b h", b=DEC), own[:, :, :], ALU.max)\
                    .then_inc(SV.sem, SV.one("mxa"))
                dve.wait_ge(SV.sem, SV.at("mxa"))
                v.tensor_tensor(S[:, :, :, :], S[:, :, :, :], mxa[:, :, None, :].to_broadcast([P, DEC, PAGES, HEADS]), ALU.subtract)\
                    .then_inc(SV.sem, SV.one("shift"))
                v.tensor_tensor(po[:, :, :], own[:, :, :], mxa[:, :, :], ALU.subtract).then_inc(SV.sem, SV.one("oshift"))
                dve.wait_ge(SA.sem, SA.at("oexp"))
                v.tensor_reduce(mxt[:, :, :], S[:, :, :, :].rearrange("p b g h -> p b h g"), AX_X, ALU.add).then_inc(SV.sem, SV.one("tsum"))
                dve.wait_ge(SP_.sem, SP_.at("den"))
                v.tensor_tensor(mxa[:, :, :], m[4][:, 0:64].rearrange("p (b h) -> p b h", b=DEC), po[:, :, :], ALU.add)\
                    .then_inc(SV.sem, SV.one("den"))
                dve.wait_ge(SV.sem, SV.at("den"))
                v.reciprocal(own[:, :, :], mxa[:, :, :]).then_inc(SV.sem, SV.one("rden"))
                dve.wait_ge(SV.sem, SV.at("rden"))
                v.tensor_tensor(S[:, :, :, :], S[:, :, :, :], own[:, :, None, :].to_broadcast([P, DEC, PAGES, HEADS]), ALU.mult)\
                    .then_inc(SV.sem, SV.one("p"))
                v.tensor_tensor(po[:, :, :], po[:, :, :], own[:, :, :], ALU.mult).then_inc(SV.sem, SV.one("po"))

            def retention_stage(h, par, stage):
                z = ZH * par
                if stage == 0:
                    for w, first, dst, s in (("q", z + Z_Q, qr, 1.0), ("k", z + Z_K, kr, RK ** -0.5)):
                        x1, x2 = zo[:, first, :], zo[:, first + 1, :]
                        if w == "q":
                            dve.wait_ge(QA.sem, QA.before(h))
                            dve.wait_ge(QP.sem, QP.before(h))
                            dve.wait_ge(QV.sem, QV.before(h))
                            dve.wait_ge(tile_free, ZH * h + (O_IN.t0 + ZH))
                        else:
                            dve.wait_ge(QV.sem, QV.at("qx2", h))
                        for a, b, o, op, n in ((x1, x2, 0, ALU.subtract, ("a", "b", "x1")), (x2, x1, 1, ALU.add, ("c", "d", "x2"))):
                            if o:
                                dve.wait_ge(QV.sem, QV.at(w + "x1", h))
                            v.scalar_tensor_tensor(out=r1[:, :], in0=a, scalar=s, in1=ropec[:, 0, :], op0=ALU.mult, op1=ALU.mult)\
                                .then_inc(QV.sem, QV.one(w + n[0]))
                            v.scalar_tensor_tensor(out=r2[:, :], in0=b, scalar=s, in1=ropec[:, 1, :], op0=ALU.mult, op1=ALU.mult)\
                                .then_inc(QV.sem, QV.one(w + n[1]))
                            dve.wait_ge(QV.sem, QV.at(w + n[1], h))
                            v.tensor_tensor(dst[:, o, :], r1[:, :], r2[:, :], op).then_inc(QV.sem, QV.one(w + n[2]))
                elif stage == 1:
                    dve.wait_ge(QP.sem, QP.at("att", h))
                    dve.wait_ge(dm_landed, 16 * h + 16)
                    v.tensor_tensor(aT[:, :], m[0][:, 0:384], dmat[:, :], ALU.mult).then_inc(QV.sem, QV.one("att"))
                    dve.wait_ge(QP.sem, QP.at("k_turned", h))
                    for s in range(2):
                        v.tensor_scalar(rk_[:, s, :], m[2][:, s * RK:(s + 1) * RK],
                                        sdec[:, bass.ds(h, 1), s:s + 1].rearrange("p o n -> p (o n)"), None, ALU.mult)\
                            .then_inc(QV.sem, QV.one(f"k{s}"))
                    for d in range(2):
                        ins = v.tensor_tensor(rqm[:, d, :, :], qr[:, d:d + 1, SEQ:TOK].to_broadcast([P, 8, 8]), reye[:, :, :], ALU.mult)
                    ins.then_inc(QV.sem, QV.one("qm"))
                    dve.wait_ge(QA.sem, QA.at("kv8", h))
                    spread_values(0)
                elif stage in (2, 3):
                    dve.wait_ge(r_s0_landed, 32 * h + 32)
                    banks = (1, 2, 5, 0) if stage == 2 else (1, 2, 5, 4)
                    for q in (2 * stage - 4, 2 * stage - 3):
                        for d in range(2):
                            dve.wait_ge(QP.sem, QP.at(f"kv{q}{d}", h))
                            v.scalar_tensor_tensor(out=R0[:, d, 2 * q:2 * q + 2, :], in0=R0[:, d, 2 * q:2 * q + 2, :],
                                                   scalar=gam[:, bass.ds(h, 1)],
                                                   in1=m[banks[2 * (q % 2) + d]][:, :].rearrange("p (b e) -> p b e", b=2),
                                                   op0=ALU.mult, op1=ALU.add).then_inc(QV.sem, QV.one(f"s{d}_{q}"))
                    if stage == 2:
                        spread_values(1)
                elif stage == 5:
                    dve.wait_ge(QP.sem, QP.at("ssum", h))
                    v.tensor_scalar(r1[:, :], m[1][:, 0:TOK], 1.0 / RK, None, ALU.mult).then_inc(QV.sem, QV.one("mean"))
                    dve.wait_ge(QV.sem, QV.at("mean", h))
                    v.tensor_tensor(roT[:, :, :], roT[:, :, :], r1[:, None, :].to_broadcast([P, 2, TOK]), ALU.subtract)\
                        .then_inc(QV.sem, QV.one("oc"))
                elif stage == 6:
                    dve.wait_ge(QP.sem, QP.at("vsum", h))
                    v.tensor_scalar(r2[:, :], m[2][:, 0:TOK], 1.0 / RK, EPS, ALU.mult, ALU.add).then_inc(QV.sem, QV.one("var"))
                    dve.wait_ge(QA.sem, QA.at("rough", h))
                    refine(qr[:, 0, :], r2[:, :], r1[:, :], qr[:, 1, :], QV, ("n1", "n2", "rstd"), h)
                elif stage == 7:
                    dve.wait_ge(QV.sem, QV.at("rstd", h))
                    for e in range(2):
                        ins = v.scalar_tensor_tensor(out=roT[:, e, :], in0=roT[:, e, :], scalar=col(h * 2 + (V_GNR + e)), in1=qr[:, 0, :],
                                                     op0=ALU.mult, op1=ALU.mult)
                    ins.then_inc(QV.sem, QV.one("og"))
                    dve.wait_ge(QV.sem, QV.at("og", h))
                    v.tensor_tensor(qr[:, :, :], roT[:, :, :], gate[:, :, :], ALU.mult).then_inc(QV.sem, QV.one("gated"))
                    dve.wait_ge(QA.sem, QA.at("o_hi", h))
                    v.tensor_tensor(mixed[1][:, bass.ds(h * 2, 2), :], qr[:, :, :], mixed[0][:, bass.ds(h * 2, 2), :].bitcast(F32),
                                    ALU.subtract).then_inc(QV.sem, QV.one("o_lo"))

            def spread_values(half):
                v.tensor_tensor(rvm[:, :, :], rkv8[:, None, RK:2 * RK].to_broadcast([8, 4, RK]),
                                reye8[:, 4 * half:4 * half + 4, None].to_broadcast([8, 4, RK]), ALU.mult)\
                    .then_inc(QV.sem, QV.one(f"vm{half}"))

            v.memset(ones[:, :], 1.0).then_inc(consts_set, 1)
            for t in range(MT):
                dve.wait_ge(first_hi, t + 1)
                v.scalar_tensor_tensor(out=hA[1][:, t, :], in0=x[:, t, :], scalar=vec[:, V_MIX0 + t:V_MIX0 + t + 1],
                                       in1=hA[0][:, t, :].bitcast(F32), op0=ALU.mult, op1=ALU.subtract).then_inc(first_lo, 1)
                if t == 3:
                    lo_tile(E_IN, 0, 0)
            lo_tile(E_IN, 0, 1)
            norm_factor(0)
            norm_root(0)
            with dve.Fori(0, 4) as i:
                for j in range(2):
                    lo_tile(E_IN, i + 1, j)
                    evac(E_IN, i, j)
            dve.wait_ge(const_landed, 16 * N_CONST)
            dve.wait_ge(tile_free, HEADS)
            rope(Z_QB, 0)
            share = (3, 3, 3, 3, 2, 2)
            with dve.Fori(0, 7) as b:
                g = 0
                dve.wait_ge(q_copied, b + 1)
                for n, k in enumerate(share):
                    lo_tile(E_IN, b * 3 + (5 + n // 2), n % 2)
                    evac(E_IN, b * 3 + (4 + n // 2), n % 2)
                    for _ in range(k):
                        score_page(b, g)
                        g += 1
                save_scores(b)
            for i in (26, 27):
                for j in range(2):
                    lo_tile(E_IN, i, j)
                    evac(E_IN, i - 1, j)
            dve.wait_ge(q_copied, DEC)
            for g in range(PAGES):
                score_page(7, g)
            save_scores(7)
            turn_over(E_IN, None)
            dve.wait_ge(tile_free, ZE)
            rope(Z_KB, HEADS)
            dve.wait_ge(RV.sem, RV.before(2 * HEADS))
            with dve.Fori(0, HEADS) as h:
                attention_head(h)
            dve.wait_ge(BV.sem, BV.before(HEADS))
            v.tensor_tensor(qk[:, :, :], ze[:, Z_QB:Z_QB + HEADS, SEQ:TOK], ze[:, Z_KB:Z_KB + HEADS, SEQ:TOK], ALU.mult)\
                .then_inc(SV.sem, SV.one("qk"))
            v.tensor_copy(vs[:, :, :], ze[:, Z_VB:Z_VB + HEADS, SEQ:TOK]).then_inc(SV.sem, SV.one("vs"))
            dve.wait_ge(SV.sem, SV.at("vs"))
            select_blocks()
            dve.wait_ge(SV.sem, SV.before(1))
            dve.wait_ge(hc_landed, 48)
            with dve.Fori(0, HEADS) as h:
                hgrn_head(h)
            dve.wait_ge(HV.sem, HV.before(HEADS))
            dve.wait_ge(HP.sem, HP.before(HEADS))
            dve.wait_ge(h_stored, 32 * HEADS + 1)
            dve.wait_ge(SV.sem, SV.before(1))
            v.tensor_tensor(oS2[:, :, :], po[:, :, :].rearrange("p b h -> p h b"), vs[:, :, :], ALU.mult)\
                .then_inc(TV.sem, TV.one("pv"))
            dve.wait_ge(v_saved, DEC)
            dve.wait_ge(TV.sem, TV.at("pv"))
            v.tensor_tensor(oS2[:, :, :], oS2[:, :, :], oS[:, :, :], ALU.add).then_inc(TV.sem, TV.one("sum"))
            dve.wait_ge(TA.sem, TA.at("hi"))
            v.tensor_tensor(hA[1][:, HEADS:MT, SEQ:TOK], oS2[:, :, :], hA[0][:, HEADS:MT, SEQ:TOK].bitcast(F32), ALU.subtract)\
                .then_inc(TV.sem, TV.one("lo"))
            dve.wait_ge(kv_stored, 32)
            start_phase(E_OUT)
            for j in range(2):
                lo_tile(E_OUT, 0, j)
            body(E_OUT)
            turn_over(E_OUT, F0[0])

            def clear_pad(n):
                v.memset(ab[:, 0:PAD], 0.0).then_inc(ab_cleared, 1)
                dve.wait_ge(ab_cleared, n)
            norm_factor(1)
            norm_root(1)
            clear_pad(1)
            for a, b in zip(F0, F0[1:] + [O_IN]):
                start_phase(a)
                body(a)
                turn_over(a, b)
            norm_factor(2)
            norm_root(2)
            dve.wait_ge(cout_stored, 16)

            def project(h, par, s):
                if isinstance(h, int) and h == HEADS - 1 and s >= ZH - 2:
                    lo_tile(O_OUT, 0, s % 2)
                else:
                    lo_tile(O_IN, h * (ZH // 2) + (s // 2 + 1), s % 2)
                dve.wait_ge(unit_used, 4 * ZH * h + (O_IN.u0 + 4 * s + 4))
                v.tensor_tensor(zo[:, ZH * par + s, :], st[s % 2][:, 0:TOK], rstd[:, :], ALU.mult).then_inc(tile_free, 1)
            for s in range(ZH):
                project(0, 0, s)
            dve.wait_ge(oc_landed, 16 * 5)
            with dve.Fori(0, HEADS // 2 - 1) as i:
                for j in range(2):
                    for s in range(ZH):
                        project(i * 2 + (j + 1), 1 - j, s)
                        retention_stage(i * 2 + j, j, s)
            for s in range(ZH):
                project(HEADS - 1, 1, s)
                retention_stage(HEADS - 2, 0, s)
            for s in range(ZH):
                retention_stage(HEADS - 1, 1, s)
            dve.wait_ge(QV.sem, QV.before(HEADS))
            dve.wait_ge(QP.sem, QP.before(HEADS))
            dve.wait_ge(r_s0_stored, 32 * HEADS)
            dve.wait_ge(r_sf_stored, 16 * HEADS)
            start_phase(O_OUT)
            body(O_OUT)
            turn_over(O_OUT, F1[0])
            norm_factor(3)
            norm_root(3)
            clear_pad(2)
            for a, b in zip(F1, F1[1:] + [None]):
                start_phase(a)
                body(a)
                turn_over(a, b)
            norm_factor(4)
            norm_root(4)
            with dve.Fori(0, MT) as t:
                v.scalar_tensor_tensor(out=tile(x, t), in0=tile(x, t), scalar=col(t + V_FINAL), in1=rstd[:, :],
                                       op0=ALU.mult, op1=ALU.mult).then_inc(y_ready, 1)

        @block.gpsimd
        def _(pool):
            pool.dma_start(pt[:, :], page_table).then_inc(pt_landed, 16)
            pool.wait_ge(pt_landed, 16)

            def load_page(cache, ring, b, g, landed, used, first):
                page = pool.snap(pool.value_load(pt[0:1, bass.ds(b * PAGES + g, 1)], min_val=0, max_val=cache.shape[0] - 1))
                if not first:
                    pool.wait_ge(used, b * PAGES + (g - 3))
                pool.dma_start(ring[:, g % 4, :], cache[bass.ds(page, 1), :, :].rearrange("o t n -> t (o n)"))\
                    .then_inc(landed[g % 4], 16)

            for g in range(PAGES):
                load_page(cache_k, kring, 0, g, k_landed, k_used, g < 4)
            with pool.Fori(1, DEC) as b:
                for g in range(PAGES):
                    load_page(cache_k, kring, b, g, k_landed, k_used, False)
            pool.wait_ge(tile_free, ZE)
            pool.wait_ge(RV.sem, RV.before(2 * HEADS))
            pool.dma_start(kT_out, ze[:, Z_KB:Z_KB + HEADS, :]).then_inc(kv_stored, 16)
            pool.dma_start(vT_out, ze[:, Z_VB:Z_VB + HEADS, :]).then_inc(kv_stored, 16)
            pool.wait_ge(unit_used, 4 * ZE)
            pool.dma_start(blk[:, :], c_blk).then_inc(hc_landed, 16)
            for g in range(4):
                load_page(cache_v, vring, 0, g, v_landed, v_used, True)
            pool.wait_ge(BV.sem, BV.before(HEADS))
            pool.wait_ge(BP.sem, BP.before(HEADS))
            pool.wait_ge(BA.sem, BA.before(HEADS))
            pool.wait_ge(SV.sem, SV.before(1))
            pool.wait_ge(kv_stored, 32)
            pool.dma_start(levm[:, :, :], c_level).then_inc(hc_landed, 16)
            pool.dma_start(reset[:, :], c_reset).then_inc(hc_landed, 16)
            for g in range(4, PAGES):
                load_page(cache_v, vring, 0, g, v_landed, v_used, False)
            with pool.Fori(1, DEC) as b:
                for g in range(PAGES):
                    load_page(cache_v, vring, b, g, v_landed, v_used, False)
            pool.wait_ge(TV.sem, TV.before(1))
            pool.wait_ge(kv_stored, 32)
            pool.dma_start(cst[:, :, :], conv_state[0]).then_inc(cst_landed, 16)
            pool.wait_ge(FA.sem, FA.before(FT))
            pool.dma_start(conv_out[0], cout[:, :, :]).then_inc(cout_stored, 16)
            pool.wait_ge(cout_stored, 16)
            pool.wait_ge(FV.sem, FV.before(FT))
            pool.wait_ge(unit_used, 4 * F0[-1].end())
            for dst, src in ((ropec[:, :, :], c_rope_c), (sdec[:, :, :], c_sdec), (gam[:, :], c_gamma), (reye8[:, :], c_eye8),
                             (reye[:, :, :], c_eye)):
                pool.dma_start(dst, src).then_inc(oc_landed, 16)

            pool.wait_ge(QA.sem, QA.before(HEADS))
            pool.wait_ge(QV.sem, QV.before(HEADS))
            pool.wait_ge(QP.sem, QP.before(HEADS))
            pool.wait_ge(r_s0_stored, 32 * HEADS)
            pool.wait_ge(r_sf_stored, 16 * HEADS)
            pool.dma_start(cst[:, :, :], conv_state[1]).then_inc(cst_landed, 16)
            pool.wait_ge(FA.sem, FA.before(2 * FT))
            pool.dma_start(conv_out[1], cout[:, :, :]).then_inc(cout_stored, 16)
            pool.wait_ge(cout_stored, 32)


def _tiles(w, ktu):
    k, n = w.shape
    return np.ascontiguousarray(w.reshape(2, k // 256, P, n // P, P).transpose(3, 0, 2, 1, 4)).reshape(n // P, 2, P, 2 * ktu * P)


def _columns(a):
    return np.ascontiguousarray(a.reshape(-1, P).T)


def _constants():
    f = np.float32
    pos = np.concatenate([np.arange(SEQ), np.full(DEC, 2048)]).astype(f)

    def angles(half, theta):
        inv = f(theta) ** (-np.arange(half, dtype=f) / f(half))
        return (pos[None, :] * inv.astype(f)[:, None]).astype(f)
    ab_, ac = angles(16, 500000.0), angles(P, 10000.0)
    rope_b = np.stack([np.concatenate([np.cos(ab_)] * 2), np.concatenate([-np.sin(ab_), np.sin(ab_)])], 1).astype(f)
    rope_c = np.stack([np.cos(ac), np.sin(ac)], 1).astype(f)
    perm = np.zeros((32, 32), f)
    perm[np.arange(32), (np.arange(32) + 16) % 32] = 1
    i = np.arange(P)
    causal = np.where(i[None, :] <= i[:, None], 0, -BIG).astype(f)
    cau = np.concatenate([causal, np.zeros((P, P), f), causal], 1)
    lg = np.log(1.0 - 2.0 ** (-5.0 - np.arange(HEADS)))
    t = np.arange(SEQ)
    d = np.where(t[None, :] >= t[:, None], t[None, :] - t[:, None], 0)
    full = np.where(t[None, :] >= t[:, None], np.exp(d * lg[:, None, None]), 0.0)
    decay = np.concatenate([full[:, 0:P, :], full[:, P:, P:]], 2).astype(f)
    sdec = np.exp((SEQ - 1 - t)[None, :] * lg[:, None]).reshape(HEADS, 2, P).transpose(2, 0, 1).astype(f)
    gamma = np.broadcast_to(np.exp(lg)[None, :], (P, HEADS)).astype(f)
    level = np.zeros((P, LEVELS + 1, P), f)
    for l in range(LEVELS):
        B = 1 << l
        level[:, l, :] = ((i[:, None] // (2 * B)) == (i[None, :] // (2 * B))) & (i[:, None] % (2 * B) < B) & (i[None, :] % (2 * B) >= B)
    level[:, LEVELS, :] = np.eye(P)
    reset = np.broadcast_to((t % CHUNK != 0).astype(f), (P, SEQ))
    return {
        "c_ident": np.eye(P, dtype=f), "c_eye8": np.eye(8, dtype=f),
        "c_eye": np.broadcast_to(np.eye(8, dtype=f), (P, 8, 8)), "c_blk": np.kron(np.eye(8), np.ones((1, P))).astype(f),
        "c_causal": cau, "c_rope_b": rope_b, "c_perm": perm, "c_rope_c": rope_c, "c_decay": decay, "c_sdec": sdec,
        "c_gamma": gamma, "c_level": level, "c_reset": reset,
    }


_OUTS = [("y_out", (P, MT, TOK)), ("kT_out", (P, HEADS, TOK)), ("vT_out", (P, HEADS, TOK)), ("hgrn_p_out", (HEADS, P, P)),
         ("hgrn_s_out", (DEC, HEADS, P, P)), ("ret_p_out", (HEADS, RK, RK)), ("ret_s_out", (DEC, HEADS, RK, RK)),
         ("conv_out", (2, P, FT, PAD + 2 * DEC))]


def _layout(inp):
    x = np.concatenate([inp["x_prompt"][0], inp["x_sample"][:, 0]], 0)
    a = {"x_in": x.T.reshape(MT, P, TOK).transpose(1, 0, 2)}
    a["vecs"] = np.concatenate(
        [_columns(inp[n][l]) for l in range(2) for n in ("norm_mix", "norm_ffn")]
        + [_columns(inp["norm_final"]), _columns(inp["gn_hgrn"]), _columns(inp["gn_ret"])]
        + [b for l in range(2) for b in (_columns(inp["conv_w"][l]), _columns(inp["conv_b"][l]))], 1)
    a["conv_state"] = inp["state_conv"].transpose(0, 3, 1, 2).reshape(2, FT, P, 2 * DEC).transpose(0, 2, 1, 3)
    w = inp["w_in_even"][0]
    A, B = 4 * HEADS * P, HEADS * P
    a["w_even_in"] = _tiles(np.concatenate([w[:, A:A + 3 * B], w[:, :A]], 1), 4)
    a["w_even_out"] = _tiles(inp["w_out_even"][0], 4)
    a["w_odd_in"] = _tiles(inp["w_in_odd"][0], 4).reshape(4, HEADS, 2, 2, P, 8 * P).transpose(1, 0, 2, 3, 4, 5).reshape(ZO, 2, P, 8 * P)
    a["w_odd_out"] = _tiles(inp["w_out_odd"][0], 4)
    for l in range(2):
        t = _tiles(inp["w_ffn_in"][l], 4)
        a[f"w_f{l}_in"] = t.reshape(2, FT, 2, P, 8 * P).transpose(1, 0, 2, 3, 4).reshape(2 * FT, 2, P, 8 * P)
        r = 0
        for n, c in enumerate(CHUNKS):
            a[f"w_f{l}_o{n}"] = _tiles(inp["w_ffn_out"][l][r * P:(r + c) * P], c // 4)
            r += c
    for n in ("cache_k", "cache_v"):
        a[n] = inp[n][0].reshape(-1, PAGE, HEADS * P)
    a["page_table"] = inp["page_table"].reshape(1, -1)
    a["state_hgrn"], a["state_ret"] = inp["state_hgrn"][0], inp["state_ret"][0]
    a.update(_constants())
    return {k: np.ascontiguousarray(v) for k, v in a.items()}


def kernel(**inputs):
    import concourse.bacc as bacc
    from concourse.bass_utils import run_bass_kernel_spmd as run
    inputs = {k: np.asarray(v) for k, v in inputs.items()}
    arrays = _layout(inputs)
    nc = bacc.Bacc("TRN2", target_bir_lowering=False, num_devices=1)
    aps = {k: nc.dram_tensor("in_" + k, a.shape, mybir.dt.from_np(a.dtype), kind="ExternalInput").ap() for k, a in arrays.items()}
    for k, shape in _OUTS:
        aps[k] = nc.dram_tensor("out_" + k, shape, F32, kind="ExternalOutput").ap()
    hybrid_step(nc, **aps)
    r = run(nc, [{"in_" + k: a for k, a in arrays.items()}], core_ids=[0]).results[0]
    o = {k: np.asarray(r["out_" + k]) for k, _ in _OUTS}

    def rows(t):
        return np.ascontiguousarray(t.transpose(2, 1, 0).reshape(TOK, -1))
    y, k, v = rows(o["y_out"]), rows(o["kT_out"]), rows(o["vT_out"])
    c = o["conv_out"].transpose(0, 3, 2, 1).reshape(2, PAD + 2 * DEC, D_FF)
    return (y[:SEQ][None], y[SEQ:][:, None],
            k[:SEQ].reshape(1, 1, SEQ, HEADS, P), v[:SEQ].reshape(1, 1, SEQ, HEADS, P),
            k[SEQ:].reshape(1, DEC, 1, HEADS, P), v[SEQ:].reshape(1, DEC, 1, HEADS, P),
            o["hgrn_p_out"][None, None], o["hgrn_s_out"][None], o["ret_p_out"][None, None], o["ret_s_out"][None],
            np.ascontiguousarray(c[:, None, :PAD]), np.ascontiguousarray(c[:, PAD:].reshape(2, DEC, 2, D_FF)))
```

```python
from contextlib import ExitStack

import numpy as np

import concourse.bass as bass
from concourse import mybir

F32 = mybir.dt.float32
F32R = mybir.dt.float32r
I32 = mybir.dt.int32
ALU = mybir.AluOpType
ACT = mybir.ActivationFunctionType
AX_X = mybir.AxisListType.X

P = 128
SEQ, DEC = 256, 8
TOK = SEQ + DEC
D_MODEL, D_FF = 2048, 5632
MT = D_MODEL // P
FT = D_FF // P
HEADS = 8
PAGES = 16
PAGE = 128
BLOCKS = 8
TOPK = 3
CHUNK = 64
NCH = SEQ // CHUNK
LEVELS = 6
EPS = 1e-6
RK = 256
SLOTS = 8
UNIT = 4 * P
BIG = 1e30
CHUNKS = (16, 16, 12)
PAD = 2
CONV_COLS = PAD + SEQ + 3 * DEC
CONV_OUT = CONV_COLS - 2

V_MIX0, V_FFN0, V_MIX1, V_FFN1, V_FINAL = (MT * n for n in range(5))
V_GNH = 5 * MT
V_GNR = V_GNH + HEADS
V_CONV = V_GNR + 2 * HEADS
V_ALL = V_CONV + 2 * 4 * FT

Z_QB, Z_KB, Z_VB, Z_QA, Z_FA, Z_IA, Z_GA = (HEADS * n for n in range(7))
ZE = 7 * HEADS
Z_Q, Z_K, Z_V, Z_G = range(0, 8, 2)
ZH = 8
ZO = ZH * HEADS


class Steps:

    def __init__(self, sem, names):
        self.sem, self.names, self.K = sem, list(names), len(names)
        self.index = {n: k + 1 for k, n in enumerate(self.names)}
        assert len(self.index) == self.K
        self.next = 0

    def start(self, engine):
        engine.sem_inc(self.sem, 1)

    def one(self, name):
        assert self.names[self.next % self.K] == name, (self.names[self.next % self.K], name)
        self.next += 1
        return 1

    def at(self, name, turn=0):
        return turn * self.K + (1 + self.index[name])

    def before(self, turn):
        return turn * self.K + 1


class Phase:

    def __init__(self, kind, weights, first, tiles, ktu, src, t0):
        self.kind, self.w, self.first, self.n, self.ktu, self.src, self.t0 = kind, weights, first, tiles, ktu, src, t0
        self.u0 = 4 * t0

    def end(self):
        return self.t0 + self.n


def hybrid_step(nc, x_in, vecs, conv_state, w_even_in, w_even_out, w_odd_in, w_odd_out, w_f0_in, w_f0_o0, w_f0_o1,
                w_f0_o2, w_f1_in, w_f1_o0, w_f1_o1, w_f1_o2, cache_k, cache_v, page_table, state_hgrn, state_ret,
                c_ident, c_eye8, c_eye4, c_pairs, c_eye, c_blk, c_causal, c_rope_b, c_perm, c_rope_c, c_decay, c_sdec, c_gamma,
                c_level, c_reset, y_out, kT_out, vT_out, hgrn_p_out, hgrn_s_out, ret_p_out, ret_s_out, conv_out):
    ctx = ExitStack()
    with ctx:
        def sb(name, shape, dt=F32, stack=ctx):
            return stack.enter_context(nc.sbuf_tensor(name, shape, dt))

        def sem(name):
            return ctx.enter_context(nc.semaphore(name))

        raw = sb("raw", [P, SLOTS, UNIT])
        with ExitStack() as part:
            whi = sb("whi", [P, SLOTS, UNIT], F32R, part)
            wlo = sb("wlo", [P, SLOTS, UNIT], F32R, part)
        with ExitStack() as part:
            vring = sb("vring", [P, 4, HEADS * P], F32, part)
            blk = sb("blk", [P, 2 * P], F32, part)
            om = sb("om", [8, HEADS * P], F32, part)
            QE = sb("QE", [P, LEVELS, SEQ], F32, part)
        with ExitStack() as part:
            qh = [sb(f"qh{j}", [P, TOK], F32, part) for j in range(2)]
            vh = [sb(f"vh{j}", [P, TOK], F32, part) for j in range(2)]
            sm = [sb(f"sm{j}", [P, 384], F32, part) for j in range(2)]
            mx2 = [sb(f"mx2{j}", [P, 2], F32, part) for j in range(2)]
            nmx = [sb(f"nmx{j}", [P, 2], F32, part) for j in range(2)]
            lsum = [sb(f"lsum{j}", [P, 2], F32, part) for j in range(2)]
            rl = [sb(f"rl{j}", [P, 2], F32, part) for j in range(2)]
            vtok = [sb(f"vtok{j}", [P, 2, P], F32, part) for j in range(2)]
            pT = [sb(f"pT{j}", [P, 384], F32, part) for j in range(2)]
        sb("ring_space", [P, 2 * SLOTS, UNIT])
        x = sb("x", [P, MT, TOK])
        hA = (sb("hA_hi", [P, MT, TOK], F32R), sb("hA_lo", [P, MT, TOK], F32R))
        vec = sb("vec", [P, V_ALL])
        rstd = sb("rstd", [P, TOK])
        acc = sb("acc", [P, TOK])
        sq = sb("sq", [P, TOK])
        var = sb("var", [P, TOK])
        root_tmp = sb("root_tmp", [P, TOK])
        ones = sb("ones", [P, P])
        ident = sb("ident", [P, P])

        with ExitStack() as part:
            def se(name, shape, dt=F32):
                return sb(name, shape, dt, part)
            ze = se("ze", [P, ZE, TOK])
            S = se("S", [P, DEC, PAGES, HEADS])
            cau = se("cau", [P, 384])
            ropeb = se("ropeb", [32, 2, TOK])
            perm = se("perm", [32, 32])
            eye8 = se("eye8", [8, 8])
            eye = se("eye", [P, 8, 8])
            rt = se("rt", [32, 2, TOK])
            pt = se("pt", [1, DEC * PAGES], I32)
            own = se("own", [P, DEC, HEADS])
            po = se("po", [P, DEC, HEADS])
            qk = se("qk", [P, HEADS, DEC])
            mxt = se("mxt", [P, DEC, HEADS])
            mxa = se("mxa", [P, DEC, HEADS])
            mx64 = se("mx64", [64, 1])
            dg = se("dg", [64, 64])
            oS = se("oS", [P, HEADS, DEC])
            oS2 = se("oS2", [P, HEADS, DEC])
            vs = se("vs", [P, HEADS, DEC])
            Pb = se("Pb", [P, PAGES * HEADS])
            Sb = se("Sb", [P, PAGES, HEADS])
            with ExitStack() as sub:
                kring = sb("kring", [P, 4, HEADS * P], F32, sub)
                qbc = sb("qbc", [P, HEADS * P], F32, sub)
                qt8 = sb("qt8", [8, HEADS * P], F32, sub)
                qm8 = sb("qm8", [8, HEADS * P], F32, sub)
            with ExitStack() as sub:
                G = sb("G", [P, DEC, BLOCKS, HEADS], F32, sub)
                cmp = sb("cmp", [P, DEC, BLOCKS, HEADS], F32, sub)
                rank = sb("rank", [P, DEC, BLOCKS, HEADS], F32, sub)
            with ExitStack() as sub:
                def sh(name, shape, dt=F32):
                    return sb(name, shape, dt, sub)
                levm = sh("levm", [P, LEVELS + 1, P])
                reset = sh("reset", [P, SEQ])
                t1 = sh("t1", [P, TOK])
                t2 = sh("t2", [P, TOK])
                lsg = sh("lsg", [P, TOK])
                ka = [sh(f"ka{n}", [P, TOK]) for n in range(2)]
                va = [sh(f"va{n}", [P, TOK]) for n in range(2)]
                sg = [sh(f"sg{n}", [P, TOK]) for n in range(2)]
                fg = [sh(f"fg{n}", [P, 8]) for n in range(2)]
                bcum = [sh(f"bcum{n}", [P, SEQ]) for n in range(2)]
                g1 = sh("g1", [P, TOK])
                g2 = sh("g2", [P, TOK])
                hvar = sh("hvar", [P, TOK])
                kd = [sh(f"kd{n}", [P, SEQ]) for n in range(2)]
                root_a = sh("root_a", [P, TOK])
                pr = sh("pr", [P, LEVELS + 1, P])
                Aatt = sh("Aatt", [P, 2, P])
                hv = sh("hv", [P, 2, P])
                hk = sh("hk", [P, 2, P])
                ebl = sh("ebl", [P, NCH])
                kv8 = sh("kv8", [8, 2 * P])
                qm = sh("qm", [P, 8, 8])
                so8 = sh("so8", [8, P])
        with ExitStack() as part:
            def sg_(name, shape, dt=F32):
                return sb(name, shape, dt, part)
            EL = sg_("EL", [P, LEVELS, SEQ])
            KE = sg_("KE", [P, LEVELS, SEQ])
            qdec = sg_("qdec", [P, SEQ])
            Sst = sg_("Sst", [P, NCH, P])
            S0 = sg_("S0", [P, DEC, P])
            vm8 = sg_("vm8", [8, 8, P])
            oT = sg_("oT", [P, TOK])
        with ExitStack() as part:
            def so(name, shape, dt=F32):
                return sb(name, shape, dt, part)
            zo = so("zo", [P, 2 * ZH, TOK])
            R0 = so("R0", [P, 2, DEC, RK])
            ropec = so("ropec", [P, 2, TOK])
            mixed = (so("mixed_hi", [P, MT, TOK], F32R), so("mixed_lo", [P, MT, TOK], F32R))
            dmat = so("dmat", [P, 384])
            sdec = so("sdec", [P, HEADS, 2])
            gam = so("gam", [P, HEADS])
            eye4 = so("eye4", [P, 8])
            pairs = so("pairs", [P, 2])
            reye = so("reye", [P, 8, 8])
            r1 = so("r1", [P, TOK])
            r2 = so("r2", [P, TOK])
            qr = so("qr", [P, 2, TOK])
            kr = so("kr", [P, 2, TOK])
            gate = so("gate", [P, 2, TOK])
            aT = so("aT", [P, 384])
            rv = so("rv", [P, 2, RK])
            rk_ = so("rk", [P, 2, RK])
            Sf = so("Sf", [P, 2, RK])
            rkv = so("rkv", [P, 2 * RK])
            rvm = so("rvm", [P, 2, RK])
            rqm = so("rqm", [P, 2, 8, 8])
            ro4 = so("ro4", [P, RK])
            roT = so("roT", [P, 2, TOK])
        with ExitStack() as part:
            def sf(name, shape, dt=F32):
                return sb(name, shape, dt, part)
            hB = (sf("hB_hi", [P, MT, TOK], F32R), sf("hB_lo", [P, MT, TOK], F32R))
            hid1 = (sf("hid1_hi", [P, MT, TOK], F32R), sf("hid1_lo", [P, MT, TOK], F32R))
            bt = sf("bt", [P, TOK])
            ug = sf("ug", [P, TOK])
            cst = sf("cst", [P, FT, 2 * DEC])
            cout = sf("cout", [P, FT, PAD + 2 * DEC])
            ab = sf("ab", [P, CONV_COLS])
            cv1 = sf("cv1", [P, CONV_OUT])
            cv2 = sf("cv2", [P, CONV_OUT])
            sil = sf("sil", [P, CONV_OUT])

        st = [ctx.enter_context(nc.psum_tensor(f"stream{n}", [P, 512], F32)) for n in range(2)]
        m = [ctx.enter_context(nc.psum_tensor(f"mix{n}", [P, 512], F32)) for n in range(6)]

        phases = []

        def add(kind, w, first, tiles, ktu, src):
            phases.append(Phase(kind, w, first, tiles, ktu, src, phases[-1].end() if phases else 0))
            return phases[-1]
        E_IN = add("z_even", w_even_in, 0, ZE, 4, hA)
        E_OUT = add("out_norm_hB", w_even_out, 0, MT, 4, hA)

        def ffn(w_in, w_o, last):
            a = [add("ffn_hid1", w_in, 0, 2 * CHUNKS[0], 4, hB),
                 add("ffn_hA", w_in, 2 * CHUNKS[0], 2 * CHUNKS[1], 4, hB),
                 add("out", w_o[0], 0, MT, 4, hid1),
                 add("ffn_hid1", w_in, 2 * (CHUNKS[0] + CHUNKS[1]), 2 * CHUNKS[2], 4, hB),
                 add("out", w_o[1], 0, MT, 4, hA),
                 add(last, w_o[2], 0, MT, 3, hid1)]
            layer = 0 if w_in is w_f0_in else 1
            for p, pair0 in zip((a[0], a[1], a[3]), (0, CHUNKS[0], CHUNKS[0] + CHUNKS[1])):
                p.pair0, p.layer = pair0, layer
            for p, need in zip((a[2], a[4], a[5]), (CHUNKS[0], CHUNKS[0] + CHUNKS[1], FT)):
                p.need = need + FT * layer
            return a
        F0 = ffn(w_f0_in, (w_f0_o0, w_f0_o1, w_f0_o2), "out_norm_hA")
        O_IN = add("z_odd", w_odd_in, 0, ZO, 4, hA)
        O_OUT = add("out_norm_hB", w_odd_out, 0, MT, 4, mixed)
        F1 = ffn(w_f1_in, (w_f1_o0, w_f1_o1, w_f1_o2), "out_final")
        E_OUT.norm, F0[-1].norm, O_OUT.norm, F1[-1].norm = (1, V_FFN0), (2, V_MIX1), (3, V_FFN1), (4, V_FINAL)

        x_landed, vec_landed = [sem(f"x_landed{c}") for c in range(4)], sem("vec_landed")
        first_hi, first_lo, first_squares = sem("first_hi"), sem("first_lo"), sem("first_squares")
        const_landed = sem("const_landed")
        raw_landed = [sem(f"raw_landed{n}") for n in range(SLOTS // 2)]
        hi_done, lo_done, unit_used, tile_free = sem("hi_done"), sem("lo_done"), sem("unit_used"), sem("tile_free")
        consts_set = sem("consts_set")
        acc_cleared, norm_summed = sem("acc_cleared"), sem("norm_summed")
        NV = Steps(sem("norm_vector"), ["lo", "sum"])
        NA = Steps(sem("norm_scalar"), ["square", "hi"])
        IV = Steps(sem("root_vector"), ["var", "n1", "n2", "rstd"])
        IA = Steps(sem("root_scalar"), ["ln", "rough"])
        FV = Steps(sem("ffn_vector"), ["a_prompt", "c1", "c2", "c3", "u_prompt", "u_sample", "hid_lo"])
        FA = Steps(sem("ffn_scalar"), ["history", "new_p", "new_s", "silu", "hid_hi"])
        y_ready, y_stored = sem("y_ready"), sem("y_stored")
        ab_cleared = sem("ab_cleared")
        cst_landed, cout_stored = sem("cst_landed"), sem("cout_stored")
        RP = sem("rope_swapped")
        RV = Steps(sem("rope_vector"), ["cos", "sin", "add"])
        q8_turned, q8_saved, q_picked, q_spread, q_copied = sem("q8_turned"), sem("q8_saved"), sem("q_picked"), sem("q_spread"), sem("q_copied")
        pt_landed = sem("pt_landed")
        k_landed = [sem(f"k_landed{n}") for n in range(4)]
        k_used, s_saved = sem("k_used"), sem("s_saved")
        kv_stored = sem("kv_stored")
        def both(*names):
            return [f"{n}_{j}" for n in names for j in range(2)]
        BV = Steps(sem("attn_vector"), both("masked", "max0", "max1", "negmax", "recip", "p0", "p1", "o_lo"))
        BA = Steps(sem("attn_scalar"), both("q", "v", "v_rows", "exp0", "exp1", "pT", "o_hi"))
        BP = Steps(sem("attn_tensor"), both("scores", "v_turned", "p_turned", "o"))
        GV = Steps(sem("hgrn_gates_vector"),
                   ["ls", "mxf", "g1", "sg", "i1", "ir", "va", "cum", "dk"] + [f"d{l}{s}" for l in range(LEVELS) for s in "lr"] + ["kd"])
        GA = Steps(sem("hgrn_gates_scalar"), ["abs", "exp", "ln", "ka", "fg", "eg", "ei", "dke", "levels"])
        HV = Steps(sem("hgrn_vector"),
                   ["qe", "ke", "qdec", "vm", "qm", "pr0a", "pr0b", "att0", "pr1a", "pr1b", "att1", "s1", "s2", "s3", "s4"] + [f"sn{b}" for b in range(DEC)] + ["var", "n1", "n2", "rstd", "og", "gated", "o_lo"])
        HA = Steps(sem("hgrn_scalar"),
                   ["v_rows", "k_rows", "kv8", "ebl", "eb", "so8", "o_p", "o_s", "square", "lnv", "rough", "o_hi"])
        HP = Steps(sem("hgrn_tensor"),
                   ["v_turned", "k_turned", "t8", "lev0", "lev1", "U", "kv_a", "kv_b", "o", "so", "so_turned", "ssum"])
        h_s0_landed, h_stored = sem("h_s0_landed"), sem("h_stored")
        SVn = (["qk", "vs", "clear_cmp", "rank0"] + [f"{w}{i}" for i in range(BLOCKS) for w in (("gt", "ge", "add") if 0 < i < BLOCKS - 1 else (("ge", "add") if i == 0 else ("gt", "add")))]
               + ["keep", "minus", "bias", "tmax", "rmax", "diag", "mxa", "shift", "oshift", "tsum", "den", "rden", "p", "po"])
        SV = Steps(sem("sel_vector"), SVn)
        SA = Steps(sem("sel_scalar"), ["own", "G", "exp", "oexp"])
        SP_ = Steps(sem("sel_tensor"), ["own", "gates", "mxT", "mxb", "den"])
        v_landed = [sem(f"v_landed{n}") for n in range(4)]
        v_used, v_saved = sem("v_used"), sem("v_saved")
        pb_ready, om_ready, o8_ready = sem("pb_ready"), sem("om_ready"), sem("o8_ready")
        TV = Steps(sem("tail_vector"), ["pv", "sum", "lo"])
        TA = Steps(sem("tail_scalar"), ["hi"])
        QV = Steps(sem("ret_vector"),
                   [f"{w}{s}" for w in "qk" for s in ("a", "b", "x1", "c", "d", "x2")]
                   + ["att", "k0", "k1", "qm", "vm", "s0_0", "s0_1", "s0_2", "s0_3", "s1_0", "s1_1", "s1_2", "s1_3",
                      "mean", "oc", "var", "n1", "n2", "rstd", "og", "gated", "o_lo"])
        QA = Steps(sem("ret_scalar"), ["silu", "v_rows", "kv0", "kv1", "kv2", "kv3", "o_p", "sfin", "ro0", "ro1", "ro2", "ro3", "o_s", "square", "lnv", "rough", "o_hi"])
        QP = Steps(sem("ret_tensor"), ["v_turned", "att", "k_turned", "t8", "o", "sfin", "kv0_0", "kv0_1", "kv0_2", "kv0_3",
                                       "kv1_0", "kv1_1", "kv1_2", "kv1_3", "so", "so_turned", "ssum", "vsum"])
        r_s0_landed, r_s0_stored, r_sf_stored, dm_landed = sem("r_s0_landed"), sem("r_s0_stored"), sem("r_sf_stored"), sem("dm_landed")
        ret_cleared = sem("ret_cleared")
        XV, NFA = Steps(sem("final_sum"), ["sum"]), sem("final_square")
        consts = [(ident[:, :], c_ident), (eye8[:, :], c_eye8), (eye[:, :, :], c_eye), (cau[:, :], c_causal),
                  (ropeb[:, :, :], c_rope_b), (perm[:, :], c_perm)]
        N_CONST = len(consts)
        oc_landed = sem("odd_const_landed")
        hc_landed = sem("hgrn_const_landed")

        def tile(buf, t, a=0, b=TOK):
            return buf[:, bass.ds(t, 1), a:b].rearrange("p o n -> p (o n)")

        def col(t):
            return vec[:, bass.ds(t, 1)]

        ab_s = ab[:, PAD + SEQ:CONV_COLS].rearrange("p (b c) -> p b c", c=3)
        block = ctx.enter_context(nc.Block())

        @block.sync
        def _(sp):
            sp.sem_inc(h_stored, 1)
            sp.dma_start(vec[:, :], vecs).then_inc(vec_landed, 16)
            for c in range(4):
                sp.dma_start(x[:, 4 * c:4 * c + 4, :], x_in[:, 4 * c:4 * c + 4, :]).then_inc(x_landed[c], 16)

            def hgrn_states():
                sp.wait_ge(BV.sem, BV.before(HEADS // 2))
                sp.wait_ge(BP.sem, BP.before(HEADS // 2))
                sp.wait_ge(BA.sem, BA.before(HEADS // 2))
                sp.wait_ge(kv_stored, 32)
                sp.wait_ge(SV.sem, SV.at("vs"))
                with sp.Fori(0, HEADS) as h:
                    load = state_hgrn[bass.ds(h, 1), :, :, :].rearrange("o d b e -> d (o b) e")
                    sp.wait_ge(h_stored, 32 * h + 1)
                    sp.dma_start(S0[:, :, :], load).then_inc(h_s0_landed, 16)
                    sp.wait_ge(HV.sem, HV.at("s4", h))
                    sp.dma_start(hgrn_p_out[bass.ds(h, 1), :, :].rearrange("o d e -> d (o e)"), Sst[:, NCH - 1, :]).then_inc(h_stored, 16)
                    sp.wait_ge(HP.sem, HP.at("so", h))
                    sp.dma_start(hgrn_s_out[bass.ds(h, 1), :, :, :].rearrange("o d b e -> d (o b) e"), S0[:, :, :]).then_inc(h_stored, 16)

            def load_pair(p, i):
                for half in range(4):
                    n = p.ktu * P
                    row = i * 2 + (p.first + half // 2)
                    if not (isinstance(i, int) and p is phases[0] and i == 0):
                        row = row if isinstance(i, int) else sp.snap(row)
                        sp.wait_ge(lo_done, i * 8 + (p.u0 + 2 * half + 2 - SLOTS))
                    src = p.w[bass.ds(row, 1), half % 2, :, :].rearrange("o p (s n) -> p (o s) n", s=2)
                    sp.dma_start(raw[:, 2 * half:2 * half + 2, 0:n], src).then_inc(raw_landed[half], 16)

            for p in phases:
                peeled = p is E_IN or p is E_OUT
                if peeled:
                    load_pair(p, 0)
                if p is E_OUT:
                    hgrn_states()
                with sp.Fori(1 if peeled else 0, p.n // 2) as i:
                    load_pair(p, i)
            for c in range(4):
                sp.wait_ge(y_ready, 4 * c + 4)
                sp.dma_start(y_out[:, 4 * c:4 * c + 4, :], x[:, 4 * c:4 * c + 4, :]).then_inc(y_stored, 16)
            sp.wait_ge(y_stored, 64)

        @block.tensor
        def _(pe):
            mm, tr = nc.tensor.matmul, nc.tensor.transpose
            for steps in (BP, HP, SP_, QP):
                steps.start(pe)

            def stream_tile(p, i, j, last_k=None):
                bank = st[j][:, 0:TOK]
                if not (isinstance(i, int) and p.t0 + 2 * i + j < 2):
                    pe.wait_ge(tile_free, 2 * i + (p.t0 + j - 1))
                for k in range(4):
                    pe.wait_ge(lo_done, 8 * i + (p.u0 + 4 * j + k + 1))
                    for q in range(p.ktu):
                        kt, c = k * p.ktu + q, slice(q * P, (q + 1) * P)
                        hi, lo = whi[:, 4 * j + k, c], wlo[:, 4 * j + k, c]
                        first, last = kt == 0, kt == 4 * p.ktu - 1
                        if p is E_IN and isinstance(i, int) and i == 0 and j == 0:
                            pe.wait_ge(first_lo, kt + 1)
                        if last_k is not None and last:
                            pe.wait_ge(NV.sem, NV.at("lo", MT * last_k - 1))
                        mm(bank, hi, p.src[0][:, kt, :], start=first, stop=False)
                        mm(bank, hi, p.src[1][:, kt, :], start=False, stop=False)
                        ins = mm(bank, lo, p.src[0][:, kt, :], start=False, stop=last)
                    ins.then_inc(unit_used, 1)

            def stream(p, a, b):
                with pe.Fori(a, b) as i:
                    for j in range(2):
                        stream_tile(p, i, j)

            def norm_sum(n):
                if n < 4:
                    pe.wait_ge(NV.sem, NV.before(MT * n))
                    pe.wait_ge(NA.sem, NA.before(MT * n))
                else:
                    pe.wait_ge(XV.sem, XV.before(MT))
                mm(m[5][:, 0:TOK], ones[:, :], acc[:, :], start=True, stop=True).then_inc(norm_summed, 1)

            def stream_under_norm(p, n):
                pe.wait_ge(NV.sem, NV.before(MT * n - 1))
                pe.wait_ge(NA.sem, NA.before(MT * n - 1))
                stream_tile(p, 0, 0, last_k=n)
                norm_sum(n)
                stream_tile(p, 0, 1)
                stream(p, 1, p.n // 2)

            def rope(first, turn0):
                for half in range(2):
                    for t in range(4):
                        n = turn0 + 4 * half + t
                        if half:
                            pe.wait_ge(RV.sem, RV.at("sin", n - 4))
                        mm(m[t][0:32, 0:TOK], perm[:, :], ze[0:32, first + 4 * half + t, :], start=True, stop=True).then_inc(RP, 1)

            def attention_pair(i):
                banks = (m[0:4], m[4:6] + st)
                pe.wait_ge(BV.sem, BV.before(i))
                for j, (b0, b1, b2, b3) in enumerate(banks):
                    pe.wait_ge(BA.sem, BA.at(f"v_{j}", i))
                    mm(b0[:, 0:P], qh[j][:, 0:P], tile(ze, i * 2 + (j + Z_KB), 0, P), start=True, stop=False, skip_group_check=True)
                    mm(b0[:, P:384], qh[j][:, P:SEQ], tile(ze, i * 2 + (j + Z_KB), 0, SEQ), start=False, stop=True,
                       skip_group_check=True).then_inc(BP.sem, BP.one(f"scores_{j}"))
                for j, (b0, b1, b2, b3) in enumerate(banks):
                    tr(b1[:, 0:P], vh[j][:, 0:P], ident[:, :])
                    tr(b1[:, P:SEQ], vh[j][:, P:SEQ], ident[:, :]).then_inc(BP.sem, BP.one(f"v_turned_{j}"))
                for j, (b0, b1, b2, b3) in enumerate(banks):
                    pe.wait_ge(BV.sem, BV.at(f"p1_{j}", i))
                    for k in range(3):
                        ins = tr(b2[:, k * P:(k + 1) * P], sm[j][:, k * P:(k + 1) * P], ident[:, :])
                    ins.then_inc(BP.sem, BP.one(f"p_turned_{j}"))
                for j, (b0, b1, b2, b3) in enumerate(banks):
                    pe.wait_ge(BA.sem, BA.at(f"pT_{j}", i))
                    mm(b3[:, 0:SEQ], vtok[j][:, 0, :], pT[j][:, 0:SEQ], start=True, stop=False, skip_group_check=True)
                    mm(b3[:, P:SEQ], vtok[j][:, 1, :], pT[j][:, SEQ:384], start=False, stop=True,
                       skip_group_check=True).then_inc(BP.sem, BP.one(f"o_{j}"))

            def value_pages(b, first, last):
                if first == 0:
                    pe.wait_ge(pb_ready, b + 1)
                for g in range(first, last):
                    pe.wait_ge(v_landed[g % 4], 64 * b + 16 * (g // 4 + 1))
                    for j in range(4):
                        ins = mm(st[0][32 * j:32 * j + 8, 0:2 * P], Pb[:, g * HEADS:(g + 1) * HEADS], vring[:, g % 4, j * 2 * P:(j + 1) * 2 * P],
                                 start=(g == 0), stop=(g == PAGES - 1), tile_position=(0, 32 * j))
                    ins.then_inc(v_used, 1)

            def value_columns(b):
                pe.wait_ge(om_ready, 4 * b + 4)
                for h in range(HEADS):
                    ins = mm(st[1][:, h:h + 1], om[:, h * P:(h + 1) * P], ones[0:8, 0:1], start=(h == 0), stop=(h == HEADS - 1),
                             skip_group_check=True)
                ins.then_inc(o8_ready, 1)

            def hgrn_head(h, par):
                value_pages(h, 0, 3)
                pe.wait_ge(HV.sem, HV.before(h))
                pe.wait_ge(GA.sem, GA.before(h + 1))
                for c in range(2):
                    ins = tr(m[2][:, c * P:(c + 1) * P], va[par][:, c * P:(c + 1) * P], ident[:, :])
                ins.then_inc(HP.sem, HP.one("v_turned"))
                pe.wait_ge(GV.sem, GV.before(h + 1))
                for c in range(2):
                    ins = tr(m[2][:, (2 + c) * P:(3 + c) * P], kd[par][:, c * P:(c + 1) * P], ident[:, :])
                ins.then_inc(HP.sem, HP.one("k_turned"))
                tr(m[5][0:8, 0:P], ka[par][:, SEQ:TOK], ident[:, :])
                tr(m[5][0:8, P:2 * P], va[par][:, SEQ:TOK], ident[:, :]).then_inc(HP.sem, HP.one("t8"))
                value_pages(h, 3, 5)
                pe.wait_ge(HV.sem, HV.at("ke", h))
                for c, banks in enumerate(((0, 1), (3, 4))):
                    for l in range(LEVELS + 1):
                        s = slice(c * P, (c + 1) * P)
                        k_, q_ = (KE[:, l, s], QE[:, l, s]) if l < LEVELS else (ka[par][:, s], tile(ze, h + Z_QA, c * P, (c + 1) * P))
                        ins = mm(m[banks[l // 4]][:, (l % 4) * P:(l % 4 + 1) * P], k_, q_, start=(l % 4 == 0),
                                 stop=(l in (3, LEVELS)), skip_group_check=True)
                    ins.then_inc(HP.sem, HP.one(f"lev{c}"))
                value_pages(h, 5, 9)
                pe.wait_ge(HA.sem, HA.at("k_rows", h))
                pe.wait_ge(HV.sem, HV.at("pr1b", h))
                for c in range(NCH):
                    r = slice((c % 2) * CHUNK, (c % 2 + 1) * CHUNK)
                    ins = mm(m[4 - c % 2][:, (c // 2) * P:(c // 2 + 1) * P], hk[r, c // 2, :], hv[r, c // 2, :], start=(c < 2),
                             stop=(c >= NCH - 2), skip_group_check=True)
                ins.then_inc(HP.sem, HP.one("U"))
                pe.wait_ge(HV.sem, HV.at("qm", h))
                for k, w in enumerate("ab"):
                    mm(m[1 + k][:, :], kv8[:, 0:P], vm8[:, 4 * k:4 * k + 4, :], start=True, stop=True)\
                        .then_inc(HP.sem, HP.one(f"kv_{w}"))
                value_pages(h, 9, 13)
                pe.wait_ge(HV.sem, HV.at("s4", h))
                for c in range(2):
                    mm(m[5][:, c * P:(c + 1) * P], hv[:, c, :], Aatt[:, c, :], start=(c == 0), stop=False, skip_group_check=True)
                for c in range(1, NCH):
                    ins = mm(m[5][:, c * CHUNK:(c + 1) * CHUNK], Sst[:, c - 1, :], qdec[:, c * CHUNK:(c + 1) * CHUNK],
                             start=False, stop=(c == NCH - 1), skip_group_check=True)
                ins.then_inc(HP.sem, HP.one("o"))
                value_pages(h, 13, 16)
                pe.wait_ge(HV.sem, HV.at(f"sn{DEC - 1}", h))
                for b in range(DEC):
                    ins = mm(m[3][0:8, 0:P], qm[:, b, :], S0[:, b, :], start=(b == 0), stop=(b == DEC - 1))
                ins.then_inc(HP.sem, HP.one("so"))
                pe.wait_ge(HA.sem, HA.at("so8", h))
                mm(m[4][:, 0:8], so8[:, :], ident[0:8, 0:8], start=True, stop=True).then_inc(HP.sem, HP.one("so_turned"))
                value_columns(h)
                pe.wait_ge(HA.sem, HA.at("square", h))
                mm(m[0][:, 0:TOK], ones[:, :], t1[:, :], start=True, stop=True).then_inc(HP.sem, HP.one("ssum"))
                pe.wait_ge(v_saved, h + 1)

            def retention_stage(h, par, stage):
                z = ZH * par
                if stage == 0:
                    pe.wait_ge(QV.sem, QV.before(h))
                    pe.wait_ge(tile_free, ZH * h + (O_IN.t0 + ZH))
                    for s in range(2):
                        for e in range(2):
                            ins = tr(m[1][:, s * RK + e * P:s * RK + (e + 1) * P], zo[:, z + Z_V + e, s * P:(s + 1) * P], ident[:, :])
                    ins.then_inc(QP.sem, QP.one("v_turned"))
                elif stage == 1:
                    pe.wait_ge(QV.sem, QV.at("kx2", h))
                    for d in range(2):
                        mm(m[0][:, 0:SEQ], kr[:, d, 0:P], qr[:, d, 0:SEQ], start=(d == 0), stop=False, skip_group_check=True)
                    for d in range(2):
                        ins = mm(m[0][:, SEQ:384], kr[:, d, P:SEQ], qr[:, d, P:SEQ], start=False, stop=(d == 1), skip_group_check=True)
                    ins.then_inc(QP.sem, QP.one("att"))
                    for s in range(2):
                        for e in range(2):
                            ins = tr(m[2][:, s * RK + e * P:s * RK + (e + 1) * P], kr[:, e, s * P:(s + 1) * P], ident[:, :])
                    ins.then_inc(QP.sem, QP.one("k_turned"))
                    for d in range(2):
                        tr(m[5][0:8, d * P:(d + 1) * P], kr[:, d, SEQ:TOK], ident[:, :])
                    for d in range(2):
                        ins = tr(m[5][0:8, RK + d * P:RK + (d + 1) * P], zo[:, z + Z_V + d, SEQ:TOK], ident[:, :])
                    ins.then_inc(QP.sem, QP.one("t8"))
                elif stage == 2:
                    pe.wait_ge(QV.sem, QV.at("att", h))
                    pe.wait_ge(QA.sem, QA.at("v_rows", h))
                    for e in range(2):
                        mm(m[3][:, e * SEQ:(e + 1) * SEQ], rv[:, 0, e * P:(e + 1) * P], aT[:, 0:SEQ], start=(e == 0),
                           stop=False, skip_group_check=True)
                        ins = mm(m[3][:, e * SEQ + P:(e + 1) * SEQ], rv[:, 1, e * P:(e + 1) * P], aT[:, SEQ:384], start=False,
                                 stop=(e == 1), skip_group_check=True)
                    ins.then_inc(QP.sem, QP.one("o"))
                    pe.wait_ge(QV.sem, QV.at("k1", h))
                    for d in range(2):
                        for s in range(2):
                            ins = mm(m[4][:, d * RK:(d + 1) * RK], rk_[:, s, d * P:(d + 1) * P], rv[:, s, :],
                                     start=(d == 0 and s == 0), stop=(d == 1 and s == 1), skip_group_check=True)
                    ins.then_inc(QP.sem, QP.one("sfin"))
                    pe.wait_ge(QV.sem, QV.at("vm", h))
                    sample_updates(0, (1, 2, 5, 0))
                elif stage == 3:
                    pe.wait_ge(QV.sem, QV.at("s0_3", h))
                    pe.wait_ge(QA.sem, QA.at("sfin", h))
                    sample_updates(1, (1, 2, 5, 4))
                    sample_out(0)
                elif stage == 4:
                    pe.wait_ge(QV.sem, QV.at("s1_3", h))
                    sample_out(1).then_inc(QP.sem, QP.one("so"))
                elif stage == 5:
                    pe.wait_ge(QA.sem, QA.at("ro3", h))
                    for e in range(2):
                        ins = mm(m[0][:, e * 8:(e + 1) * 8], ro4[:, e * P:(e + 1) * P], eye4[:, :], start=(e == 0), stop=(e == 1),
                                 skip_group_check=True)
                    ins.then_inc(QP.sem, QP.one("so_turned"))
                    pe.wait_ge(QA.sem, QA.at("o_s", h))
                    for e in range(2):
                        ins = mm(m[1][:, 0:TOK], ones[:, :], roT[:, e, :], start=(e == 0), stop=(e == 1))
                    ins.then_inc(QP.sem, QP.one("ssum"))
                elif stage == 6:
                    pe.wait_ge(QA.sem, QA.at("square", h))
                    for e in range(2):
                        ins = mm(m[2][:, 0:TOK], ones[:, :], kr[:, e, :], start=(e == 0), stop=(e == 1))
                    ins.then_inc(QP.sem, QP.one("vsum"))

            def sample_updates(d, banks):
                for q in range(4):
                    r = slice(32 * q, 32 * q + 8)
                    mm(m[banks[q]][:, :], rkv[r, d * P:(d + 1) * P], rvm[r, :, :], start=True, stop=True, tile_position=(32 * q, 0))\
                        .then_inc(QP.sem, QP.one(f"kv{d}_{q}"))

            def sample_out(d):
                for b in range(DEC):
                    c = 32 * (b % 4)
                    ins = mm(m[3][c:c + 8, 0:RK], rqm[:, d, b, :], R0[:, d, b, :], start=(b < 4 and d == 0),
                             stop=(b >= 4 and d == 1), tile_position=(0, c))
                return ins

            pe.wait_ge(consts_set, 1)
            pe.wait_ge(const_landed, 16 * N_CONST)
            for j in range(2):
                stream_tile(E_IN, 0, j)
                if j == 0:
                    pe.wait_ge(first_squares, 4)
                    for t in range(MT):
                        ins = mm(m[5][:, 0:TOK], ones[:, :], ze[:, t, :], start=(t == 0), stop=(t == MT - 1))
                    ins.then_inc(norm_summed, 1)
            stream(E_IN, 1, 4)
            pe.wait_ge(tile_free, HEADS)
            rope(Z_QB, 0)
            pe.wait_ge(RV.sem, RV.before(HEADS))
            for h in range(HEADS):
                ins = tr(m[4 + h // 4][0:8, (h % 4) * P:(h % 4 + 1) * P], ze[:, Z_QB + h, SEQ:TOK], ident[:, :])
            ins.then_inc(q8_turned, 1)

            def spread_query():
                for k in range(2):
                    ins = mm(m[4 + k][:, :], ones[0:8, :], qm8[:, k * 512:(k + 1) * 512], start=True, stop=True)
                ins.then_inc(q_spread, 1)
            pe.wait_ge(q_picked, 1)
            spread_query()
            for j in range(2):
                stream_tile(E_IN, 4, j)
            with pe.Fori(0, 7) as b:
                for c in range(3):
                    for j in range(2):
                        stream_tile(E_IN, b * 3 + (5 + c), j)
                    if c == 1:
                        pe.wait_ge(q_picked, b + 2)
                        pe.wait_ge(q_copied, b + 1)
                        spread_query()
            stream(E_IN, 26, 28)
            pe.wait_ge(tile_free, ZE)
            pe.wait_ge(q_copied, DEC)
            rope(Z_KB, HEADS)
            pe.wait_ge(RV.sem, RV.before(2 * HEADS))
            with pe.Fori(0, HEADS // 2) as i:
                attention_pair(i)
            pe.wait_ge(BV.sem, BV.before(HEADS // 2))
            pe.wait_ge(BA.sem, BA.before(HEADS // 2))
            pe.wait_ge(s_saved, DEC - 1 + PAGES // 4)
            pe.wait_ge(SV.sem, SV.at("qk"))
            mm(m[0][:, 0:64], ones[:, :], qk[:, :, :], start=True, stop=True).then_inc(SP_.sem, SP_.one("own"))
            Sv = S[:, :, :, :].rearrange("p b (j two) h -> p b j two h", two=2)
            for k in range(2):
                ins = mm(m[1][:, :], ones[:, :], Sv[:, :, :, k, :], start=(k == 0), stop=(k == 1))
            ins.then_inc(SP_.sem, SP_.one("gates"))
            pe.wait_ge(SV.sem, SV.at("tmax"))
            tr(m[2][0:64, 0:P], mxt[:, :, :].rearrange("p b h -> p (b h)"), ident[:, :]).then_inc(SP_.sem, SP_.one("mxT"))
            pe.wait_ge(SV.sem, SV.at("diag"))
            mm(m[3][:, 0:64], ones[0:64, :], dg[:, :], start=True, stop=True).then_inc(SP_.sem, SP_.one("mxb"))
            pe.wait_ge(SV.sem, SV.at("tsum"))
            mm(m[4][:, 0:64], ones[:, :], mxt[:, :, :], start=True, stop=True).then_inc(SP_.sem, SP_.one("den"))
            pe.wait_ge(SV.sem, SV.before(1))
            with pe.Fori(0, HEADS // 2 - 1) as i:
                for j in range(2):
                    hgrn_head(i * 2 + j, j)
            for j in range(2):
                hgrn_head(HEADS - 2 + j, j)
            pe.wait_ge(HV.sem, HV.before(HEADS))
            pe.wait_ge(HA.sem, HA.before(HEADS))
            pe.wait_ge(TV.sem, TV.before(1))
            pe.wait_ge(TA.sem, TA.before(1))
            stream(E_OUT, 0, MT // 2)
            for p in F0:
                if p.src is not hB:
                    pe.wait_ge(FV.sem, FV.before(p.need))
                if p is F0[0]:
                    stream_under_norm(p, 1)
                else:
                    stream(p, 0, p.n // 2)
            def project(h, s):
                stream_tile(O_IN, h * (ZH // 2) + s // 2, s % 2)
            pe.wait_ge(NV.sem, NV.before(MT * 2 - 1))
            pe.wait_ge(NA.sem, NA.before(MT * 2 - 1))
            stream_tile(O_IN, 0, 0, last_k=2)
            norm_sum(2)
            for s in range(1, ZH):
                project(0, s)
            pe.wait_ge(ret_cleared, 2)
            pe.wait_ge(oc_landed, 16 * 6)
            with pe.Fori(0, HEADS // 2 - 1) as i:
                for j in range(2):
                    for s in range(ZH):
                        project(i * 2 + (j + 1), s)
                        retention_stage(i * 2 + j, j, s)
            for s in range(ZH):
                project(HEADS - 1, s)
                retention_stage(HEADS - 2, 0, s)
            for s in range(ZH):
                retention_stage(HEADS - 1, 1, s)
            pe.wait_ge(QV.sem, QV.before(HEADS))
            pe.wait_ge(QA.sem, QA.before(HEADS))
            stream(O_OUT, 0, MT // 2)
            for p in F1:
                if p.src is not hB:
                    pe.wait_ge(FV.sem, FV.before(p.need))
                if p is F1[0]:
                    stream_under_norm(p, 3)
                else:
                    stream(p, 0, p.n // 2)
            norm_sum(4)

        @block.scalar
        def _(act):
            A = nc.scalar.activation
            for steps in (NA, FA, BA, GA, HA, SA, TA, QA, IA):
                steps.start(act)
            for dst, src in consts:
                act.dma_start(dst, src).then_inc(const_landed, 16)

            def hi_tile(p, i, j):
                for k in range(4):
                    if k % 2 == 0:
                        act.wait_ge(raw_landed[2 * j + k // 2], 16 * i + 16 * (p.u0 // 8 + 1))
                    if not (isinstance(i, int) and p.u0 + 8 * i == 0):
                        act.wait_ge(unit_used, 8 * i + (p.u0 + 4 * j + k + 1 - SLOTS))
                    n = p.ktu * P
                    A(whi[:, 4 * j + k, 0:n], raw[:, 4 * j + k, 0:n], ACT.Copy).then_inc(hi_done, 1)

            def norm_tile(n, t, g, dst):
                act.wait_ge(NV.sem, t * 2 + NV.before(MT * (n - 1)))
                A(sq[:, :], tile(x, t), ACT.Square).then_inc(NA.sem, NA.one("square"))
                A(tile(dst[0], t), tile(x, t), ACT.Copy, scale=col(t + g)).then_inc(NA.sem, NA.one("hi"))

            def rough_root(n):
                act.wait_ge(IV.sem, IV.at("var", n))
                A(sq[:, :], var[:, :], ACT.Ln).then_inc(IA.sem, IA.one("ln"))
                act.wait_ge(IA.sem, IA.at("ln", n))
                A(rstd[:, :], sq[:, :], ACT.Exp, scale=-0.5).then_inc(IA.sem, IA.one("rough"))

            def evac(p, i, j):
                t = 2 * i + j
                if p.kind.startswith("out_"):
                    n, g = p.norm
                    act.wait_ge(tile_free, t + (p.t0 + 1))
                    if p.kind == "out_final":
                        act.wait_ge(XV.sem, XV.before(t))
                        A(sq[:, :], tile(x, t), ACT.Square).then_inc(NFA, 1)
                    else:
                        norm_tile(n, t, g, hB if p.kind == "out_norm_hB" else hA)
                elif p.kind.startswith("ffn") and j == 0:
                    pair = i + p.pair0
                    act.wait_ge(FV.sem, FV.before(pair + FT * p.layer))
                    A(ab_s[:, :, 0:2], tile(cst, pair, 0, 2 * DEC).rearrange("p (b c) -> p b c", c=2), ACT.Copy)\
                        .then_inc(FA.sem, FA.one("history"))
                elif p.kind.startswith("ffn"):
                    pair = i + p.pair0
                    turn = pair + FT * p.layer
                    act.wait_ge(tile_free, 2 * i + (p.t0 + 1))
                    act.wait_ge(FA.sem, FA.at("history", turn))
                    A(tile(cout, pair, 0, PAD), ab[:, SEQ:SEQ + PAD], ACT.Copy).then_inc(FA.sem, FA.one("new_p"))
                    A(tile(cout, pair, PAD, PAD + 2 * DEC).rearrange("p (b c) -> p b c", c=2), ab_s[:, :, 1:3], ACT.Copy)\
                        .then_inc(FA.sem, FA.one("new_s"))
                    act.wait_ge(FV.sem, FV.at("c3", turn))
                    A(sil[:, :], cv1[:, :], ACT.Silu).then_inc(FA.sem, FA.one("silu"))
                    act.wait_ge(FV.sem, FV.at("u_sample", turn))
                    A(tile(hid1[0] if p.kind == "ffn_hid1" else hA[0], i), ug[:, :], ACT.Copy).then_inc(FA.sem, FA.one("hid_hi"))

            def body(p):
                with act.Fori(0, p.n // 2 - 1) as i:
                    for j in range(2):
                        hi_tile(p, i + 1, j)
                        evac(p, i, j)

            def turn_over(p, nxt):
                for j in range(2):
                    if nxt is not None:
                        hi_tile(nxt, 0, j)
                    evac(p, p.n // 2 - 1, j)

            def attention_pair(i):
                banks = (m[0:4], m[4:6] + st)
                act.wait_ge(BP.sem, BP.before(i))
                for w, buf, first in (("q", qh, Z_QB), ("v", vh, Z_VB)):
                    for j in range(2):
                        A(buf[j][:, :], tile(ze, i * 2 + (j + first)), ACT.Copy).then_inc(BA.sem, BA.one(f"{w}_{j}"))
                for j, (b0, b1, b2, b3) in enumerate(banks):
                    act.wait_ge(BP.sem, BP.at(f"v_turned_{j}", i))
                    A(vtok[j][:, :, :], b1[:, 0:SEQ].rearrange("p (s e) -> p s e", s=2), ACT.Copy).then_inc(BA.sem, BA.one(f"v_rows_{j}"))
                for k, (a, b) in enumerate(((0, P), (P, 384))):
                    for j in range(2):
                        act.wait_ge(BV.sem, BV.at(f"negmax_{j}", i))
                        A(sm[j][:, a:b], sm[j][:, a:b], ACT.Exp, bias=nmx[j][:, k:k + 1], scale=P ** -0.5, accum_out=lsum[j][:, k:k + 1])\
                            .then_inc(BA.sem, BA.one(f"exp{k}_{j}"))
                for j, (b0, b1, b2, b3) in enumerate(banks):
                    act.wait_ge(BP.sem, BP.at(f"p_turned_{j}", i))
                    A(pT[j][:, :], b2[:, 0:384], ACT.Copy).then_inc(BA.sem, BA.one(f"pT_{j}"))
                for j, (b0, b1, b2, b3) in enumerate(banks):
                    act.wait_ge(BP.sem, BP.at(f"o_{j}", i))
                    A(tile(hA[0], i * 2 + (j + HEADS), 0, SEQ), b3[:, 0:SEQ], ACT.Copy).then_inc(BA.sem, BA.one(f"o_hi_{j}"))

            def hgrn_gates(h, par, piece):
                f = tile(ze, h + Z_FA)
                if piece == 0:
                    act.wait_ge(GV.sem, GV.before(h))
                    A(g1[:, :], f, ACT.Abs).then_inc(GA.sem, GA.one("abs"))
                    act.wait_ge(GA.sem, GA.at("abs", h))
                    A(g2[:, :], g1[:, :], ACT.Exp, scale=-1.0).then_inc(GA.sem, GA.one("exp"))
                    act.wait_ge(GA.sem, GA.at("exp", h))
                    A(g1[:, :], g2[:, :], ACT.Ln, bias=1.0).then_inc(GA.sem, GA.one("ln"))
                elif piece == 1:
                    act.wait_ge(GV.sem, GV.at("mxf", h))
                    A(ka[par][:, :], g2[:, :], ACT.Exp, scale=-1.0).then_inc(GA.sem, GA.one("ka"))
                    A(fg[par][:, :], lsg[:, SEQ:TOK], ACT.Exp).then_inc(GA.sem, GA.one("fg"))
                    A(sg[par][:, :], tile(ze, h + Z_GA), ACT.Exp, scale=-1.0).then_inc(GA.sem, GA.one("eg"))
                    A(va[par][:, :], tile(ze, h + Z_IA), ACT.Exp, scale=-1.0).then_inc(GA.sem, GA.one("ei"))
                else:
                    act.wait_ge(GV.sem, GV.at("dk", h))
                    A(kd[par][:, :], kd[par][:, :], ACT.Exp).then_inc(GA.sem, GA.one("dke"))
                    act.wait_ge(GV.sem, GV.at(f"d{LEVELS - 1}r", h))
                    A(EL[:, :, :], EL[:, :, :], ACT.Exp).then_inc(GA.sem, GA.one("levels"))

            def take_weights(b):
                A(Pb[:, :], S[:, bass.ds(b, 1), :, :].rearrange("p o g h -> p (o g h)"), ACT.Copy).then_inc(pb_ready, 1)

            def hgrn_head(h, par, ahead=True):
                act.wait_ge(HV.sem, HV.before(h))
                act.wait_ge(HP.sem, HP.at("k_turned", h))
                A(hv[:, :, :], m[2][:, 0:SEQ].rearrange("p (s e) -> p s e", s=2), ACT.Copy).then_inc(HA.sem, HA.one("v_rows"))
                A(hk[:, :, :], m[2][:, SEQ:2 * SEQ].rearrange("p (s e) -> p s e", s=2), ACT.Copy).then_inc(HA.sem, HA.one("k_rows"))
                act.wait_ge(HP.sem, HP.at("t8", h))
                A(kv8[:, :], m[5][0:8, 0:2 * P], ACT.Copy).then_inc(HA.sem, HA.one("kv8"))
                bl = bcum[par][:, :].rearrange("p (c n) -> p c n", n=CHUNK)[:, :, CHUNK - 1]
                A(ebl[:, :], bl, ACT.Exp).then_inc(HA.sem, HA.one("ebl"))
                A(t1[:, 0:SEQ], bcum[par][:, :], ACT.Exp).then_inc(HA.sem, HA.one("eb"))
                if ahead:
                    hgrn_gates(h + 1, 1 - par, 0)
                    hgrn_gates(h + 1, 1 - par, 1)
                act.wait_ge(HP.sem, HP.at("so", h))
                A(so8[:, :], m[3][0:8, 0:P], ACT.Copy).then_inc(HA.sem, HA.one("so8"))
                A(oT[:, 0:SEQ], m[5][:, 0:SEQ], ACT.Copy).then_inc(HA.sem, HA.one("o_p"))
                act.wait_ge(HP.sem, HP.at("so_turned", h))
                A(oT[:, SEQ:TOK], m[4][:, 0:8], ACT.Copy).then_inc(HA.sem, HA.one("o_s"))
                act.wait_ge(HA.sem, HA.at("o_s", h))
                A(t1[:, :], oT[:, :], ACT.Square).then_inc(HA.sem, HA.one("square"))
                act.wait_ge(o8_ready, h + 1)
                A(oS[:, :, bass.ds(h, 1)].rearrange("p h o -> p (h o)"), st[1][:, 0:HEADS], ACT.Copy).then_inc(v_saved, 1)
                if ahead:
                    take_weights(h + 1)
                act.wait_ge(HV.sem, HV.at("var", h))
                A(t2[:, :], hvar[:, :], ACT.Ln).then_inc(HA.sem, HA.one("lnv"))
                act.wait_ge(HA.sem, HA.at("lnv", h))
                A(t1[:, :], t2[:, :], ACT.Exp, scale=-0.5).then_inc(HA.sem, HA.one("rough"))
                if ahead:
                    hgrn_gates(h + 1, 1 - par, 2)
                act.wait_ge(HV.sem, HV.at("gated", h))
                A(tile(hA[0], h), t2[:, :], ACT.Copy).then_inc(HA.sem, HA.one("o_hi"))

            def load_states(h):
                for d in range(2):
                    act.dma_start(R0[:, d, :, :], state_ret[bass.ds(h, 1), :, d, :, :].rearrange("o p b e -> p (o b) e"))\
                        .then_inc(r_s0_landed, 16)

            def load_decay(h):
                act.dma_start(dmat[:, :], c_decay[bass.ds(h, 1), :, :].rearrange("o p n -> p (o n)")).then_inc(dm_landed, 16)

            def retention_stage(h, par, stage, more=True):
                z = ZH * par
                if stage == 0:
                    act.wait_ge(QV.sem, QV.before(h))
                    act.wait_ge(QP.sem, QP.before(h))
                    act.wait_ge(tile_free, ZH * h + (O_IN.t0 + ZH))
                    A(gate[:, :, :], zo[:, z + Z_G:z + Z_G + 2, :], ACT.Silu).then_inc(QA.sem, QA.one("silu"))
                    act.wait_ge(QP.sem, QP.at("v_turned", h))
                    A(rv[:, :, :], m[1][:, :].rearrange("p (s e) -> p s e", s=2), ACT.Copy).then_inc(QA.sem, QA.one("v_rows"))
                elif stage == 1:
                    act.wait_ge(QP.sem, QP.at("t8", h))
                    for q in range(4):
                        A(rkv[32 * q:32 * q + 8, :], m[5][0:8, :], ACT.Copy).then_inc(QA.sem, QA.one(f"kv{q}"))
                elif stage == 2:
                    if more:
                        act.wait_ge(QV.sem, QV.at("att", h))
                        load_decay(h + 1)
                    act.wait_ge(QP.sem, QP.at("o", h))
                    A(roT[:, :, 0:SEQ], m[3][:, :].rearrange("p (e t) -> p e t", e=2), ACT.Copy).then_inc(QA.sem, QA.one("o_p"))
                    act.wait_ge(QP.sem, QP.at("sfin", h))
                    A(Sf[:, :, :], m[4][:, :].rearrange("p (d e) -> p d e", d=2), ACT.Copy).then_inc(QA.sem, QA.one("sfin"))
                elif stage == 3:
                    act.wait_ge(QA.sem, QA.at("sfin", h))
                    act.dma_start(ret_p_out[bass.ds(h, 1), :, :].rearrange("o (d p) e -> p (o d) e", p=P), Sf[:, :, :])\
                        .then_inc(r_sf_stored, 16)
                elif stage == 4:
                    act.wait_ge(QP.sem, QP.at("so", h))
                    for q in range(4):
                        A(ro4[32 * q:32 * q + 8, :], m[3][32 * q:32 * q + 8, 0:RK], ACT.Copy).then_inc(QA.sem, QA.one(f"ro{q}"))
                    for d in range(2):
                        act.dma_start(ret_s_out[bass.ds(h, 1), :, d, :, :].rearrange("o p b e -> p (o b) e"), R0[:, d, :, :])\
                            .then_inc(r_s0_stored, 16)
                elif stage == 5:
                    act.wait_ge(QP.sem, QP.at("so_turned", h))
                    A(roT[:, :, SEQ:TOK], m[0][:, 0:16].rearrange("p (e t) -> p e t", e=2), ACT.Copy).then_inc(QA.sem, QA.one("o_s"))
                    act.wait_ge(QV.sem, QV.at("oc", h))
                    A(kr[:, :, :], roT[:, :, :], ACT.Square).then_inc(QA.sem, QA.one("square"))
                elif stage == 6:
                    act.wait_ge(QV.sem, QV.at("var", h))
                    A(r1[:, :], r2[:, :], ACT.Ln).then_inc(QA.sem, QA.one("lnv"))
                    act.wait_ge(QA.sem, QA.at("lnv", h))
                    A(qr[:, 0, :], r1[:, :], ACT.Exp, scale=-0.5).then_inc(QA.sem, QA.one("rough"))
                    if more:
                        act.wait_ge(r_s0_stored, 32 * h + 32)
                        load_states(h + 1)
                elif stage == 7:
                    act.wait_ge(r_sf_stored, 16 * h + 16)
                    act.wait_ge(QV.sem, QV.at("gated", h))
                    A(mixed[0][:, bass.ds(h * 2, 2), :], qr[:, :, :], ACT.Copy).then_inc(QA.sem, QA.one("o_hi"))

            act.wait_ge(vec_landed, 16)
            for c in range(4):
                act.wait_ge(x_landed[c], 16)
                for t in range(4 * c, 4 * c + 4):
                    A(hA[0][:, t, :], x[:, t, :], ACT.Copy, scale=vec[:, V_MIX0 + t:V_MIX0 + t + 1]).then_inc(first_hi, 1)
                if c == 0:
                    hi_tile(E_IN, 0, 0)
            for c in range(4):
                A(ze[:, 4 * c:4 * c + 4, :], x[:, 4 * c:4 * c + 4, :], ACT.Square).then_inc(first_squares, 1)
            hi_tile(E_IN, 0, 1)
            rough_root(0)
            act.wait_ge(const_landed, 16 * N_CONST)

            def pick_query(b):
                act.wait_ge(q_spread, b)
                A(qm8[:, :], qt8[:, :], ACT.Copy, scale=eye8[:, bass.ds(b, 1)]).then_inc(q_picked, 1)

            def copy_query(b):
                act.wait_ge(q_spread, b + 1)
                act.wait_ge(k_used, PAGES * b)
                for k in range(2):
                    ins = A(qbc[:, k * 512:(k + 1) * 512], m[4 + k][:, :], ACT.Copy)
                ins.then_inc(q_copied, 1)
            for i in range(1, 5):
                for j in range(2):
                    hi_tile(E_IN, i, j)
            act.wait_ge(q8_turned, 1)
            for k in range(2):
                ins = A(qt8[:, k * 512:(k + 1) * 512], m[4 + k][0:8, :], ACT.Copy)
            ins.then_inc(q8_saved, 1)
            act.wait_ge(q8_saved, 1)
            pick_query(0)
            copy_query(0)
            with act.Fori(0, 7) as b:
                pick_query(b + 1)
                for c in range(3):
                    for j in range(2):
                        hi_tile(E_IN, b * 3 + (5 + c), j)
                copy_query(b + 1)
            for i in (26, 27):
                for j in range(2):
                    hi_tile(E_IN, i, j)
            act.wait_ge(RV.sem, RV.before(2 * HEADS))
            act.wait_ge(unit_used, 4 * ZE)
            with act.Fori(0, HEADS // 2) as i:
                attention_pair(i)
            act.wait_ge(SV.sem, SV.at("vs"))
            act.wait_ge(SP_.sem, SP_.at("own"))
            A(own[:, :, :], m[0][:, 0:64].rearrange("p (h b) -> p b h", h=HEADS), ACT.Copy).then_inc(SA.sem, SA.one("own"))
            act.wait_ge(SP_.sem, SP_.at("gates"))
            A(G[:, :, :, :].rearrange("p b j h -> p (b j h)"), m[1][:, :], ACT.Copy).then_inc(SA.sem, SA.one("G"))
            act.wait_ge(SV.sem, SV.at("oshift"))
            A(S[:, :, :, :], S[:, :, :, :], ACT.Exp, scale=P ** -0.5).then_inc(SA.sem, SA.one("exp"))
            A(po[:, :, :], po[:, :, :], ACT.Exp, scale=P ** -0.5).then_inc(SA.sem, SA.one("oexp"))
            act.wait_ge(SV.sem, SV.before(1))
            take_weights(0)
            for piece in range(3):
                hgrn_gates(0, 0, piece)
            with act.Fori(0, HEADS // 2 - 1) as i:
                for j in range(2):
                    hgrn_head(i * 2 + j, j)
            for j in range(2):
                hgrn_head(HEADS - 2 + j, j, ahead=(j == 0))
            act.wait_ge(HV.sem, HV.before(HEADS))
            act.wait_ge(h_stored, 32 * HEADS + 1)
            act.wait_ge(TV.sem, TV.at("sum"))
            A(hA[0][:, HEADS:MT, SEQ:TOK], oS2[:, :, :], ACT.Copy).then_inc(TA.sem, TA.one("hi"))
            act.wait_ge(kv_stored, 32)
            for j in range(2):
                hi_tile(E_OUT, 0, j)
            body(E_OUT)
            turn_over(E_OUT, F0[0])
            rough_root(1)
            for a, b in zip(F0, F0[1:] + [O_IN]):
                if a is F0[0]:
                    act.wait_ge(cst_landed, 16)
                body(a)
                turn_over(a, b)
            rough_root(2)
            act.wait_ge(cout_stored, 16)
            load_states(0)
            load_decay(0)

            def project(h, s):
                if isinstance(h, int) and h == HEADS - 1 and s >= ZH - 2:
                    hi_tile(O_OUT, 0, s % 2)
                else:
                    hi_tile(O_IN, h * (ZH // 2) + (s // 2 + 1), s % 2)
            for s in range(ZH):
                project(0, s)
            act.wait_ge(ret_cleared, 2)
            with act.Fori(0, HEADS // 2 - 1) as i:
                for j in range(2):
                    for s in range(ZH):
                        project(i * 2 + (j + 1), s)
                        retention_stage(i * 2 + j, j, s)
            for s in range(ZH):
                project(HEADS - 1, s)
                retention_stage(HEADS - 2, 0, s)
            for s in range(ZH):
                retention_stage(HEADS - 1, 1, s, more=False)
            act.wait_ge(QV.sem, QV.before(HEADS))
            act.wait_ge(r_s0_stored, 32 * HEADS)
            act.wait_ge(r_sf_stored, 16 * HEADS)
            body(O_OUT)
            turn_over(O_OUT, F1[0])
            rough_root(3)
            for a, b in zip(F1, F1[1:] + [None]):
                if a is F1[0]:
                    act.wait_ge(cst_landed, 32)
                body(a)
                turn_over(a, b)
            rough_root(4)

        @block.vector
        def _(dve):
            v = nc.vector
            for steps in (NV, FV, RV, BV, GV, HV, SV, TV, QV, IV, XV):
                steps.start(dve)

            def lo_tile(p, i, j):
                for k in range(4):
                    dve.wait_ge(hi_done, 8 * i + (p.u0 + 4 * j + k + 1))
                    n = p.ktu * P
                    v.tensor_tensor(wlo[:, 4 * j + k, 0:n], raw[:, 4 * j + k, 0:n], whi[:, 4 * j + k, 0:n].bitcast(F32),
                                    ALU.subtract).then_inc(lo_done, 1)

            def clear_sum(n):
                dve.wait_ge(norm_summed, n)
                v.memset(acc[:, :], 0.0).then_inc(acc_cleared, 1)

            def norm_tile(n, t, g, dst):
                dve.wait_ge(NA.sem, t * 2 + NA.at("hi", MT * (n - 1)))
                v.scalar_tensor_tensor(out=tile(dst[1], t), in0=tile(x, t), scalar=col(t + g),
                                       in1=tile(dst[0], t).bitcast(F32), op0=ALU.mult, op1=ALU.subtract)\
                    .then_inc(NV.sem, NV.one("lo"))
                dve.wait_ge(NA.sem, t * 2 + NA.at("square", MT * (n - 1)))
                dve.wait_ge(NV.sem, t * 2 + NV.at("lo", MT * (n - 1)))
                v.tensor_tensor(acc[:, :], acc[:, :], sq[:, :], ALU.add).then_inc(NV.sem, NV.one("sum"))

            def norm_factor(n):
                dve.wait_ge(norm_summed, n + 1)
                v.tensor_scalar(var[:, :], m[5][:, 0:TOK], 1.0 / D_MODEL, EPS, ALU.mult, ALU.add).then_inc(IV.sem, IV.one("var"))

            def refine(root, square, a, b, count, steps, turn):
                v.scalar_tensor_tensor(out=a, in0=square, scalar=-0.5, in1=root, op0=ALU.mult, op1=ALU.mult)\
                    .then_inc(count.sem, count.one(steps[0]))
                dve.wait_ge(count.sem, count.at(steps[0], turn))
                v.tensor_tensor(b, a, root, ALU.mult).then_inc(count.sem, count.one(steps[1]))
                dve.wait_ge(count.sem, count.at(steps[1], turn))
                v.scalar_tensor_tensor(out=root, in0=b, scalar=1.5, in1=root, op0=ALU.add, op1=ALU.mult)\
                    .then_inc(count.sem, count.one(steps[2]))

            def norm_root(n):
                dve.wait_ge(IA.sem, IA.at("rough", n))
                refine(rstd[:, :], var[:, :], sq[:, :], root_tmp[:, :], IV, ("n1", "n2", "rstd"), n)
                dve.wait_ge(IV.sem, IV.at("rstd", n))

            def evac(p, i, j):
                t = 2 * i + j
                if not p.kind.startswith("ffn") or j == 0:
                    dve.wait_ge(unit_used, 4 * t + (p.u0 + 4))
                bank = st[j]
                if p.kind.startswith("z_"):
                    v.tensor_tensor(tile(ze if p.kind == "z_even" else zo, t), bank[:, 0:TOK], rstd[:, :], ALU.mult)\
                        .then_inc(tile_free, 1)
                elif p.kind.startswith("out"):
                    v.tensor_tensor(tile(x, t), bank[:, 0:TOK], tile(x, t), ALU.add).then_inc(tile_free, 1)
                    if p.kind == "out_final":
                        dve.wait_ge(NFA, t + 1)
                        dve.wait_ge(XV.sem, XV.before(t))
                        v.tensor_tensor(acc[:, :], acc[:, :], sq[:, :], ALU.add).then_inc(XV.sem, XV.one("sum"))
                    elif p.kind != "out":
                        n, g = p.norm
                        dve.wait_ge(tile_free, t + (p.t0 + 1))
                        norm_tile(n, t, g, hB if p.kind == "out_norm_hB" else hA)
                elif j == 0:
                    pair = i + p.pair0
                    turn = pair + FT * p.layer
                    w = V_CONV + 4 * FT * p.layer
                    dve.wait_ge(FA.sem, FA.before(turn))
                    v.tensor_tensor(ab[:, PAD:PAD + SEQ], bank[:, 0:SEQ], rstd[:, 0:SEQ], ALU.mult)\
                        .then_inc(FV.sem, FV.one("a_prompt"))
                    v.tensor_tensor(ab_s[:, :, 2], bank[:, SEQ:TOK], rstd[:, SEQ:TOK], ALU.mult).then_inc(tile_free, 1)
                    dve.wait_ge(FA.sem, FA.at("history", turn))
                    dve.wait_ge(tile_free, 2 * i + (p.t0 + 1))
                    v.tensor_scalar(cv1[:, :], ab[:, 0:CONV_OUT], col(pair + w), col(pair + (w + 3 * FT)), ALU.mult, ALU.add)\
                        .then_inc(FV.sem, FV.one("c1"))
                    dve.wait_ge(FV.sem, FV.at("c1", turn))
                    v.scalar_tensor_tensor(out=cv2[:, :], in0=ab[:, 1:1 + CONV_OUT], scalar=col(pair + (w + FT)), in1=cv1[:, :],
                                           op0=ALU.mult, op1=ALU.add).then_inc(FV.sem, FV.one("c2"))
                    dve.wait_ge(FV.sem, FV.at("c2", turn))
                    v.scalar_tensor_tensor(out=cv1[:, :], in0=ab[:, 2:2 + CONV_OUT], scalar=col(pair + (w + 2 * FT)), in1=cv2[:, :],
                                           op0=ALU.mult, op1=ALU.add).then_inc(FV.sem, FV.one("c3"))
                else:
                    pair = i + p.pair0
                    turn = pair + FT * p.layer
                    dve.wait_ge(unit_used, 4 * t + (p.u0 + 4))
                    v.tensor_tensor(bt[:, :], bank[:, 0:TOK], rstd[:, :], ALU.mult).then_inc(tile_free, 1)
                    dve.wait_ge(FA.sem, FA.at("silu", turn))
                    dve.wait_ge(tile_free, 2 * i + (p.t0 + 2))
                    v.tensor_tensor(ug[:, 0:SEQ], sil[:, 0:SEQ], bt[:, 0:SEQ], ALU.mult).then_inc(FV.sem, FV.one("u_prompt"))
                    v.tensor_tensor(ug[:, SEQ:TOK], sil[:, PAD + SEQ:CONV_OUT:3], bt[:, SEQ:TOK], ALU.mult)\
                        .then_inc(FV.sem, FV.one("u_sample"))
                    dst = hid1 if p.kind == "ffn_hid1" else hA
                    dve.wait_ge(FA.sem, FA.at("hid_hi", turn))
                    v.tensor_tensor(tile(dst[1], i), ug[:, :], tile(dst[0], i).bitcast(F32), ALU.subtract)\
                        .then_inc(FV.sem, FV.one("hid_lo"))

            def start_phase(p):
                if p.kind == "out" or p.kind.startswith("out_"):
                    dve.wait_ge(tile_free, p.t0)
                if p.kind.startswith("out_"):
                    clear_sum(p.norm[0])
                    dve.wait_ge(acc_cleared, p.norm[0])

            def body(p):
                with dve.Fori(0, p.n // 2 - 1) as i:
                    for j in range(2):
                        lo_tile(p, i + 1, j)
                        evac(p, i, j)

            def turn_over(p, nxt):
                for j in range(2):
                    if nxt is not None:
                        lo_tile(nxt, 0, j)
                    evac(p, p.n // 2 - 1, j)

            def rope(first, turn0):
                with dve.Fori(0, 2) as half:
                    for t in range(4):
                        n = half * 4 + (turn0 + t)
                        z_ = ze[0:32, bass.ds(half * 4 + (first + t), 1), :].rearrange("p o n -> p (o n)")
                        dve.wait_ge(RP, n + 1)
                        dve.wait_ge(RV.sem, RV.before(n))
                        v.tensor_tensor(rt[:, 0, :], z_, ropeb[:, 0, :], ALU.mult).then_inc(RV.sem, RV.one("cos"))
                        v.tensor_tensor(rt[:, 1, :], m[t][0:32, 0:TOK], ropeb[:, 1, :], ALU.mult).then_inc(RV.sem, RV.one("sin"))
                        dve.wait_ge(RV.sem, RV.at("sin", n))
                        v.tensor_tensor(z_, rt[:, 0, :], rt[:, 1, :], ALU.add).then_inc(RV.sem, RV.one("add"))

            def score_page(b, g):
                dve.wait_ge(k_landed[g % 4], 64 * b + 16 * (g // 4 + 1))
                for h in range(HEADS):
                    kk = kring[:, g % 4, h * P:(h + 1) * P]
                    ins = v.tensor_tensor_reduce(kk, kk, qbc[:, h * P:(h + 1) * P], 1.0, 0.0, ALU.mult, ALU.add,
                                                 Sb[:, g, h:h + 1])
                ins.then_inc(k_used, 1)

            def save_scores(b):
                dve.wait_ge(k_used, PAGES * (b + 1))
                v.tensor_copy(S[:, bass.ds(b, 1), :, :].rearrange("p o g h -> p (o g h)"),
                              Sb[:, :, :].rearrange("p g h -> p (g h)")).then_inc(s_saved, 1)
                dve.wait_ge(s_saved, b + 1)

            def score_slot(i, c):
                dve.wait_ge(k_landed[c], 16 * i + (16 * (DEC - 1) * (PAGES // 4) + 16))
                for h in range(HEADS):
                    kk = kring[:, c, h * P:(h + 1) * P]
                    ins = v.tensor_tensor_reduce(kk, kk, qbc[:, h * P:(h + 1) * P], 1.0, 0.0, ALU.mult, ALU.add,
                                                 Sb[:, c, h:h + 1])
                ins.then_inc(k_used, 1)

            def attention_pair(i):
                banks = (m[0:4], m[4:6] + st)
                for j, (b0, b1, b2, b3) in enumerate(banks):
                    dve.wait_ge(BP.sem, BP.at(f"scores_{j}", i))
                    v.tensor_tensor(sm[j][:, :], b0[:, 0:384], cau[:, :], ALU.add).then_inc(BV.sem, BV.one(f"masked_{j}"))
                for k, (a, b) in enumerate(((0, P), (P, 384))):
                    for j in range(2):
                        dve.wait_ge(BV.sem, BV.at(f"masked_{j}", i))
                        v.tensor_reduce(mx2[j][:, k:k + 1], sm[j][:, a:b], AX_X, ALU.max).then_inc(BV.sem, BV.one(f"max{k}_{j}"))
                for j in range(2):
                    dve.wait_ge(BV.sem, BV.at(f"max1_{j}", i))
                    v.tensor_scalar(nmx[j][:, :], mx2[j][:, :], -(P ** -0.5), None, ALU.mult).then_inc(BV.sem, BV.one(f"negmax_{j}"))
                score_slot(i, 0)
                score_slot(i, 1)
                for j in range(2):
                    dve.wait_ge(BA.sem, BA.at(f"exp1_{j}", i))
                    v.reciprocal(rl[j][:, :], lsum[j][:, :]).then_inc(BV.sem, BV.one(f"recip_{j}"))
                for k, (a, b) in enumerate(((0, P), (P, 384))):
                    for j in range(2):
                        dve.wait_ge(BV.sem, BV.at(f"recip_{j}", i))
                        v.tensor_scalar(sm[j][:, a:b], sm[j][:, a:b], rl[j][:, k:k + 1], None, ALU.mult).then_inc(BV.sem, BV.one(f"p{k}_{j}"))
                score_slot(i, 2)
                score_slot(i, 3)
                dve.wait_ge(k_used, 4 * i + (PAGES * (DEC - 1) + 4))
                v.tensor_copy(S[:, DEC - 1, bass.ds(i * 4, 4), :], Sb[:, 0:4, :]).then_inc(s_saved, 1)
                dve.wait_ge(s_saved, i + DEC)
                for j, (b0, b1, b2, b3) in enumerate(banks):
                    dve.wait_ge(BA.sem, BA.at(f"o_hi_{j}", i))
                    v.tensor_tensor(tile(hA[1], i * 2 + (j + HEADS), 0, SEQ), b3[:, 0:SEQ], tile(hA[0], i * 2 + (j + HEADS), 0, SEQ).bitcast(F32),
                                    ALU.subtract).then_inc(BV.sem, BV.one(f"o_lo_{j}"))

            def hgrn_gates(h, par, piece):
                f = tile(ze, h + Z_FA)
                if piece == 0:
                    dve.wait_ge(GA.sem, GA.at("ln", h))
                    v.scalar_tensor_tensor(out=lsg[:, :], in0=f, scalar=0.0, in1=g1[:, :], op0=ALU.min, op1=ALU.subtract)\
                        .then_inc(GV.sem, GV.one("ls"))
                    v.scalar_tensor_tensor(out=g2[:, :], in0=f, scalar=0.0, in1=g1[:, :], op0=ALU.max, op1=ALU.add)\
                        .then_inc(GV.sem, GV.one("mxf"))
                elif piece == 1:
                    dve.wait_ge(GA.sem, GA.at("ei", h))
                    v.tensor_scalar(sg[par][:, :], sg[par][:, :], 1.0, None, ALU.add).then_inc(GV.sem, GV.one("g1"))
                    dve.wait_ge(GV.sem, GV.at("g1", h))
                    v.reciprocal(sg[par][:, :], sg[par][:, :]).then_inc(GV.sem, GV.one("sg"))
                    v.tensor_scalar(va[par][:, :], va[par][:, :], 1.0, None, ALU.add).then_inc(GV.sem, GV.one("i1"))
                    dve.wait_ge(GV.sem, GV.at("i1", h))
                    v.reciprocal(va[par][:, :], va[par][:, :]).then_inc(GV.sem, GV.one("ir"))
                    dve.wait_ge(GV.sem, GV.at("ir", h))
                    v.tensor_tensor(va[par][:, :], va[par][:, :], tile(ze, h + Z_IA), ALU.mult).then_inc(GV.sem, GV.one("va"))
                else:
                    v.tensor_tensor_scan(bcum[par][:, :], reset[:, :], lsg[:, 0:SEQ], 0.0, ALU.mult, ALU.add).then_inc(GV.sem, GV.one("cum"))
                    dve.wait_ge(GV.sem, GV.at("cum", h))
                    bc = bcum[par][:, :].rearrange("p (c n) -> p c n", n=CHUNK)
                    v.tensor_tensor(kd[par][:, :].rearrange("p (c n) -> p c n", n=CHUNK), bc[:, :, CHUNK - 1:CHUNK].to_broadcast([P, NCH, CHUNK]),
                                    bc, ALU.subtract).then_inc(GV.sem, GV.one("dk"))
                    for l in range(LEVELS):
                        B = 1 << l
                        bv = bcum[par][:, :].rearrange("p (n w) -> p n w", w=2 * B)
                        ev = EL[:, l, :].rearrange("p (n w) -> p n w", w=2 * B)
                        ref = bv[:, :, B - 1:B].to_broadcast([P, SEQ // (2 * B), B])
                        v.tensor_tensor(ev[:, :, 0:B], ref, bv[:, :, 0:B], ALU.subtract).then_inc(GV.sem, GV.one(f"d{l}l"))
                        v.tensor_tensor(ev[:, :, B:2 * B], bv[:, :, B:2 * B], ref, ALU.subtract).then_inc(GV.sem, GV.one(f"d{l}r"))
                    dve.wait_ge(GA.sem, GA.at("dke", h))
                    v.tensor_tensor(kd[par][:, :], kd[par][:, :], ka[par][:, 0:SEQ], ALU.mult).then_inc(GV.sem, GV.one("kd"))

            def hgrn_head(h, par, ahead=True):
                dve.wait_ge(GA.sem, GA.at("levels", h))
                q_ = ze[:, bass.ds(h + Z_QA, 1), 0:SEQ].to_broadcast([P, LEVELS, SEQ])
                v.tensor_tensor(QE[:, :, :], EL[:, :, :], q_, ALU.mult).then_inc(HV.sem, HV.one("qe"))
                v.tensor_tensor(KE[:, :, :], EL[:, :, :], ka[par][:, None, 0:SEQ].to_broadcast([P, LEVELS, SEQ]), ALU.mult)\
                    .then_inc(HV.sem, HV.one("ke"))
                dve.wait_ge(HA.sem, HA.at("eb", h))
                v.tensor_tensor(qdec[:, :], t1[:, 0:SEQ], tile(ze, h + Z_QA, 0, SEQ), ALU.mult).then_inc(HV.sem, HV.one("qdec"))
                v.tensor_tensor(vm8[:, :, :], kv8[:, None, P:2 * P].to_broadcast([8, 8, P]), eye8[:, :, None].to_broadcast([8, 8, P]),
                                ALU.mult).then_inc(HV.sem, HV.one("vm"))
                v.tensor_tensor(qm[:, :, :], ze[:, bass.ds(h + Z_QA, 1), SEQ:TOK].to_broadcast([P, 8, 8]), eye[:, :, :], ALU.mult)\
                    .then_inc(HV.sem, HV.one("qm"))
                if ahead:
                    hgrn_gates(h + 1, 1 - par, 0)
                for c, (b0, b1) in enumerate(((m[0], m[1]), (m[3], m[4]))):
                    dve.wait_ge(HP.sem, HP.at(f"lev{c}", h))
                    if c:
                        dve.wait_ge(HV.sem, HV.at("att0", h))
                    v.tensor_tensor(pr[:, 0:4, :], b0[:, :].rearrange("p (l t) -> p l t", l=4), levm[:, 0:4, :], ALU.mult)\
                        .then_inc(HV.sem, HV.one(f"pr{c}a"))
                    v.tensor_tensor(pr[:, 4:7, :], b1[:, 0:384].rearrange("p (l t) -> p l t", l=3), levm[:, 4:7, :], ALU.mult)\
                        .then_inc(HV.sem, HV.one(f"pr{c}b"))
                    dve.wait_ge(HV.sem, HV.at(f"pr{c}b", h))
                    v.tensor_reduce(Aatt[:, c, :], pr[:, :, :].rearrange("p l t -> p t l"), AX_X, ALU.add)\
                        .then_inc(HV.sem, HV.one(f"att{c}"))
                if ahead:
                    hgrn_gates(h + 1, 1 - par, 1)
                dve.wait_ge(HP.sem, HP.at("U", h))
                dve.wait_ge(h_s0_landed, 16 * h + 16)
                v.tensor_copy(Sst[:, 0, :], m[4][:, 0:P]).then_inc(HV.sem, HV.one("s1"))
                for c in range(1, NCH):
                    dve.wait_ge(HV.sem, HV.at(f"s{c}", h))
                    v.scalar_tensor_tensor(out=Sst[:, c, :], in0=Sst[:, c - 1, :], scalar=ebl[:, c:c + 1],
                                           in1=m[4 - c % 2][:, (c // 2) * P:(c // 2 + 1) * P], op0=ALU.mult, op1=ALU.add)\
                        .then_inc(HV.sem, HV.one(f"s{c + 1}"))
                for b in range(DEC):
                    if b % 4 == 0:
                        dve.wait_ge(HP.sem, HP.at("kv_a" if b == 0 else "kv_b", h))
                    v.scalar_tensor_tensor(out=S0[:, b, :], in0=S0[:, b, :], scalar=fg[par][:, b:b + 1],
                                           in1=m[1 + b // 4][:, (b % 4) * P:(b % 4 + 1) * P], op0=ALU.mult, op1=ALU.add)\
                        .then_inc(HV.sem, HV.one(f"sn{b}"))
                dve.wait_ge(v_used, PAGES * (h + 1))
                for j in range(4):
                    v.tensor_tensor(om[:, j * 2 * P:(j + 1) * 2 * P], st[0][32 * j:32 * j + 8, 0:2 * P], blk[32 * j:32 * j + 8, :], ALU.mult)\
                        .then_inc(om_ready, 1)
                dve.wait_ge(HP.sem, HP.at("ssum", h))
                v.tensor_scalar(hvar[:, :], m[0][:, 0:TOK], 1.0 / P, EPS, ALU.mult, ALU.add).then_inc(HV.sem, HV.one("var"))
                if ahead:
                    hgrn_gates(h + 1, 1 - par, 2)
                dve.wait_ge(HA.sem, HA.at("rough", h))
                refine(t1[:, :], hvar[:, :], t2[:, :], root_a[:, :], HV, ("n1", "n2", "rstd"), h)
                dve.wait_ge(HV.sem, HV.at("rstd", h))
                v.scalar_tensor_tensor(out=t1[:, :], in0=oT[:, :], scalar=col(h + V_GNH), in1=t1[:, :], op0=ALU.mult, op1=ALU.mult)\
                    .then_inc(HV.sem, HV.one("og"))
                dve.wait_ge(HV.sem, HV.at("og", h))
                v.tensor_tensor(t2[:, :], t1[:, :], sg[par][:, :], ALU.mult).then_inc(HV.sem, HV.one("gated"))
                dve.wait_ge(HA.sem, HA.at("o_hi", h))
                v.tensor_tensor(tile(hA[1], h), t2[:, :], tile(hA[0], h).bitcast(F32), ALU.subtract).then_inc(HV.sem, HV.one("o_lo"))

            def select_blocks():
                v.memset(cmp[:, :, :, :], 0.0).then_inc(SV.sem, SV.one("clear_cmp"))
                v.memset(rank[:, :, :, :], 0.0).then_inc(SV.sem, SV.one("rank0"))
                dve.wait_ge(SA.sem, SA.at("G"))
                last = "rank0"
                for i in range(BLOCKS):
                    dve.wait_ge(SV.sem, SV.at(last))
                    if i > 0:
                        v.tensor_tensor(cmp[:, :, 0:i, :], G[:, :, i:i + 1, :].to_broadcast([P, DEC, i, HEADS]), G[:, :, 0:i, :],
                                        ALU.is_gt).then_inc(SV.sem, SV.one(f"gt{i}"))
                        last = f"gt{i}"
                    if i < BLOCKS - 1:
                        n = BLOCKS - 1 - i
                        v.tensor_tensor(cmp[:, :, i + 1:BLOCKS, :], G[:, :, i:i + 1, :].to_broadcast([P, DEC, n, HEADS]),
                                        G[:, :, i + 1:BLOCKS, :], ALU.is_ge).then_inc(SV.sem, SV.one(f"ge{i}"))
                        last = f"ge{i}"
                    dve.wait_ge(SV.sem, SV.at(last))
                    if i > 0:
                        ins = v.tensor_tensor(rank[:, :, 0:i, :], rank[:, :, 0:i, :], cmp[:, :, 0:i, :], ALU.add)
                    if i < BLOCKS - 1:
                        ins = v.tensor_tensor(rank[:, :, i + 1:BLOCKS, :], rank[:, :, i + 1:BLOCKS, :], cmp[:, :, i + 1:BLOCKS, :], ALU.add)
                    ins.then_inc(SV.sem, SV.one(f"add{i}"))
                    last = f"add{i}"
                dve.wait_ge(SV.sem, SV.at(last))
                v.tensor_scalar(cmp[:, :, :, :], rank[:, :, :, :], float(TOPK), -1.0, ALU.is_lt, ALU.add).then_inc(SV.sem, SV.one("keep"))
                dve.wait_ge(SV.sem, SV.at("keep"))
                v.tensor_scalar(cmp[:, :, :, :], cmp[:, :, :, :], BIG, None, ALU.mult).then_inc(SV.sem, SV.one("minus"))
                dve.wait_ge(SV.sem, SV.at("minus"))
                Sv = S[:, :, :, :].rearrange("p b (j two) h -> p (b j) two h", two=2)
                kb = cmp[:, :, :, :].rearrange("p b j h -> p (b j) h")[:, :, None, :].to_broadcast([P, DEC * BLOCKS, 2, HEADS])
                dve.wait_ge(SP_.sem, SP_.at("gates"))
                v.tensor_tensor(Sv, Sv, kb, ALU.add).then_inc(SV.sem, SV.one("bias"))
                dve.wait_ge(SV.sem, SV.at("bias"))
                v.tensor_reduce(mxt[:, :, :], S[:, :, :, :].rearrange("p b g h -> p b h g"), AX_X, ALU.max).then_inc(SV.sem, SV.one("tmax"))
                dve.wait_ge(SP_.sem, SP_.at("mxT"))
                v.tensor_reduce(mx64[:, :], m[2][0:64, 0:P], AX_X, ALU.max).then_inc(SV.sem, SV.one("rmax"))
                dve.wait_ge(SV.sem, SV.at("rmax"))
                v.tensor_scalar(dg[:, :], ident[0:64, 0:64], mx64[:, :], None, ALU.mult).then_inc(SV.sem, SV.one("diag"))
                dve.wait_ge(SP_.sem, SP_.at("mxb"))
                v.tensor_tensor(mxa[:, :, :], m[3][:, 0:64].rearrange("p (b h) -> p b h", b=DEC), own[:, :, :], ALU.max)\
                    .then_inc(SV.sem, SV.one("mxa"))
                dve.wait_ge(SV.sem, SV.at("mxa"))
                v.tensor_tensor(S[:, :, :, :], S[:, :, :, :], mxa[:, :, None, :].to_broadcast([P, DEC, PAGES, HEADS]), ALU.subtract)\
                    .then_inc(SV.sem, SV.one("shift"))
                v.tensor_tensor(po[:, :, :], own[:, :, :], mxa[:, :, :], ALU.subtract).then_inc(SV.sem, SV.one("oshift"))
                dve.wait_ge(SA.sem, SA.at("oexp"))
                v.tensor_reduce(mxt[:, :, :], S[:, :, :, :].rearrange("p b g h -> p b h g"), AX_X, ALU.add).then_inc(SV.sem, SV.one("tsum"))
                dve.wait_ge(SP_.sem, SP_.at("den"))
                v.tensor_tensor(mxa[:, :, :], m[4][:, 0:64].rearrange("p (b h) -> p b h", b=DEC), po[:, :, :], ALU.add)\
                    .then_inc(SV.sem, SV.one("den"))
                dve.wait_ge(SV.sem, SV.at("den"))
                v.reciprocal(own[:, :, :], mxa[:, :, :]).then_inc(SV.sem, SV.one("rden"))
                dve.wait_ge(SV.sem, SV.at("rden"))
                v.tensor_tensor(S[:, :, :, :], S[:, :, :, :], own[:, :, None, :].to_broadcast([P, DEC, PAGES, HEADS]), ALU.mult)\
                    .then_inc(SV.sem, SV.one("p"))
                v.tensor_tensor(po[:, :, :], po[:, :, :], own[:, :, :], ALU.mult).then_inc(SV.sem, SV.one("po"))

            def retention_stage(h, par, stage):
                z = ZH * par
                if stage == 0:
                    for w, first, dst, s in (("q", z + Z_Q, qr, 1.0), ("k", z + Z_K, kr, RK ** -0.5)):
                        x1, x2 = zo[:, first, :], zo[:, first + 1, :]
                        if w == "q":
                            dve.wait_ge(QA.sem, QA.before(h))
                            dve.wait_ge(QP.sem, QP.before(h))
                            dve.wait_ge(QV.sem, QV.before(h))
                            dve.wait_ge(tile_free, ZH * h + (O_IN.t0 + ZH))
                        else:
                            dve.wait_ge(QV.sem, QV.at("qx2", h))
                        for a, b, o, op, n in ((x1, x2, 0, ALU.subtract, ("a", "b", "x1")), (x2, x1, 1, ALU.add, ("c", "d", "x2"))):
                            if o:
                                dve.wait_ge(QV.sem, QV.at(w + "x1", h))
                            v.scalar_tensor_tensor(out=r1[:, :], in0=a, scalar=s, in1=ropec[:, 0, :], op0=ALU.mult, op1=ALU.mult)\
                                .then_inc(QV.sem, QV.one(w + n[0]))
                            v.scalar_tensor_tensor(out=r2[:, :], in0=b, scalar=s, in1=ropec[:, 1, :], op0=ALU.mult, op1=ALU.mult)\
                                .then_inc(QV.sem, QV.one(w + n[1]))
                            dve.wait_ge(QV.sem, QV.at(w + n[1], h))
                            v.tensor_tensor(dst[:, o, :], r1[:, :], r2[:, :], op).then_inc(QV.sem, QV.one(w + n[2]))
                elif stage == 1:
                    dve.wait_ge(QP.sem, QP.at("att", h))
                    dve.wait_ge(dm_landed, 16 * h + 16)
                    v.tensor_tensor(aT[:, :], m[0][:, 0:384], dmat[:, :], ALU.mult).then_inc(QV.sem, QV.one("att"))
                    dve.wait_ge(QP.sem, QP.at("k_turned", h))
                    for s in range(2):
                        v.tensor_scalar(rk_[:, s, :], m[2][:, s * RK:(s + 1) * RK],
                                        sdec[:, bass.ds(h, 1), s:s + 1].rearrange("p o n -> p (o n)"), None, ALU.mult)\
                            .then_inc(QV.sem, QV.one(f"k{s}"))
                    for d in range(2):
                        ins = v.tensor_tensor(rqm[:, d, :, :], qr[:, d:d + 1, SEQ:TOK].to_broadcast([P, 8, 8]), reye[:, :, :], ALU.mult)
                    ins.then_inc(QV.sem, QV.one("qm"))
                    dve.wait_ge(QA.sem, QA.at("kv3", h))
                    v.tensor_tensor(rvm[:, :, :], rkv[:, None, RK:2 * RK].to_broadcast([P, 2, RK]),
                                    pairs[:, :, None].to_broadcast([P, 2, RK]), ALU.mult).then_inc(QV.sem, QV.one("vm"))
                elif stage in (2, 3):
                    dve.wait_ge(r_s0_landed, 32 * h + 32)
                    d = stage - 2
                    for q, bank in enumerate(((1, 2, 5, 0), (1, 2, 5, 4))[d]):
                        dve.wait_ge(QP.sem, QP.at(f"kv{d}_{q}", h))
                        v.scalar_tensor_tensor(out=R0[:, d, 2 * q:2 * q + 2, :], in0=R0[:, d, 2 * q:2 * q + 2, :],
                                               scalar=gam[:, bass.ds(h, 1)], in1=m[bank][:, :].rearrange("p (b e) -> p b e", b=2),
                                               op0=ALU.mult, op1=ALU.add).then_inc(QV.sem, QV.one(f"s{d}_{q}"))
                elif stage == 5:
                    dve.wait_ge(QP.sem, QP.at("ssum", h))
                    v.tensor_scalar(r1[:, :], m[1][:, 0:TOK], 1.0 / RK, None, ALU.mult).then_inc(QV.sem, QV.one("mean"))
                    dve.wait_ge(QV.sem, QV.at("mean", h))
                    v.tensor_tensor(roT[:, :, :], roT[:, :, :], r1[:, None, :].to_broadcast([P, 2, TOK]), ALU.subtract)\
                        .then_inc(QV.sem, QV.one("oc"))
                elif stage == 6:
                    dve.wait_ge(QP.sem, QP.at("vsum", h))
                    v.tensor_scalar(r2[:, :], m[2][:, 0:TOK], 1.0 / RK, EPS, ALU.mult, ALU.add).then_inc(QV.sem, QV.one("var"))
                    dve.wait_ge(QA.sem, QA.at("rough", h))
                    refine(qr[:, 0, :], r2[:, :], r1[:, :], qr[:, 1, :], QV, ("n1", "n2", "rstd"), h)
                elif stage == 7:
                    dve.wait_ge(QV.sem, QV.at("rstd", h))
                    for e in range(2):
                        ins = v.scalar_tensor_tensor(out=roT[:, e, :], in0=roT[:, e, :], scalar=col(h * 2 + (V_GNR + e)), in1=qr[:, 0, :],
                                                     op0=ALU.mult, op1=ALU.mult)
                    ins.then_inc(QV.sem, QV.one("og"))
                    dve.wait_ge(QV.sem, QV.at("og", h))
                    v.tensor_tensor(qr[:, :, :], roT[:, :, :], gate[:, :, :], ALU.mult).then_inc(QV.sem, QV.one("gated"))
                    dve.wait_ge(QA.sem, QA.at("o_hi", h))
                    v.tensor_tensor(mixed[1][:, bass.ds(h * 2, 2), :], qr[:, :, :], mixed[0][:, bass.ds(h * 2, 2), :].bitcast(F32),
                                    ALU.subtract).then_inc(QV.sem, QV.one("o_lo"))

            v.memset(ones[:, :], 1.0).then_inc(consts_set, 1)
            for t in range(MT):
                dve.wait_ge(first_hi, t + 1)
                v.scalar_tensor_tensor(out=hA[1][:, t, :], in0=x[:, t, :], scalar=vec[:, V_MIX0 + t:V_MIX0 + t + 1],
                                       in1=hA[0][:, t, :].bitcast(F32), op0=ALU.mult, op1=ALU.subtract).then_inc(first_lo, 1)
                if t == 3:
                    lo_tile(E_IN, 0, 0)
            lo_tile(E_IN, 0, 1)
            norm_factor(0)
            norm_root(0)
            with dve.Fori(0, 4) as i:
                for j in range(2):
                    lo_tile(E_IN, i + 1, j)
                    evac(E_IN, i, j)
            dve.wait_ge(const_landed, 16 * N_CONST)
            dve.wait_ge(tile_free, HEADS)
            rope(Z_QB, 0)
            share = (3, 3, 3, 3, 2, 2)
            with dve.Fori(0, 7) as b:
                g = 0
                dve.wait_ge(q_copied, b + 1)
                for n, k in enumerate(share):
                    lo_tile(E_IN, b * 3 + (5 + n // 2), n % 2)
                    evac(E_IN, b * 3 + (4 + n // 2), n % 2)
                    for _ in range(k):
                        score_page(b, g)
                        g += 1
                save_scores(b)
            for i in (26, 27):
                for j in range(2):
                    lo_tile(E_IN, i, j)
                    evac(E_IN, i - 1, j)
            turn_over(E_IN, None)
            dve.wait_ge(tile_free, ZE)
            rope(Z_KB, HEADS)
            dve.wait_ge(RV.sem, RV.before(2 * HEADS))
            dve.wait_ge(q_copied, DEC)
            with dve.Fori(0, HEADS // 2) as i:
                attention_pair(i)
            dve.wait_ge(BV.sem, BV.before(HEADS // 2))
            v.tensor_tensor(qk[:, :, :], ze[:, Z_QB:Z_QB + HEADS, SEQ:TOK], ze[:, Z_KB:Z_KB + HEADS, SEQ:TOK], ALU.mult)\
                .then_inc(SV.sem, SV.one("qk"))
            v.tensor_copy(vs[:, :, :], ze[:, Z_VB:Z_VB + HEADS, SEQ:TOK]).then_inc(SV.sem, SV.one("vs"))
            dve.wait_ge(SV.sem, SV.at("vs"))
            select_blocks()
            dve.wait_ge(SV.sem, SV.before(1))
            dve.wait_ge(hc_landed, 48)
            for piece in range(3):
                hgrn_gates(0, 0, piece)
            with dve.Fori(0, HEADS // 2 - 1) as i:
                for j in range(2):
                    hgrn_head(i * 2 + j, j)
            for j in range(2):
                hgrn_head(HEADS - 2 + j, j, ahead=(j == 0))
            dve.wait_ge(HV.sem, HV.before(HEADS))
            dve.wait_ge(HP.sem, HP.before(HEADS))
            dve.wait_ge(h_stored, 32 * HEADS + 1)
            dve.wait_ge(SV.sem, SV.before(1))
            v.tensor_tensor(oS2[:, :, :], po[:, :, :].rearrange("p b h -> p h b"), vs[:, :, :], ALU.mult)\
                .then_inc(TV.sem, TV.one("pv"))
            dve.wait_ge(v_saved, DEC)
            dve.wait_ge(TV.sem, TV.at("pv"))
            v.tensor_tensor(oS2[:, :, :], oS2[:, :, :], oS[:, :, :], ALU.add).then_inc(TV.sem, TV.one("sum"))
            dve.wait_ge(TA.sem, TA.at("hi"))
            v.tensor_tensor(hA[1][:, HEADS:MT, SEQ:TOK], oS2[:, :, :], hA[0][:, HEADS:MT, SEQ:TOK].bitcast(F32), ALU.subtract)\
                .then_inc(TV.sem, TV.one("lo"))
            dve.wait_ge(kv_stored, 32)
            start_phase(E_OUT)
            for j in range(2):
                lo_tile(E_OUT, 0, j)
            body(E_OUT)
            turn_over(E_OUT, F0[0])

            def clear_pad(n):
                v.memset(ab[:, 0:PAD], 0.0).then_inc(ab_cleared, 1)
                dve.wait_ge(ab_cleared, n)
            norm_factor(1)
            norm_root(1)
            clear_pad(1)
            for a, b in zip(F0, F0[1:] + [O_IN]):
                start_phase(a)
                body(a)
                turn_over(a, b)
            norm_factor(2)
            norm_root(2)
            dve.wait_ge(cout_stored, 16)

            def project(h, par, s):
                if isinstance(h, int) and h == HEADS - 1 and s >= ZH - 2:
                    lo_tile(O_OUT, 0, s % 2)
                else:
                    lo_tile(O_IN, h * (ZH // 2) + (s // 2 + 1), s % 2)
                dve.wait_ge(unit_used, 4 * ZH * h + (O_IN.u0 + 4 * s + 4))
                v.tensor_tensor(zo[:, ZH * par + s, :], st[s % 2][:, 0:TOK], rstd[:, :], ALU.mult).then_inc(tile_free, 1)
            dve.wait_ge(unit_used, 4 * F0[-1].end())
            v.memset(rkv[:, :], 0.0).then_inc(ret_cleared, 1)
            v.memset(ro4[:, :], 0.0).then_inc(ret_cleared, 1)
            for s in range(ZH):
                project(0, 0, s)
            dve.wait_ge(ret_cleared, 2)
            dve.wait_ge(oc_landed, 16 * 6)
            with dve.Fori(0, HEADS // 2 - 1) as i:
                for j in range(2):
                    for s in range(ZH):
                        project(i * 2 + (j + 1), 1 - j, s)
                        retention_stage(i * 2 + j, j, s)
            for s in range(ZH):
                project(HEADS - 1, 1, s)
                retention_stage(HEADS - 2, 0, s)
            for s in range(ZH):
                retention_stage(HEADS - 1, 1, s)
            dve.wait_ge(QV.sem, QV.before(HEADS))
            dve.wait_ge(QP.sem, QP.before(HEADS))
            dve.wait_ge(r_s0_stored, 32 * HEADS)
            dve.wait_ge(r_sf_stored, 16 * HEADS)
            start_phase(O_OUT)
            body(O_OUT)
            turn_over(O_OUT, F1[0])
            norm_factor(3)
            norm_root(3)
            clear_pad(2)
            for a, b in zip(F1, F1[1:] + [None]):
                start_phase(a)
                body(a)
                turn_over(a, b)
            norm_factor(4)
            norm_root(4)
            with dve.Fori(0, MT) as t:
                v.scalar_tensor_tensor(out=tile(x, t), in0=tile(x, t), scalar=col(t + V_FINAL), in1=rstd[:, :],
                                       op0=ALU.mult, op1=ALU.mult).then_inc(y_ready, 1)

        @block.gpsimd
        def _(pool):
            pool.dma_start(pt[:, :], page_table).then_inc(pt_landed, 16)
            pool.wait_ge(pt_landed, 16)

            def load_page(cache, ring, b, g, landed, used, first):
                page = pool.snap(pool.value_load(pt[0:1, bass.ds(b * PAGES + g, 1)], min_val=0, max_val=cache.shape[0] - 1))
                if not first:
                    pool.wait_ge(used, b * PAGES + (g - 3))
                pool.dma_start(ring[:, g % 4, :], cache[bass.ds(page, 1), :, :].rearrange("o t n -> t (o n)"))\
                    .then_inc(landed[g % 4], 16)

            for g in range(PAGES):
                load_page(cache_k, kring, 0, g, k_landed, k_used, g < 4)
            with pool.Fori(1, DEC) as b:
                for g in range(PAGES):
                    load_page(cache_k, kring, b, g, k_landed, k_used, False)
            pool.wait_ge(tile_free, ZE)
            pool.wait_ge(RV.sem, RV.before(2 * HEADS))
            pool.dma_start(kT_out, ze[:, Z_KB:Z_KB + HEADS, :]).then_inc(kv_stored, 16)
            pool.dma_start(vT_out, ze[:, Z_VB:Z_VB + HEADS, :]).then_inc(kv_stored, 16)
            pool.wait_ge(BV.sem, BV.before(HEADS // 2))
            pool.wait_ge(BP.sem, BP.before(HEADS // 2))
            pool.wait_ge(BA.sem, BA.before(HEADS // 2))
            pool.dma_start(blk[:, :], c_blk).then_inc(hc_landed, 16)
            for g in range(4):
                load_page(cache_v, vring, 0, g, v_landed, v_used, True)
            pool.wait_ge(SV.sem, SV.before(1))
            pool.wait_ge(kv_stored, 32)
            pool.dma_start(levm[:, :, :], c_level).then_inc(hc_landed, 16)
            pool.dma_start(reset[:, :], c_reset).then_inc(hc_landed, 16)
            for g in range(4, PAGES):
                load_page(cache_v, vring, 0, g, v_landed, v_used, False)
            with pool.Fori(1, DEC) as b:
                for g in range(PAGES):
                    load_page(cache_v, vring, b, g, v_landed, v_used, False)
            pool.wait_ge(TV.sem, TV.before(1))
            pool.wait_ge(kv_stored, 32)
            pool.dma_start(cst[:, :, :], conv_state[0]).then_inc(cst_landed, 16)
            pool.wait_ge(FA.sem, FA.before(FT))
            pool.dma_start(conv_out[0], cout[:, :, :]).then_inc(cout_stored, 16)
            pool.wait_ge(cout_stored, 16)
            pool.wait_ge(FV.sem, FV.before(FT))
            pool.wait_ge(unit_used, 4 * F0[-1].end())
            for dst, src in ((ropec[:, :, :], c_rope_c), (sdec[:, :, :], c_sdec), (gam[:, :], c_gamma), (eye4[:, :], c_eye4), (pairs[:, :], c_pairs),
                             (reye[:, :, :], c_eye)):
                pool.dma_start(dst, src).then_inc(oc_landed, 16)

            pool.wait_ge(QA.sem, QA.before(HEADS))
            pool.wait_ge(QV.sem, QV.before(HEADS))
            pool.wait_ge(QP.sem, QP.before(HEADS))
            pool.wait_ge(r_s0_stored, 32 * HEADS)
            pool.wait_ge(r_sf_stored, 16 * HEADS)
            pool.dma_start(cst[:, :, :], conv_state[1]).then_inc(cst_landed, 16)
            pool.wait_ge(FA.sem, FA.before(2 * FT))
            pool.dma_start(conv_out[1], cout[:, :, :]).then_inc(cout_stored, 16)
            pool.wait_ge(cout_stored, 32)


def _tiles(w, ktu):
    k, n = w.shape
    return np.ascontiguousarray(w.reshape(2, k // 256, P, n // P, P).transpose(3, 0, 2, 1, 4)).reshape(n // P, 2, P, 2 * ktu * P)


def _columns(a):
    return np.ascontiguousarray(a.reshape(-1, P).T)


def _constants():
    f = np.float32
    pos = np.concatenate([np.arange(SEQ), np.full(DEC, 2048)]).astype(f)

    def angles(half, theta):
        inv = f(theta) ** (-np.arange(half, dtype=f) / f(half))
        return (pos[None, :] * inv.astype(f)[:, None]).astype(f)
    ab_, ac = angles(16, 500000.0), angles(P, 10000.0)
    rope_b = np.stack([np.concatenate([np.cos(ab_)] * 2), np.concatenate([-np.sin(ab_), np.sin(ab_)])], 1).astype(f)
    rope_c = np.stack([np.cos(ac), np.sin(ac)], 1).astype(f)
    perm = np.zeros((32, 32), f)
    perm[np.arange(32), (np.arange(32) + 16) % 32] = 1
    i = np.arange(P)
    causal = np.where(i[None, :] <= i[:, None], 0, -BIG).astype(f)
    cau = np.concatenate([causal, np.zeros((P, P), f), causal], 1)
    lg = np.log(1.0 - 2.0 ** (-5.0 - np.arange(HEADS)))
    t = np.arange(SEQ)
    d = np.where(t[None, :] >= t[:, None], t[None, :] - t[:, None], 0)
    full = np.where(t[None, :] >= t[:, None], np.exp(d * lg[:, None, None]), 0.0)
    decay = np.concatenate([full[:, 0:P, :], full[:, P:, P:]], 2).astype(f)
    sdec = np.exp((SEQ - 1 - t)[None, :] * lg[:, None]).reshape(HEADS, 2, P).transpose(2, 0, 1).astype(f)
    gamma = np.broadcast_to(np.exp(lg)[None, :], (P, HEADS)).astype(f)
    level = np.zeros((P, LEVELS + 1, P), f)
    for l in range(LEVELS):
        B = 1 << l
        level[:, l, :] = ((i[:, None] // (2 * B)) == (i[None, :] // (2 * B))) & (i[:, None] % (2 * B) < B) & (i[None, :] % (2 * B) >= B)
    level[:, LEVELS, :] = np.eye(P)
    reset = np.broadcast_to((t % CHUNK != 0).astype(f), (P, SEQ))
    blk = np.zeros((P, 2, P), f)
    for h in range(HEADS):
        blk[32 * (h // 2) + h, h % 2] = 1
    blk = blk.reshape(P, 2 * P)
    eye4 = np.zeros((P, 8), f)
    eye4[(32 * np.arange(4)[:, None] + i[None, :8]).reshape(-1), np.tile(i[:8], 4)] = 1
    pairs = np.zeros((P, 2), f)
    pairs[32 * (i[:8] // 2) + i[:8], i[:8] % 2] = 1
    return {
        "c_eye4": eye4, "c_pairs": pairs,
        "c_ident": np.eye(P, dtype=f), "c_eye8": np.eye(8, dtype=f),
        "c_eye": np.broadcast_to(np.eye(8, dtype=f), (P, 8, 8)), "c_blk": blk,
        "c_causal": cau, "c_rope_b": rope_b, "c_perm": perm, "c_rope_c": rope_c, "c_decay": decay, "c_sdec": sdec,
        "c_gamma": gamma, "c_level": level, "c_reset": reset,
    }


_OUTS = [("y_out", (P, MT, TOK)), ("kT_out", (P, HEADS, TOK)), ("vT_out", (P, HEADS, TOK)), ("hgrn_p_out", (HEADS, P, P)),
         ("hgrn_s_out", (HEADS, P, DEC, P)), ("ret_p_out", (HEADS, RK, RK)), ("ret_s_out", (HEADS, P, 2, DEC, RK)),
         ("conv_out", (2, P, FT, PAD + 2 * DEC))]


def _layout(inp):
    assert inp["lb_hgrn"].shape[0] == 1
    x = np.concatenate([inp["x_prompt"][0], inp["x_sample"][:, 0]], 0)
    a = {"x_in": x.T.reshape(MT, P, TOK).transpose(1, 0, 2)}
    a["vecs"] = np.concatenate(
        [_columns(inp[n][l]) for l in range(2) for n in ("norm_mix", "norm_ffn")]
        + [_columns(inp["norm_final"]), _columns(inp["gn_hgrn"]), _columns(inp["gn_ret"])]
        + [b for l in range(2) for b in (_columns(inp["conv_w"][l]), _columns(inp["conv_b"][l]))], 1)
    a["conv_state"] = inp["state_conv"].transpose(0, 3, 1, 2).reshape(2, FT, P, 2 * DEC).transpose(0, 2, 1, 3)
    w = inp["w_in_even"][0]
    A, B = 4 * HEADS * P, HEADS * P
    a["w_even_in"] = _tiles(np.concatenate([w[:, A:A + 3 * B], w[:, :A]], 1), 4)
    a["w_even_out"] = _tiles(inp["w_out_even"][0], 4)
    a["w_odd_in"] = _tiles(inp["w_in_odd"][0], 4).reshape(4, HEADS, 2, 2, P, 8 * P).transpose(1, 0, 2, 3, 4, 5).reshape(ZO, 2, P, 8 * P)
    a["w_odd_out"] = _tiles(inp["w_out_odd"][0], 4)
    for l in range(2):
        t = _tiles(inp["w_ffn_in"][l], 4)
        a[f"w_f{l}_in"] = t.reshape(2, FT, 2, P, 8 * P).transpose(1, 0, 2, 3, 4).reshape(2 * FT, 2, P, 8 * P)
        r = 0
        for n, c in enumerate(CHUNKS):
            a[f"w_f{l}_o{n}"] = _tiles(inp["w_ffn_out"][l][r * P:(r + c) * P], c // 4)
            r += c
    for n in ("cache_k", "cache_v"):
        a[n] = inp[n][0].reshape(-1, PAGE, HEADS * P)
    a["page_table"] = inp["page_table"].reshape(1, -1)
    a["state_hgrn"] = inp["state_hgrn"][0].transpose(1, 2, 0, 3)
    a["state_ret"] = inp["state_ret"][0].reshape(DEC, HEADS, 2, P, RK).transpose(1, 3, 2, 0, 4)
    a.update(_constants())
    return {k: np.ascontiguousarray(v) for k, v in a.items()}


def kernel(**inputs):
    import concourse.bacc as bacc
    from concourse.bass_utils import run_bass_kernel_spmd as run
    inputs = {k: np.asarray(v) for k, v in inputs.items()}
    arrays = _layout(inputs)
    nc = bacc.Bacc("TRN2", target_bir_lowering=False, num_devices=1)
    aps = {k: nc.dram_tensor("in_" + k, a.shape, mybir.dt.from_np(a.dtype), kind="ExternalInput").ap() for k, a in arrays.items()}
    for k, shape in _OUTS:
        aps[k] = nc.dram_tensor("out_" + k, shape, F32, kind="ExternalOutput").ap()
    hybrid_step(nc, **aps)
    r = run(nc, [{"in_" + k: a for k, a in arrays.items()}], core_ids=[0]).results[0]
    o = {k: np.asarray(r["out_" + k]) for k, _ in _OUTS}

    def rows(t):
        return np.ascontiguousarray(t.transpose(2, 1, 0).reshape(TOK, -1))
    y, k, v = rows(o["y_out"]), rows(o["kT_out"]), rows(o["vT_out"])
    c = o["conv_out"].transpose(0, 3, 2, 1).reshape(2, PAD + 2 * DEC, D_FF)
    return (y[:SEQ][None], y[SEQ:][:, None],
            k[:SEQ].reshape(1, 1, SEQ, HEADS, P), v[:SEQ].reshape(1, 1, SEQ, HEADS, P),
            k[SEQ:].reshape(1, DEC, 1, HEADS, P), v[SEQ:].reshape(1, DEC, 1, HEADS, P),
            o["hgrn_p_out"][None, None], np.ascontiguousarray(o["hgrn_s_out"].transpose(2, 0, 1, 3))[None], o["ret_p_out"][None, None], np.ascontiguousarray(o["ret_s_out"].transpose(3, 0, 2, 1, 4).reshape(DEC, HEADS, RK, RK))[None],
            np.ascontiguousarray(c[:, None, :PAD]), np.ascontiguousarray(c[:, PAD:].reshape(2, DEC, 2, D_FF)))
```
